# Optimizing a Trainium2 kernel written in Bass

```python
import jax, jax.numpy as jnp
from jax import lax
import numpy as np

D_MODEL = 1024
BATCH = 1
SEQ = 1024
DEPTH = 1

DN_HEADS = 8
DN_HEAD_DIM = 128
DN_WIDTH = DN_HEADS * DN_HEAD_DIM
CONV_K = 4
CHUNK = 64
S5_WIDTH = D_MODEL // 2
S5_GROUP = 16
S5_GROUPS = S5_WIDTH // S5_GROUP
S5_STATE = 64
EPS = 1e-6
IN_COLS = 4 * DN_WIDTH + 2 * DN_HEADS + 2 * S5_WIDTH + 2 * D_MODEL

kernel_name = 'hybrid_deltanet_s5_adaln_block'

def rmsnorm(x):
    xf = x.astype(jnp.float32)
    return (xf * lax.rsqrt(jnp.mean(xf * xf, axis=-1, keepdims=True) + EPS)).astype(x.dtype)

def l2norm(x):
    return x * lax.rsqrt(jnp.sum(x * x, axis=-1, keepdims=True) + EPS)

def causal_depthwise_conv(x, w):
    k = w.shape[0]
    return lax.conv_general_dilated(
        x, w[:, None, :], window_strides=(1,), padding=[(k - 1, 0)],
        dimension_numbers=('NWC', 'WIO', 'NWC'), feature_group_count=x.shape[-1])

def gated_delta_rule(q, k, v, g, beta):
    b, l, h, dk = q.shape
    dv = v.shape[-1]
    n = l // CHUNK

    def chunks(t):
        t = t.reshape((b, n, CHUNK, h) + t.shape[3:])
        return jnp.moveaxis(t, (1, 3), (0, 2))

    qc, kc, vc, bc = chunks(q), chunks(k), chunks(v), chunks(beta)
    gc = jnp.cumsum(chunks(g), axis=-1)
    causal = jnp.tril(jnp.ones((CHUNK, CHUNK), bool))
    strict = jnp.tril(jnp.ones((CHUNK, CHUNK), bool), -1)
    decay = jnp.exp(jnp.where(causal, gc[..., :, None] - gc[..., None, :], -jnp.inf))
    kk = jnp.einsum('nbhid,nbhjd->nbhij', kc, kc)
    tmat = jnp.eye(CHUNK, dtype=q.dtype) + jnp.where(strict, bc[..., :, None] * kk * decay, 0.0)
    u = lax.linalg.triangular_solve(tmat, vc * bc[..., None], left_side=True, lower=True, unit_diagonal=True)
    w = lax.linalg.triangular_solve(tmat, kc * (bc * jnp.exp(gc))[..., None], left_side=True, lower=True, unit_diagonal=True)
    attn = jnp.where(causal, jnp.einsum('nbhid,nbhjd->nbhij', qc, kc) * decay, 0.0)
    q_dec = qc * jnp.exp(gc)[..., None]
    k_dec = kc * jnp.exp(gc[..., -1:] - gc)[..., None]
    g_last = jnp.exp(gc[..., -1])

    def step(state, inp):
        u_i, w_i, attn_i, qd_i, kd_i, gl_i = inp
        v_new = u_i - jnp.einsum('bhcd,bhde->bhce', w_i, state)
        o = jnp.einsum('bhcd,bhde->bhce', qd_i, state) + jnp.einsum('bhij,bhje->bhie', attn_i, v_new)
        state = state * gl_i[..., None, None] + jnp.einsum('bhcd,bhce->bhde', kd_i, v_new)
        return state, o

    s0 = jnp.zeros((b, h, dk, dv), q.dtype)
    _, o = lax.scan(step, s0, (u, w, attn, q_dec, k_dec, g_last))
    return jnp.moveaxis(o, (0, 2), (1, 3)).reshape(b, l, h, dv)

def deltanet_branch(qkv, z, beta_in, a_in, conv_w, a_log, dt_bias, norm_w, w_proj):
    b, l, _ = qkv.shape
    f32 = jnp.float32
    qkv = jax.nn.silu(causal_depthwise_conv(qkv, conv_w)).astype(f32)
    q, k, v = jnp.split(qkv, 3, axis=-1)
    q = l2norm(q.reshape(b, l, DN_HEADS, DN_HEAD_DIM)) * (DN_HEAD_DIM ** -0.5)
    k = l2norm(k.reshape(b, l, DN_HEADS, DN_HEAD_DIM))
    v = v.reshape(b, l, DN_HEADS, DN_HEAD_DIM)
    beta = jax.nn.sigmoid(beta_in.astype(f32))
    g = -jnp.exp(a_log.astype(f32)) * jax.nn.softplus(a_in.astype(f32) + dt_bias.astype(f32))
    o = gated_delta_rule(q, k, v, g, beta)
    o = (rmsnorm(o) * norm_w.astype(f32)).reshape(b, l, DN_WIDTH).astype(z.dtype)
    return (o * jax.nn.silu(z)) @ w_proj

def s5_scan(u, lam_re, lam_im, log_dt, b_re, b_im, c_re, c_im, d_skip):
    bsz, l, _ = u.shape
    ug = u.reshape(bsz, l, S5_GROUPS, S5_GROUP)
    dt = jnp.exp(log_dt)[:, None]
    lr = jnp.minimum(lam_re, -1e-4)
    li = lam_im
    mag = jnp.exp(lr * dt)
    ab_re = mag * jnp.cos(li * dt)
    ab_im = mag * jnp.sin(li * dt)
    den = lr * lr + li * li
    f_re = ((ab_re - 1.0) * lr + ab_im * li) / den
    f_im = (ab_im * lr - (ab_re - 1.0) * li) / den
    bb_re = f_re[..., None] * b_re - f_im[..., None] * b_im
    bb_im = f_re[..., None] * b_im + f_im[..., None] * b_re
    bu_re = jnp.einsum('blgi,gpi->blgp', ug, bb_re)
    bu_im = jnp.einsum('blgi,gpi->blgp', ug, bb_im)
    shape_a = (1, l, S5_GROUPS, S5_STATE)
    a_re = jnp.broadcast_to(ab_re[None, None], shape_a)
    a_im = jnp.broadcast_to(ab_im[None, None], shape_a)

    def combine(e1, e2):
        a1r, a1i, b1r, b1i = e1
        a2r, a2i, b2r, b2i = e2
        return (a1r * a2r - a1i * a2i, a1r * a2i + a1i * a2r,
                a2r * b1r - a2i * b1i + b2r, a2r * b1i + a2i * b1r + b2i)

    _, _, xr, xi = lax.associative_scan(combine, (a_re, a_im, bu_re, bu_im), axis=1)
    y = jnp.einsum('blgp,gip->blgi', xr, c_re) - jnp.einsum('blgp,gip->blgi', xi, c_im)
    return y.reshape(bsz, l, S5_WIDTH) + d_skip * u

def s5_branch(u, z, lam_re, lam_im, log_dt, b_re, b_im, c_re, c_im, d_skip, glu_w, glu_b, w_proj):
    f32 = jnp.float32
    y = s5_scan(u.astype(f32), lam_re.astype(f32), lam_im.astype(f32), log_dt.astype(f32),
                b_re.astype(f32), b_im.astype(f32), c_re.astype(f32), c_im.astype(f32), d_skip.astype(f32))
    gy = jax.nn.gelu(y)
    y = gy * jax.nn.sigmoid(gy @ glu_w.astype(f32) + glu_b.astype(f32))
    return (y.astype(z.dtype) * jax.nn.silu(z)) @ w_proj

def setup_inputs(seed: int = 0) -> dict:
    key = jax.random.key(seed)
    ks = jax.random.split(key, 24)
    nrm = jax.random.normal
    L_, D_ = DEPTH, D_MODEL
    dt_dn = jnp.exp(jax.random.uniform(ks[4], (L_, DN_HEADS), minval=np.log(1e-3), maxval=np.log(1e-1)))
    lam_re = -0.5 + 0.01 * nrm(ks[8], (L_, S5_GROUPS, S5_STATE))
    lam_im = jnp.broadcast_to(np.pi * jnp.arange(S5_STATE, dtype=jnp.float32), (L_, S5_GROUPS, S5_STATE))
    return {
        'x': nrm(ks[0], (BATCH, SEQ, D_)),
        'c': nrm(ks[1], (BATCH, D_)),
        'w_ada': nrm(ks[2], (L_, D_, 3 * D_)) * (0.5 * D_ ** -0.5),
        'b_ada': 0.01 * nrm(ks[3], (L_, 3 * D_)),
        'w_in': nrm(ks[5], (L_, D_, IN_COLS)) * D_ ** -0.5,
        'dn_conv_w': nrm(ks[6], (L_, CONV_K, 3 * DN_WIDTH)) * CONV_K ** -0.5,
        'dn_a_log': jnp.log(jax.random.uniform(ks[7], (L_, DN_HEADS), minval=1.0, maxval=16.0)),
        'dn_dt_bias': dt_dn + jnp.log(-jnp.expm1(-dt_dn)),
        'dn_norm_w': 1.0 + 0.02 * nrm(ks[9], (L_, DN_HEAD_DIM)),
        'w_proj_a': nrm(ks[10], (L_, DN_WIDTH, D_)) * DN_WIDTH ** -0.5,
        's5_lambda_re': lam_re,
        's5_lambda_im': lam_im,
        's5_log_dt': jax.random.uniform(ks[11], (L_, S5_GROUPS), minval=np.log(1e-3), maxval=np.log(1e-1)),
        's5_b_re': nrm(ks[12], (L_, S5_GROUPS, S5_STATE, S5_GROUP)) * (2 * S5_GROUP) ** -0.5,
        's5_b_im': nrm(ks[13], (L_, S5_GROUPS, S5_STATE, S5_GROUP)) * (2 * S5_GROUP) ** -0.5,
        's5_c_re': nrm(ks[14], (L_, S5_GROUPS, S5_GROUP, S5_STATE)) * S5_STATE ** -0.5,
        's5_c_im': nrm(ks[15], (L_, S5_GROUPS, S5_GROUP, S5_STATE)) * S5_STATE ** -0.5,
        's5_d': nrm(ks[16], (L_, S5_WIDTH)),
        's5_glu_w': nrm(ks[17], (L_, S5_WIDTH, S5_WIDTH)) * S5_WIDTH ** -0.5,
        's5_glu_b': 0.01 * nrm(ks[18], (L_, S5_WIDTH)),
        'w_proj_b': nrm(ks[19], (L_, S5_WIDTH, D_)) * S5_WIDTH ** -0.5,
        'w_out': nrm(ks[20], (L_, D_, D_)) * D_ ** -0.5,
        'final_norm_w': 1.0 + 0.02 * nrm(ks[21], (D_,)),
    }

def reference(x, c, w_ada, b_ada, w_in, dn_conv_w, dn_a_log, dn_dt_bias, dn_norm_w, w_proj_a,
              s5_lambda_re, s5_lambda_im, s5_log_dt, s5_b_re, s5_b_im, s5_c_re, s5_c_im, s5_d,
              s5_glu_w, s5_glu_b, w_proj_b, w_out, final_norm_w):
    sizes = [3 * DN_WIDTH, DN_WIDTH, DN_HEADS, DN_HEADS, S5_WIDTH, S5_WIDTH, D_MODEL, D_MODEL]
    split_idx = np.cumsum(sizes)[:-1].tolist()
    for layer in range(DEPTH):
        mod = c @ w_ada[layer] + b_ada[layer]
        shift, scale, gate = jnp.split(mod, 3, axis=-1)
        h = rmsnorm(x) * (1.0 + scale[:, None, :]) + shift[:, None, :]
        proj = h @ w_in[layer]
        qkv, z_a, beta_in, a_in, u_s5, z_b, gate_a, gate_b = jnp.split(proj, split_idx, axis=-1)
        y_a = deltanet_branch(qkv, z_a, beta_in, a_in, dn_conv_w[layer], dn_a_log[layer],
                              dn_dt_bias[layer], dn_norm_w[layer], w_proj_a[layer])
        y_b = s5_branch(u_s5, z_b, s5_lambda_re[layer], s5_lambda_im[layer], s5_log_dt[layer],
                        s5_b_re[layer], s5_b_im[layer], s5_c_re[layer], s5_c_im[layer], s5_d[layer],
                        s5_glu_w[layer], s5_glu_b[layer], w_proj_b[layer])
        merged = jax.nn.sigmoid(gate_a) * y_a + jax.nn.sigmoid(gate_b) * y_b
        x = x + gate[:, None, :] * (merged @ w_out[layer])
    return rmsnorm(x) * final_norm_w


_drawn_inputs = setup_inputs


def setup_inputs(seed=0):
    import zlib

    import numpy as np

    out = dict(_drawn_inputs(seed))
    spreads = {}
    factors = {'b_ada': 8.0,
     'dn_norm_w': 22.071,
     's5_lambda_re': 64.0,
     's5_lambda_im': 43.816,
     's5_log_dt': 54.088,
     's5_b_re': 54.088,
     's5_b_im': 62.424,
     's5_c_re': 54.032,
     's5_c_im': 60.472,
     's5_glu_b': 64.0,
     'final_norm_w': 7.864,
     's5_glu_w': 3.725}
    for name, (base, spread) in spreads.items():
        noise = np.random.default_rng([zlib.crc32(name.encode()), seed]).standard_normal(out[name].shape)
        drawn = base * np.exp(spread * noise) if base else spread * noise
        out[name] = __import__('jax').numpy.asarray(drawn.astype(out[name].dtype))
    for name, factor in factors.items():
        out[name] = (out[name] * factor).astype(out[name].dtype)
    return out
```

```python
from contextlib import ExitStack
import concourse.bass as bass
from concourse import mybir

P = 128
D = 1024
T = 1024
HEADS, HD = 8, 128
KT = D // P
NT = T // P
HALF = T // 2
CONV_K = 4
S5W, GROUPS, GI, PS = 512, 32, 16, 64
CT = S5W // P
CG = P // GI
STEP = 8
NCH = T // STEP
EPS = 1e-6
NQ = 2
GT = NT // NQ

TILE_BA, TILE_UZ, TILE_GLU, TILE_HEAD = 0, 1, 9, 11
TILE_MERGE = TILE_HEAD + 4 * HEADS
TILE_OUT = TILE_MERGE + 4 * KT
LEVELS = (1, 2, 4, 8, 16, 32, 64)
IDENT, LE, GT_, GE, ONES, LEVEL0 = 0, 1, 2, 3, 4, 5
NCONST = LEVEL0 + len(LEVELS)
C_G, C_BETA, C_EG, C_ES, C_EGL, C_BEG, C_HB = range(7)
NCOL = 7

F32, F32R = mybir.dt.float32, mybir.dt.float32r
I32 = mybir.dt.int32
ACT = mybir.ActivationFunctionType
ALU = mybir.AluOpType
AX = mybir.AxisListType.X


def bc(ap, shape):
    return ap.to_broadcast(shape)


def build_program(nc, a, out, oz_dram, yg_dram, mg_dram):
    ctx = ExitStack()
    with ctx:
        def sb_in(c):
            return lambda name, shape, dt=F32: c.enter_context(nc.sbuf_tensor(name, shape, dt))

        def sem(name):
            return ctx.enter_context(nc.semaphore(name))

        sb = sb_in(ctx)
        cst = sb("cst", [P, NCONST, P])
        modT = sb("modT", [P, 2 * KT])
        raw = sb("raw", [P, 2, D])
        wH = sb("wH", [P, 2, D], F32R)
        wL = sb("wL", [P, 2, D], F32R)
        pair = [ctx.enter_context(nc.psum_tensor(f"pair{n}", [P, 2, HALF], F32)) for n in range(2)]
        work = ctx.enter_context(nc.psum_tensor("work", [P, 4, 512], F32))
        ident = cst[:, IDENT, :]

        w_landed = [sem("w_landed0"), sem("w_landed1")]
        w_hi = sem("w_hi")
        w_lo = sem("w_lo")
        w_used = sem("w_used")

        def load_w(sp, base, it=0, per=0, width=D, src=None):
            t0 = base
            if t0 >= 2:
                sp.wait_ge(w_lo, it * per + (t0 - 1))
            if src is None:
                src = a["w"][it * per + t0]
            sp.dma_start(raw[:, t0 % 2, 0:width], src[:, 0:width]).then_inc(w_landed[t0 % 2], 16)

        def split_hi(act, base, it=0, per=0, width=D):
            act.wait_ge(w_landed[base % 2], it * (8 * per) + 16 * (base // 2 + 1))
            if base >= 2:
                act.wait_ge(w_used, it * per + (base - 1))
            act.activation(wH[:, base % 2, 0:width], raw[:, base % 2, 0:width], ACT.Copy).then_inc(w_hi, 1)

        def split_lo(pool, base, it=0, per=0, width=D):
            pool.wait_ge(w_hi, it * per + (base + 1))
            pool.tensor_tensor(wL[:, base % 2, 0:width], raw[:, base % 2, 0:width],
                               wH[:, base % 2, 0:width].bitcast(F32), ALU.subtract).then_inc(w_lo, 1)

        def product3(pe, dst, wh, wl, xh, xl, first, last):
            pe.matmul(dst, wh, xh, start=first, stop=False)
            pe.matmul(dst, wh, xl, start=False, stop=False)
            return pe.matmul(dst, wl, xh, start=False, stop=last)

        hstack = ExitStack()
        hsb = sb_in(hstack)
        hH = hsb("hH", [P, KT, T], F32R)
        hL = hsb("hL", [P, KT, T], F32R)
        with ExitStack() as c1:
            s1 = sb_in(c1)
            x = s1("x", [P, NT, D])
            junk = s1("junk", [P, D])
            wada = s1("wada", [P, KT, 1024])
            cT = s1("cT", [P, KT])
            bada = s1("bada", [P, 2 * KT])
            ss = s1("ss", [P, NT])
            rstd = s1("rstd", [P, NT])
            mhalf = s1("mhalf", [P, NT])
            hf = s1("hf", [P, 4, HALF])
            x_in, c_in, b_in, k_in = sem("x_in"), sem("c_in"), sem("b_in"), sem("k_in")
            ada_in = [sem("ada_in0"), sem("ada_in1")]
            ada_used = sem("ada_used")
            sq_done, rstd_done, xn_done = sem("sq_done"), sem("rstd_done"), sem("xn_done")
            ada_done, mod_done = sem("ada_done"), sem("mod_done")
            h_full, hf_done, hH_done, hL_done = sem("h_full"), sem("hf_done"), sem("hH_done"), sem("hL_done")
            with nc.Block() as block:
                @block.sync
                def _(sp):
                    sp.dma_start(cT[:, :], a["cT"]).then_inc(c_in, 16)
                    sp.dma_start(bada[:, :], a["bada"]).then_inc(b_in, 16)
                    for n in range(2):
                        sp.dma_start(wada[:, :, 512 * n:512 * n + 512], a["wada"][0][:, :, 512 * n:512 * n + 512]).then_inc(ada_in[0], 16)
                    sp.dma_start(cst[:, :, :], a["cst"]).then_inc(k_in, 16)
                    load_w(sp, 0)
                    load_w(sp, 1)
                    sp.wait_ge(ada_used, 1)
                    sp.dma_start(wada[:, :, :], a["wada"][1]).then_inc(ada_in[1], 16)

                @block.scalar
                def _(act):
                    for n in range(NT):
                        act.dma_start(x[:, n, :], a["x"][n]).then_inc(x_in, 16)
                    for n in range(NT):
                        if n == 0:
                            act.wait_ge(x_in, 16 * NT)
                        else:
                            act.wait_ge(sq_done, n)
                        act.activation(junk[:, :], x[:, n, :], ACT.Square, accum_out=ss[:, n:n + 1]).then_inc(sq_done, 1)
                    for u in range(2 * KT):
                        k, n = u // 2, u % 2
                        act.wait_ge(hf_done, u + 1)
                        act.activation(hH[:, k, n * HALF:(n + 1) * HALF], hf[:, u % 4, :], ACT.Copy).then_inc(hH_done, 1)

                @block.gpsimd
                def _(pool):
                    pool.memset(mhalf[:, :], -0.5).then_inc(rstd_done, 1)
                    pool.wait_ge(sq_done, NT)
                    pool.tensor_scalar(ss[:, :], ss[:, :], 1.0 / D, EPS, ALU.mult, ALU.add).then_inc(rstd_done, 1)
                    pool.wait_ge(rstd_done, 2)
                    pool.tensor_tensor(rstd[:, :], ss[:, :], mhalf[:, :], ALU.pow).then_inc(rstd_done, 1)
                    for u in range(2 * KT):
                        k, n = u // 2, u % 2
                        pool.wait_ge(hH_done, u + 1)
                        pool.tensor_tensor(hL[:, k, n * HALF:(n + 1) * HALF], hf[:, u % 4, :],
                                           hH[:, k, n * HALF:(n + 1) * HALF].bitcast(F32), ALU.subtract).then_inc(hL_done, 1)

                @block.vector
                def _(dve):
                    dve.wait_ge(rstd_done, 3)
                    for n in range(NT):
                        dve.tensor_scalar(x[:, n, :], x[:, n, :], rstd[:, n:n + 1], None, ALU.mult).then_inc(xn_done, 1)
                    dve.wait_ge(b_in, 16)
                    for m in range(2):
                        dve.wait_ge(ada_done, m + 1)
                        dve.tensor_tensor(modT[:, m * KT:(m + 1) * KT], work[:, m, 0:KT], bada[:, m * KT:(m + 1) * KT],
                                          ALU.add).then_inc(mod_done, 1)
                    dve.wait_ge(mod_done, 2)
                    dve.tensor_scalar(modT[:, KT:2 * KT], modT[:, KT:2 * KT], 1.0, None, ALU.add).then_inc(mod_done, 1)
                    dve.wait_ge(mod_done, 3)
                    for u in range(2 * KT):
                        k = u // 2
                        dve.wait_ge(h_full, u + 1)
                        if u >= 4:
                            dve.wait_ge(hL_done, u - 3)
                        dve.tensor_scalar(hf[:, u % 4, :], pair[u // 2 % 2][:, u % 2, :], modT[:, KT + k:KT + k + 1],
                                          modT[:, k:k + 1], ALU.mult, ALU.add).then_inc(hf_done, 1)

                @block.tensor
                def _(pe):
                    pe.wait_ge(c_in, 16)
                    for m in range(2):
                        pe.wait_ge(ada_in[m], 32 if m == 0 else 16)
                        for q in range(KT):
                            for k in range(KT):
                                mm = pe.matmul(work[:, m, q:q + 1], wada[:, k, q * P:(q + 1) * P], cT[:, k:k + 1],
                                               start=(k == 0), stop=(k == KT - 1))
                        mm.then_inc(ada_done, 1)
                        if m == 0:
                            pe.wait_ge(ada_done, 1)
                            pe.sem_inc(ada_used, 1)
                    pe.wait_ge(k_in, 16)
                    pe.wait_ge(xn_done, NT)
                    for u in range(2 * KT):
                        k, n = u // 2, u % 2
                        if u >= 4:
                            pe.wait_ge(hf_done, u - 3)
                        for j in range(GT):
                            tr = pe.transpose(pair[u // 2 % 2][:, u % 2, j * P:(j + 1) * P],
                                              x[:, n * GT + j, k * P:(k + 1) * P], ident)
                        tr.then_inc(h_full, 1)

        dstack = ExitStack()
        dsb = sb_in(dstack)
        cols = dsb("cols", [P, HEADS, NCOL, NT])
        with ExitStack() as c2:
            s2 = sb_in(c2)
            baT = s2("baT", [2 * HEADS, T])
            ba = s2("ba", [P, NT, 2 * HEADS])
            dtb = s2("dtb", [P, HEADS])
            alog = s2("alog", [P, HEADS])
            ea = s2("ea", [P, HEADS])
            z = s2("z", [P, HEADS, NT])
            az = s2("az", [P, HEADS, NT])
            g = s2("g", [P, HEADS, NT])
            ex3 = s2("ex3", [P, 3, HEADS * NT])
            par_in = sem("par_in")
            ba_full, ba_copied, ba_t, ba_nat = sem("ba_full"), sem("ba_copied"), sem("ba_t"), sem("ba_nat")
            col_act, col_dve, col_pe = sem("col_act"), sem("col_dve"), sem("col_pe")
            with nc.Block() as block:
                @block.sync
                def _(sp):
                    sp.dma_start(dtb[:, :], a["dtb"]).then_inc(par_in, 16)
                    sp.dma_start(alog[:, :], a["alog"]).then_inc(par_in, 16)
                    load_w(sp, 2)
                    load_w(sp, 3)

                @block.gpsimd
                def _(pool):
                    split_lo(pool, 0)
                    split_lo(pool, 1)
                    split_lo(pool, 2)

                @block.tensor
                def _(pe):
                    pe.wait_ge(w_lo, 1)
                    for n in range(2):
                        for k in range(KT):
                            mm = product3(pe, pair[0][:, n, :], wH[:, 0, k * P:(k + 1) * P], wL[:, 0, k * P:(k + 1) * P],
                                          hH[:, k, n * HALF:(n + 1) * HALF], hL[:, k, n * HALF:(n + 1) * HALF],
                                          k == 0, k == KT - 1)
                    mm.then_inc(w_used, 1)
                    pe.wait_ge(ba_copied, 1)
                    for n in range(NT):
                        tr = pe.transpose(work[:, 0, n * 16:(n + 1) * 16], baT[:, n * P:(n + 1) * P], cst[0:16, IDENT, 0:16])
                    tr.then_inc(ba_t, 1)
                    pe.wait_ge(col_dve, 3)
                    gg = g[:, :, :].rearrange("p h n -> p (h n)")
                    pe.matmul(work[:, 1, 0:64], cst[:, LE, :], gg, start=True, stop=True)
                    pe.matmul(work[:, 1, 64:128], cst[:, GT_, :], gg, start=True, stop=True)
                    pe.matmul(work[:, 1, 128:192], cst[:, ONES, :], gg, start=True, stop=True).then_inc(col_pe, 1)

                @block.scalar
                def _(act):
                    split_hi(act, 0)
                    split_hi(act, 1)
                    act.wait_ge(w_used, 1)
                    act.activation(baT[:, :], pair[0][0:16, :, :].rearrange("p a b -> p (a b)"), ACT.Copy).then_inc(ba_copied, 1)
                    split_hi(act, 2)
                    act.wait_ge(ba_nat, 1)
                    act.wait_ge(par_in, 32)
                    act.activation(cols[:, :, C_BETA, :], ba[:, :, 0:HEADS].rearrange("p n h -> p h n"), ACT.Tanh,
                                   scale=0.5).then_inc(col_act, 1)
                    act.activation(ea[:, :], alog[:, :], ACT.Exp).then_inc(col_act, 1)
                    act.wait_ge(col_dve, 1)
                    act.activation(az[:, :, :], az[:, :, :], ACT.Exp, scale=-1.0).then_inc(col_act, 1)
                    act.wait_ge(col_act, 3)
                    act.activation(az[:, :, :], az[:, :, :], ACT.Ln, bias=1.0).then_inc(col_act, 1)
                    act.wait_ge(col_pe, 1)
                    act.activation(ex3[:, :, :].rearrange("p a b -> p (a b)"), work[:, 1, 0:192], ACT.Exp).then_inc(col_act, 1)

                @block.vector
                def _(dve):
                    dve.wait_ge(ba_t, 1)
                    dve.tensor_copy(ba[:, :, :].rearrange("p n c -> p (n c)"), work[:, 0, 0:16 * NT]).then_inc(ba_nat, 1)
                    dve.wait_ge(ba_nat, 1)
                    dve.wait_ge(par_in, 32)
                    dve.tensor_tensor(z[:, :, :], ba[:, :, HEADS:2 * HEADS].rearrange("p n h -> p h n"),
                                      dtb[:, :].unsqueeze(2).to_broadcast([P, HEADS, NT]), ALU.add).then_inc(ba_nat, 1)
                    dve.wait_ge(ba_nat, 2)
                    dve.scalar_tensor_tensor(az[:, :, :].rearrange("p h n -> p (h n)"), z[:, :, :].rearrange("p h n -> p (h n)"), -1.0,
                                             z[:, :, :].rearrange("p h n -> p (h n)"), ALU.mult, ALU.max).then_inc(col_dve, 1)
                    dve.wait_ge(col_act, 4)
                    dve.scalar_tensor_tensor(az[:, :, :].rearrange("p h n -> p (h n)"), z[:, :, :].rearrange("p h n -> p (h n)"), 0.0,
                                             az[:, :, :].rearrange("p h n -> p (h n)"), ALU.max, ALU.add).then_inc(col_dve, 1)
                    dve.wait_ge(col_dve, 2)
                    dve.scalar_tensor_tensor(g[:, :, :], az[:, :, :], -1.0,
                                             ea[:, :].unsqueeze(2).to_broadcast([P, HEADS, NT]), ALU.mult, ALU.mult).then_inc(col_dve, 1)
                    dve.wait_ge(col_dve, 3)
                    dve.tensor_copy(cols[:, :, C_G, :], g[:, :, :]).then_inc(col_dve, 1)
                    dve.tensor_scalar(cols[:, :, C_BETA, :], cols[:, :, C_BETA, :], 1.0, 0.5, ALU.add, ALU.mult).then_inc(col_dve, 1)
                    dve.wait_ge(col_dve, 5)
                    dve.tensor_scalar(cols[:, :, C_HB, :], cols[:, :, C_BETA, :], 0.5, None, ALU.mult).then_inc(col_dve, 1)
                    dve.wait_ge(col_act, 5)
                    for n, c in enumerate((C_EG, C_ES, C_EGL)):
                        dve.tensor_copy(cols[:, :, c, :], ex3[:, n, :].rearrange("p (h n) -> p h n", n=NT)).then_inc(col_dve, 1)
                    dve.wait_ge(col_dve, 9)
                    dve.tensor_tensor(cols[:, :, C_BEG, :], cols[:, :, C_BETA, :], cols[:, :, C_EG, :], ALU.mult).then_inc(col_dve, 1)

        gstack = ExitStack()
        gsb = sb_in(gstack)
        gy = gsb("gy", [P, CT, T])
        with ExitStack() as c3:
            s3 = sb_in(c3)
            s5p = s3("s5p", [P, 3, GROUPS])
            s5b = s3("s5b", [P, 2, GROUPS, GI])
            s5c = s3("s5c", [P, 2, GROUPS, GI])
            s5d = s3("s5d", [P, CT])
            q = s3("q", [P, 14, GROUPS])
            are = s3("are", [P, STEP + 1, GROUPS])
            aim = s3("aim", [P, STEP + 1, GROUPS])
            pw = s3("pw", [P, 2, 4, GROUPS])
            ua = s3("ua", [P, STEP, GROUPS])
            va = s3("va", [P, STEP, GROUPS])
            ca = s3("ca", [P, STEP + 1, GROUPS])
            cb = s3("cb", [P, STEP + 1, GROUPS])
            bbst = s3("bbst", [P, GROUPS, GI])
            bbs = s3("bbs", [P, CG, GI])
            pt9 = s3("pt9", [P, CG, STEP + 1, GI])
            mg8 = s3("mg8", [P, CG])
            dsk = s3("dsk", [P, 1])
            rot = s3("rot", [P, 4, CG])
            uT = s3("uT", [P, T])
            un = s3("un", [P, CG, STEP, GI])
            ug = s3("ug", [P, CG, NCH])
            dg = s3("dg", [P, CG, P])
            w1 = s3("w1", [P, CG, P])
            w2 = s3("w2", [P, CG, P])
            p1 = s3("p1", [P, CG, STEP + 1, GI])
            p2 = s3("p2", [P, CG, STEP, GI])
            ctab = s3("ctab", [P, CG, NCH])
            stab = s3("stab", [P, CG, NCH])
            yin = s3("yin", [P, CG, NCH])
            tmp = s3("tmp", [P, CG, NCH])
            t1 = s3("t1", [P, CG, NCH + 1])
            t2 = s3("t2", [P, CG, NCH + 1])
            yT, th, zs = tmp[:, :, :].rearrange("p a b -> p (a b)"), w2[:, :, :].rearrange("p a b -> p (a b)"), yin[:, :, :].rearrange("p a b -> p (a b)")
            ksb = w1[0:GI, :, :]
            LR, LI, DTT, TH, LDT, NN, SN, SH, CC, MAG, MG8, T_A, T_B, DEN = range(14)
            Q = lambda n: q[:, n, :]
            s5_in = sem("s5_in")
            par = sem("par")
            par_act = sem("par_act")
            bb_done = sem("bb_done")
            w_done, w_t, w12_done = sem("s5_w_done"), sem("s5_w_t"), sem("s5_w12_done")
            p_done, tab = sem("s5_p_done"), sem("s5_tab")
            uT_done, u_t, un_done, u_tt, ug_done = (sem(n) for n in ("uT_done", "u_t", "un_done", "u_tt", "ug_done"))
            s_full, state = sem("s_full"), sem("s5_state")
            z_act, z_dve = sem("z_act"), sem("z_dve")
            k_full, k_done, dg_zero = sem("k_full"), sem("k_done"), sem("dg_zero")
            dg_in = sem("dg_in")
            y_full, yn_done, y_t = sem("y_full"), sem("yn_done"), sem("y_t")
            tail_dve, tail_act, tail_pool = sem("tail_dve"), sem("tail_act"), sem("tail_pool")
            turn_end = sem("turn_end")
            pz_done, pz_stored = sem("pz_done"), sem("pz_stored")
            NTAB = 8 + 10 * 6
            with nc.Block() as block:
                @block.sync
                def _(sp):
                    for dst, n in ((s5p, "s5p"), (s5b, "s5b"), (s5c, "s5c"), (s5d, "s5d")):
                        ap = dst[tuple([slice(None)] * len(a[n].shape))]
                        sp.dma_start(ap, a[n]).then_inc(s5_in, 16)
                    sp.sem_inc(pz_stored, 16)
                    with sp.Fori(0, CT) as i:
                        for jr in range(STEP):
                            if jr == 0:
                                sp.wait_ge(dg_zero, i + 1)
                                sp.wait_ge(k_done, i * 2 + 2)
                            sp.dma_start(dg[jr * GI:(jr + 1) * GI, :, (STEP - 1 - jr) * GI:P],
                                         ksb[:, :, 0:(jr + 1) * GI]).then_inc(dg_in, 16)
                        load_w(sp, 4, i, 2)
                        load_w(sp, 5, i, 2)
                        sp.wait_ge(pz_done, i + 1)
                        sp.dma_start(yg_dram[i], zs).then_inc(pz_stored, 16)
                    sp.wait_ge(pz_stored, 16 * CT + 16)

                @block.tensor
                def _(pe):
                    with pe.Fori(0, CT) as i:
                        pe.wait_ge(w_done, i * 3 + 3)
                        for gr in range(CG):
                            tr = pe.transpose(work[:, gr // 4, gr % 4 * P:(gr % 4 + 1) * P], dg[:, gr, :], ident)
                        tr.then_inc(w_t, 1)
                        pe.wait_ge(w_lo, i * 2 + 2)
                        for n in range(2):
                            for k in range(KT):
                                mm = product3(pe, pair[0][:, n, :], wH[:, 1, k * P:(k + 1) * P], wL[:, 1, k * P:(k + 1) * P],
                                              hH[:, k, n * HALF:(n + 1) * HALF], hL[:, k, n * HALF:(n + 1) * HALF], k == 0, k == KT - 1)
                        mm.then_inc(w_used, 1)
                        pe.wait_ge(uT_done, i + 1)
                        for jr in range(STEP):
                            tr = pe.transpose(work[:, 2 + jr // 4, jr % 4 * P:(jr % 4 + 1) * P],
                                              uT[:, STEP - 1 - jr::STEP], ident)
                        tr.then_inc(u_t, 1)
                        pe.wait_ge(un_done, i * 2 + 2)
                        pe.wait_ge(w12_done, i * 6 + 6)
                        for gr in range(CG):
                            tr = pe.transpose(work[:, gr // 4, gr % 4 * P:(gr % 4 + 1) * P],
                                              un[:, gr, :, :].rearrange("p j i -> p (j i)"), ident)
                        tr.then_inc(u_tt, 1)
                        pe.wait_ge(p_done, i * 7 + 7)
                        for gr in range(CG):
                            mm = pe.matmul(work[0:GI, 2 + gr // 4, gr % 4 * P:(gr % 4 + 1) * P], bbs[:, gr, :],
                                           p1[:, gr, 0:STEP, :].rearrange("p k i -> p (k i)"), start=True, stop=True)
                        mm.then_inc(k_full, 1)
                        pe.wait_ge(ug_done, i * 2 + 2)
                        for gr in range(CG):
                            pe.matmul(pair[1][:, gr // 4, gr % 4 * P:(gr % 4 + 1) * P], w1[:, gr, :], ug[:, gr, :], start=True, stop=True)
                            mm = pe.matmul(pair[0][:, gr // 4, gr % 4 * P:(gr % 4 + 1) * P], w2[:, gr, :], ug[:, gr, :], start=True, stop=True)
                        mm.then_inc(s_full, 1)
                        pe.wait_ge(w_lo, i * 2 + 3)
                        for n in range(2):
                            for k in range(KT):
                                mm = product3(pe, work[:, n, :], wH[:, 0, k * P:(k + 1) * P], wL[:, 0, k * P:(k + 1) * P],
                                              hH[:, k, n * HALF:(n + 1) * HALF], hL[:, k, n * HALF:(n + 1) * HALF], k == 0, k == KT - 1)
                        mm.then_inc(w_used, 1)
                        pe.wait_ge(dg_in, i * (16 * STEP) + 16 * STEP)
                        pe.wait_ge(state, i * 13 + 13)
                        for gr in range(CG):
                            dst = pair[0][:, gr // 4, gr % 4 * P:(gr % 4 + 1) * P]
                            pe.matmul(dst, ug[:, gr, :], dg[:, gr, :], start=True, stop=False)
                            pe.matmul(dst, t1[:, gr, 0:NCH], p1[:, gr, 1:STEP + 1, :].rearrange("p k i -> p (k i)"), start=False, stop=False)
                            mm = pe.matmul(dst, t2[:, gr, 0:NCH], p2[:, gr, :, :].rearrange("p k i -> p (k i)"), start=False, stop=True)
                        mm.then_inc(y_full, 1)
                        pe.wait_ge(yn_done, i * 2 + 2)
                        yn = un[:, :, :, :].rearrange("p g j i -> p (g j i)").rearrange("p (j c) -> p j c", j=STEP)
                        for j in range(STEP):
                            tr = pe.transpose(pair[1][:, j // 4, j % 4 * P:(j % 4 + 1) * P], yn[:, j, :], ident)
                        tr.then_inc(y_t, 1)
                        pe.wait_ge(turn_end, i + 1)

                @block.scalar
                def _(act):
                    act.wait_ge(s5_in, 64)
                    act.activation(Q(DTT), s5p[:, 2, :], ACT.Exp).then_inc(par_act, 1)
                    act.wait_ge(par, 11)
                    act.activation(Q(MAG), Q(LDT), ACT.Exp).then_inc(par_act, 1)
                    act.activation(Q(MG8), Q(LDT), ACT.Exp, scale=float(STEP)).then_inc(par_act, 1)
                    act.activation(Q(SN), Q(TH), ACT.Sin).then_inc(par_act, 1)
                    act.activation(Q(SH), Q(TH), ACT.Sin, scale=0.5).then_inc(par_act, 1)
                    with act.Fori(0, CT) as i:
                        act.wait_ge(w_t, i + 1)
                        for n in range(2):
                            src = work[:, n, :].rearrange("p (g s) -> p g s", g=4)
                            act.activation(w1[:, 4 * n:4 * n + 4, :], src, ACT.Copy).then_inc(w12_done, 1)
                        for n in range(2):
                            src = work[:, n, :].rearrange("p (g s) -> p g s", g=4)
                            act.activation(w2[:, 4 * n:4 * n + 4, 0:PS], src[:, :, PS:P], ACT.Copy).then_inc(w12_done, 1)
                            act.activation(w2[:, 4 * n:4 * n + 4, PS:P], src[:, :, 0:PS], ACT.Copy, scale=-1.0).then_inc(w12_done, 1)
                        act.wait_ge(w_used, i * 2 + 2)
                        act.activation(uT[:, :], pair[0][:, :, :].rearrange("p a b -> p (a b)"), ACT.Copy).then_inc(uT_done, 1)
                        split_hi(act, 3, i, 2)
                        act.wait_ge(u_t, i + 1)
                        for n in range(2):
                            act.activation(un[:, :, 4 * n:4 * n + 4, :], work[:, 2 + n, :].rearrange("p (j g i) -> p g j i", j=4, g=CG),
                                           ACT.Copy).then_inc(un_done, 1)
                        act.wait_ge(u_tt, i + 1)
                        for n in range(2):
                            act.activation(ug[:, 4 * n:4 * n + 4, :], work[:, n, :].rearrange("p (g c) -> p g c", g=4), ACT.Copy).then_inc(ug_done, 1)
                        act.wait_ge(k_full, i + 1)
                        act.wait_ge(s_full, i + 1)
                        for n in range(2):
                            act.activation(ksb[:, 4 * n:4 * n + 4, :], work[0:GI, 2 + n, :].rearrange("p (g c) -> p g c", g=4), ACT.Copy).then_inc(k_done, 1)
                        act.wait_ge(w_used, i * 2 + 3)
                        split_hi(act, 4, i, 2)
                        act.activation(th, work[:, 0:2, :].rearrange("p a b -> p (a b)"), ACT.Tanh, scale=0.5).then_inc(z_act, 1)
                        act.wait_ge(y_full, i + 1)
                        for n in range(2):
                            act.activation(un[:, :, :, :].rearrange("p g j i -> p (g j i)").rearrange("p (j g i) -> p g j i", j=STEP, g=CG)[:, 4 * n:4 * n + 4, :, :],
                                           pair[0][:, n, :].rearrange("p (g j i) -> p g j i", g=4, j=STEP), ACT.Copy).then_inc(yn_done, 1)
                        act.wait_ge(tail_dve, i * 3 + 2)
                        act.activation(th, yT, ACT.Square).then_inc(tail_act, 1)
                        act.wait_ge(tail_dve, i * 3 + 3)
                        act.activation(th, th, ACT.Tanh, scale=0.7978845608028654).then_inc(tail_act, 1)

                @block.gpsimd
                def _(pool):
                    pool.wait_ge(par, 30)
                    pool.wait_ge(s5_in, 64)
                    br, bi = s5b[:, 0, :, :], s5b[:, 1, :, :]
                    fr = Q(T_A).unsqueeze(2).to_broadcast([P, GROUPS, GI])
                    fi = Q(T_B).unsqueeze(2).to_broadcast([P, GROUPS, GI])
                    pf = pt9[:, :, :, :].rearrange("p g k i -> p (g k i)")
                    r_, i_ = (pf[:, n * 512:(n + 1) * 512].rearrange("p (g i) -> p g i", i=GI) for n in range(2))
                    n = [0]

                    def link(ins):
                        n[0] += 1
                        ins.then_inc(bb_done, 1)
                        pool.wait_ge(bb_done, n[0])
                    link(pool.tensor_tensor(bbst[:, :, :], fi, bi, ALU.mult))
                    link(pool.tensor_tensor(r_, fr, br, ALU.mult))
                    link(pool.tensor_tensor(r_, r_, bbst[:, :, :], ALU.subtract))
                    link(pool.tensor_tensor(i_, fr, bi, ALU.mult))
                    link(pool.tensor_tensor(bbst[:, :, :], fi, br, ALU.mult))
                    link(pool.tensor_tensor(s5b[:, 1, :, :], i_, bbst[:, :, :], ALU.add))
                    link(pool.tensor_copy(s5b[:, 0, :, :], r_))
                    link(pool.tensor_copy(bbst[0:PS, :, :], s5b[0:PS, 0, :, :]))
                    link(pool.tensor_copy(bbst[PS:P, :, :], s5b[PS:P, 1, :, :]))
                    with pool.Fori(0, CT) as i:
                        split_lo(pool, 3, i, 2)
                        g8 = bass.ds(i * CG, CG)
                        cre = s5c[:, 0, g8, :].unsqueeze(2)
                        cim = s5c[:, 1, g8, :].unsqueeze(2)
                        A = lambda t, k0, k1: t[:, k0:k1, g8].rearrange("p k g -> p g k").unsqueeze(3).to_broadcast([P, CG, k1 - k0, GI])
                        C = lambda t, n: t.to_broadcast([P, CG, n, GI])
                        t9 = pt9[:, :, :, :]
                        t8 = pt9[:, :, 0:STEP, :]
                        m = [0]

                        def step(ins):
                            m[0] += 1
                            ins.then_inc(p_done, 1)
                            pool.wait_ge(p_done, i * 7 + m[0])
                        step(pool.tensor_tensor(p1[:, :, :, :], C(cre, STEP + 1), A(ca, 0, STEP + 1), ALU.mult))
                        step(pool.tensor_tensor(t9, C(cim, STEP + 1), A(cb, 0, STEP + 1), ALU.mult))
                        step(pool.tensor_tensor(p1[:, :, :, :], p1[:, :, :, :], t9, ALU.add))
                        step(pool.tensor_tensor(p2[:, :, :, :], C(cre, STEP), A(cb, 1, STEP + 1), ALU.mult))
                        step(pool.tensor_tensor(t8, C(cim, STEP), A(ca, 1, STEP + 1), ALU.mult))
                        step(pool.tensor_tensor(p2[:, :, :, :], p2[:, :, :, :], t8, ALU.subtract))
                        step(pool.tensor_copy(bbs[:, :, :], bbst[:, g8, :]))
                        split_lo(pool, 4, i, 2)
                        pool.wait_ge(tail_act, i * 2 + 1)
                        pool.tensor_tensor(th, th, yT, ALU.mult).then_inc(tail_pool, 1)
                        pool.wait_ge(turn_end, i + 1)
                        pool.wait_ge(z_dve, i + 1)
                        pool.tensor_tensor(zs, zs, gy[:, i, :], ALU.mult).then_inc(pz_done, 1)

                @block.vector
                def _(dve):
                    n = [0]

                    def link(ins):
                        n[0] += 1
                        ins.then_inc(par, 1)
                        dve.wait_ge(par, n[0])
                    tt = dve.tensor_tensor
                    MAGIC = 1.5 * 2.0 ** 23
                    TWO_PI = (6.28125, 1.9350051879882812e-3, 3.0199159819567e-07)
                    dve.wait_ge(s5_in, 64)
                    link(dve.tensor_scalar(Q(LR), s5p[:, 0, :], -1e-4, None, ALU.min))
                    link(dve.tensor_copy(Q(LI), s5p[:, 1, :]))
                    dve.wait_ge(par_act, 1)
                    link(tt(Q(TH), Q(LI), Q(DTT), ALU.mult))
                    link(tt(Q(LDT), Q(LR), Q(DTT), ALU.mult))
                    link(dve.tensor_scalar(Q(NN), Q(TH), 0.15915494309189535, None, ALU.mult))
                    link(dve.tensor_scalar(Q(NN), Q(NN), MAGIC, None, ALU.add))
                    link(dve.tensor_scalar(Q(NN), Q(NN), MAGIC, None, ALU.subtract))
                    for c in TWO_PI:
                        link(dve.scalar_tensor_tensor(Q(TH), Q(NN), -c, Q(TH), ALU.mult, ALU.add))
                    link(dve.tensor_scalar(Q(TH), Q(TH), 3.1415925, -3.1415925, ALU.min, ALU.max))
                    assert n[0] == 11
                    dve.wait_ge(par_act, 5)
                    link(tt(Q(T_A), Q(SH), Q(SH), ALU.mult))
                    link(dve.tensor_scalar(Q(CC), Q(T_A), -2.0, 1.0, ALU.mult, ALU.add))
                    link(tt(are[:, 1, :], Q(MAG), Q(CC), ALU.mult))
                    link(tt(aim[:, 1, :], Q(MAG), Q(SN), ALU.mult))
                    link(dve.memset(are[:, 0, :], 1.0))
                    link(dve.memset(aim[:, 0, :], 0.0))
                    link(tt(Q(T_A), Q(LR), Q(LR), ALU.mult))
                    link(tt(Q(T_B), Q(LI), Q(LI), ALU.mult))
                    link(tt(Q(DEN), Q(T_A), Q(T_B), ALU.add))
                    link(dve.reciprocal(Q(DEN), Q(DEN)))
                    link(dve.tensor_scalar(Q(NN), are[:, 1, :], 1.0, None, ALU.subtract))
                    link(tt(Q(T_A), Q(NN), Q(LR), ALU.mult))
                    link(tt(Q(T_B), aim[:, 1, :], Q(LI), ALU.mult))
                    link(tt(Q(T_A), Q(T_A), Q(T_B), ALU.add))
                    link(tt(Q(T_A), Q(T_A), Q(DEN), ALU.mult))
                    link(tt(Q(T_B), aim[:, 1, :], Q(LR), ALU.mult))
                    link(tt(Q(TH), Q(NN), Q(LI), ALU.mult))
                    link(tt(Q(T_B), Q(T_B), Q(TH), ALU.subtract))
                    link(tt(Q(T_B), Q(T_B), Q(DEN), ALU.mult))
                    assert n[0] == 30
                    for _r in range(3):
                        link(tt(Q(LDT), Q(CC), Q(CC), ALU.mult))
                        link(tt(Q(NN), Q(SN), Q(SN), ALU.mult))
                        link(dve.scalar_tensor_tensor(Q(SN), Q(CC), 2.0, Q(SN), ALU.mult, ALU.mult))
                        link(tt(Q(CC), Q(LDT), Q(NN), ALU.subtract))
                    for m in (1, 2, 4):
                        sr, si = are[:, 1:m + 1, :], aim[:, 1:m + 1, :]
                        br = are[:, m:m + 1, :].to_broadcast([P, m, GROUPS])
                        bi = aim[:, m:m + 1, :].to_broadcast([P, m, GROUPS])
                        x0, x1 = pw[:, 0, 0:m, :], pw[:, 1, 0:m, :]
                        link(tt(x0, sr, br, ALU.mult))
                        link(tt(x1, si, bi, ALU.mult))
                        link(tt(are[:, m + 1:2 * m + 1, :], x0, x1, ALU.subtract))
                        link(tt(x0, sr, bi, ALU.mult))
                        link(tt(x1, si, br, ALU.mult))
                        link(tt(aim[:, m + 1:2 * m + 1, :], x0, x1, ALU.add))
                    lo_, hi_ = slice(0, PS), slice(PS, P)
                    for dst, rows, src, sgn in ((ua, lo_, are, 1.0), (ua, hi_, aim, 1.0), (va, lo_, aim, -1.0), (va, hi_, are, 1.0),
                                                (ca, lo_, are, 1.0), (ca, hi_, aim, -1.0), (cb, lo_, aim, -1.0), (cb, hi_, are, -1.0)):
                        m = dst.shape[1]
                        link(dve.tensor_scalar(dst[rows, :, :], src[rows, 0:m, :], sgn, None, ALU.mult))
                    link(dve.memset(t1[:, :, 0:1], 0.0))
                    link(dve.memset(t2[:, :, 0:1], 0.0))
                    par_done = n[0]
                    dve.wait_ge(bb_done, 9)
                    with dve.Fori(0, CT) as i:
                        g8 = bass.ds(i * CG, CG)
                        B = lambda c: s5b[:, c, g8, :].unsqueeze(2).to_broadcast([P, CG, STEP, GI])
                        A = lambda t: t[:, :, g8].rearrange("p k g -> p g k").unsqueeze(3).to_broadcast([P, CG, STEP, GI])
                        v4 = lambda t: t[:, :, :].rearrange("p g (k i) -> p g k i", i=GI)
                        tt(v4(dg), B(0), A(ua), ALU.mult).then_inc(w_done, 1)
                        tt(v4(tmp), B(1), A(va), ALU.mult).then_inc(w_done, 1)
                        dve.wait_ge(w_done, i * 3 + 2)
                        tt(v4(dg), v4(dg), v4(tmp), ALU.add).then_inc(w_done, 1)
                        m = [0]

                        def step(ins, wait=True):
                            m[0] += 1
                            ins.then_inc(tab, 1)
                            if wait:
                                dve.wait_ge(tab, i * NTAB + m[0])
                        step(dve.memset(ctab[:, :, 0:1], 1.0))
                        step(dve.memset(stab[:, :, 0:1], 0.0))
                        step(dve.tensor_copy(rot[:, 0, :], q[:, CC, g8]))
                        step(dve.tensor_copy(rot[:, 1, :], q[:, SN, g8]))
                        step(dve.tensor_copy(ctab[:, :, 1:2], rot[:, 0, :].unsqueeze(2)))
                        step(dve.tensor_copy(stab[:, :, 1:2], rot[:, 1, :].unsqueeze(2)))
                        step(dve.tensor_copy(mg8[:, :], q[:, MG8, g8]))
                        step(dve.tensor_copy(dsk[:, :], s5d[:, bass.ds(i, 1)]))
                        k = 2
                        while k < NCH:
                            step(tt(rot[:, 2, :], rot[:, 0, :], rot[:, 0, :], ALU.mult))
                            step(tt(rot[:, 3, :], rot[:, 1, :], rot[:, 1, :], ALU.mult))
                            step(dve.scalar_tensor_tensor(rot[:, 1, :], rot[:, 0, :], 2.0, rot[:, 1, :], ALU.mult, ALU.mult))
                            step(tt(rot[:, 0, :], rot[:, 2, :], rot[:, 3, :], ALU.subtract))
                            cr = rot[:, 0, :].unsqueeze(2).to_broadcast([P, CG, k])
                            sr = rot[:, 1, :].unsqueeze(2).to_broadcast([P, CG, k])
                            x0, x1 = tmp[:, :, 0:k], yin[:, :, 0:k]
                            if k == 2:
                                dve.wait_ge(pz_stored, i * 16 + 16)
                            step(tt(x0, ctab[:, :, 0:k], cr, ALU.mult))
                            step(tt(x1, stab[:, :, 0:k], sr, ALU.mult))
                            step(tt(ctab[:, :, k:2 * k], x0, x1, ALU.subtract))
                            step(tt(x0, ctab[:, :, 0:k], sr, ALU.mult))
                            step(tt(x1, stab[:, :, 0:k], cr, ALU.mult))
                            step(tt(stab[:, :, k:2 * k], x0, x1, ALU.add))
                            k *= 2
                        assert m[0] == NTAB, m[0]
                        dve.wait_ge(w_t, i + 1)
                        dve.memset(dg[:, :, :], 0.0).then_inc(dg_zero, 1)
                        dve.wait_ge(s_full, i + 1)
                        m8 = lambda pp: pp[:, :, :].rearrange("p a (g c) -> p (a g) c", g=4)
                        tt(yin[:, :, :], m8(pair[1]), ctab[:, :, :], ALU.mult).then_inc(state, 1)
                        tt(tmp[:, :, :], m8(pair[0]), stab[:, :, :], ALU.mult).then_inc(state, 1)
                        dve.wait_ge(state, i * 13 + 2)
                        tt(yin[:, :, :], yin[:, :, :], tmp[:, :, :], ALU.add).then_inc(state, 1)
                        dve.wait_ge(state, i * 13 + 3)
                        for gr in range(CG):
                            dve.tensor_tensor_scan(tmp[:, gr, :], mg8[:, gr:gr + 1].to_broadcast([P, NCH]), yin[:, gr, :], 0.0,
                                                   ALU.mult, ALU.add).then_inc(state, 1)
                        dve.wait_ge(state, i * 13 + 11)
                        tt(t1[:, :, 1:NCH + 1], tmp[:, :, :], ctab[:, :, :], ALU.mult).then_inc(state, 1)
                        tt(t2[:, :, 1:NCH + 1], tmp[:, :, :], stab[:, :, :], ALU.mult).then_inc(state, 1)
                        dve.wait_ge(z_act, i + 1)
                        dve.scalar_tensor_tensor(zs, th, 1.0, work[:, 0:2, :].rearrange("p a b -> p (a b)"), ALU.add, ALU.mult).then_inc(z_dve, 1)
                        dve.wait_ge(y_t, i + 1)
                        jc = lambda t, b: t.rearrange("p (c j) -> p j c", j=STEP)[:, 4 * b:4 * b + 4, :]
                        for b in range(2):
                            dve.scalar_tensor_tensor(jc(yT, b), jc(uT[:, :], b), dsk[:, 0:1],
                                                     pair[1][:, b, :].rearrange("p (j c) -> p j c", j=4), ALU.mult, ALU.add).then_inc(tail_dve, 1)
                        dve.wait_ge(tail_pool, i + 1)
                        dve.scalar_tensor_tensor(th, th, 0.044715, yT, ALU.mult, ALU.add).then_inc(tail_dve, 1)
                        dve.wait_ge(tail_act, i * 2 + 2)
                        dve.scalar_tensor_tensor(gy[:, i, :], th, 1.0, yT, ALU.add, ALU.mult).then_inc(turn_end, 1)
                        dve.wait_ge(turn_end, i + 1)

        with ExitStack() as c4:
            s4 = sb_in(c4)
            pz = s4("pz", [P, CT, T])
            gH = s4("gH", [P, CT, T], F32R)
            gL = s4("gL", [P, CT, T], F32R)
            tg = s4("tg", [P, 2, T])
            glub = s4("glub", [P, CT])
            pz_in, gb_in, gH_done, gL_done, hb_done = sem("pz_in"), sem("gb_in"), sem("gH_done"), sem("gL_done"), sem("hb_done")
            glu_full, glu_act, yg_done, yg_stored = sem("glu_full"), sem("glu_act"), sem("yg_done"), sem("yg_stored")
            with nc.Block() as block:
                @block.sync
                def _(sp):
                    sp.dma_start(glub[:, :], a["glub"]).then_inc(gb_in, 16)
                    sp.dma_start(pz[:, :, :], yg_dram.rearrange("m p t -> p m t")).then_inc(pz_in, 16)
                    load_w(sp, 12)
                    for m in range(CT):
                        sp.wait_ge(yg_done, m + 1)
                        sp.dma_start(yg_dram[m], pz[:, m, :]).then_inc(yg_stored, 16)
                    load_w(sp, 13)
                    sp.wait_ge(yg_stored, 16 * CT)

                @block.gpsimd
                def _(pool):
                    for m in range(CT):
                        pool.wait_ge(gH_done, m + 1)
                        pool.tensor_tensor(gL[:, m, :], gy[:, m, :], gH[:, m, :].bitcast(F32), ALU.subtract).then_inc(gL_done, 1)
                    split_lo(pool, 11)
                    split_lo(pool, 12)

                @block.tensor
                def _(pe):
                    pe.wait_ge(gL_done, CT)
                    for m in range(CT):
                        if m % 2 == 0:
                            pe.wait_ge(w_lo, 10 + m // 2)
                        if m >= 2:
                            pe.wait_ge(glu_act, m - 1)
                        sl = (TILE_GLU + m // 2) % 2
                        for n in range(2):
                            for k in range(CT):
                                o = (m % 2) * HALF + k * P
                                mm = product3(pe, pair[m % 2][:, n, :], wH[:, sl, o:o + P], wL[:, sl, o:o + P],
                                              gH[:, k, n * HALF:(n + 1) * HALF], gL[:, k, n * HALF:(n + 1) * HALF], k == 0, k == CT - 1)
                        mm.then_inc(glu_full, 1)
                        if m % 2:
                            pe.wait_ge(glu_full, m + 1)
                            pe.sem_inc(w_used, 1)

                @block.scalar
                def _(act):
                    for m in range(CT):
                        act.activation(gH[:, m, :], gy[:, m, :], ACT.Copy).then_inc(gH_done, 1)
                    act.wait_ge(hb_done, 1)
                    for m in range(CT):
                        act.wait_ge(glu_full, m + 1)
                        if m >= 2:
                            act.wait_ge(yg_done, m - 1)
                        act.activation(tg[:, m % 2, :], pair[m % 2][:, :, :].rearrange("p a b -> p (a b)"), ACT.Tanh,
                                       scale=0.25, bias=glub[:, m:m + 1]).then_inc(glu_act, 1)
                        if m % 2:
                            split_hi(act, 11 + m // 2)

                @block.vector
                def _(dve):
                    dve.wait_ge(gb_in, 16)
                    dve.tensor_scalar(glub[:, :], glub[:, :], 0.5, None, ALU.mult).then_inc(hb_done, 1)
                    dve.wait_ge(pz_in, 16)
                    for m in range(CT):
                        dve.wait_ge(glu_act, m + 1)
                        dve.scalar_tensor_tensor(pz[:, m, :], tg[:, m % 2, :], 1.0, pz[:, m, :], ALU.add, ALU.mult).then_inc(yg_done, 1)
        gstack.close()

        with ExitStack() as c5:
            s5 = sb_in(c5)
            qc, kc, vc = s5("qc", [P, T]), s5("kc", [P, T]), s5("vc", [P, T])
            zs = s5("zs5", [P, T])
            cin = s5("cin", [P, CONV_K - 1 + T])
            acc = s5("acc", [P, T])
            th = s5("th5", [P, T])
            cw_all = s5("cw_all", [P, HEADS, 3 * CONV_K])
            cw = s5("cw", [P, 3 * CONV_K])
            nw = s5("nw", [P, 1])
            col = s5("col", [P, NCOL, NT])
            ssq = s5("ssq", [P, NQ, 3, GT])
            rsq = s5("rsq", [P, NQ, 3, GT])
            cqd = s5("cqd", [P, NQ, GT])
            mh = s5("mh", [P, 2 * GT])
            st = s5("state", [P, P])
            vnew = s5("vnew", [P, P])
            names = ("vb", "kh", "kbg", "kd", "khT", "qd", "qdT", "dec", "decA", "decS", "mm_", "attnT", "mb", "X", "Y", "R", "wT")
            B = {n: s5("d_" + n, [P, NT, P]) for n in names}
            B["qn"], B["kn"], B["rg"], B["attn"], B["on"], B["onx"], B["oz"] = B["X"], B["Y"], B["R"], B["mb"], B["dec"], B["decA"], B["decS"]
            SQ = [B["wT"], B["mb"]]
            tiles4 = lambda n, g: B[n][:, GT * g:GT * g + GT, :]
            flat = lambda n, g: tiles4(n, g).rearrange("p n d -> p (n d)")
            bank4 = lambda b: work[:, b, :].rearrange("p (n d) -> p n d", n=GT)
            rows = lambda c, g: col[:, c, GT * g:GT * g + GT].unsqueeze(2).to_broadcast([P, GT, P])
            mat4 = lambda m: cst[:, m:m + 1, :].to_broadcast([P, GT, P])

            order = ["nq0", "nk0", "nv0", "nq1", "nk1", "nv1", "D0", "D1", "kh0", "qd0", "kh1", "qd1", "kk0", "qk0", "kk1", "qk1",
                     "at0", "m10", "at1", "m11"]
            NL = len(LEVELS)
            for l in range(1, NL):
                order += [f"R0_{l}", f"R1_{l}"]
                order += [f"X0_{l}", f"Y0_{l}", f"X1_{l}", f"Y1_{l}"] if l < NL - 1 else [f"Y0_{l}", f"Y1_{l}"]
            order += ["w0", "w1"]
            banks = [(n, i % 4) for i, n in enumerate(order)]
            for n in range(NT):
                banks += [(f"vn{n}", 0), (f"s{n}", 1)]
            banks += [("o0", 2), ("o1", 3), ("on0", 0), ("on1", 1)]
            per_bank = [sum(b == k for _, b in banks) for k in range(4)]
            use = {n: (b, sum(bb == b for _, bb in banks[:i])) for i, (n, b) in enumerate(banks)}
            per_out = [per_bank[k] - (NT if k == 1 else 0) for k in range(4)]
            use_out = {n: (b, sum(bb == b and m[0] != "s" for m, bb in banks[:i])) for i, (n, b) in enumerate(banks)}
            full = [sem(f"bank_full{b}") for b in range(4)]
            evicted = [sem(f"bank_evicted{b}") for b in range(4)]
            R_ = {n: sem("r_" + n) for n in ("rg", "sqq", "sqk", "ssq", "rr", "kh", "qd", "kbg", "kd", "decI", "decS", "decB", "decA", "cq", "X1",
                                              "sqo", "sso", "ro", "onx", "oz")}
            mb_done, mh_ready = sem("mb_done"), sem("mh_ready")
            col_ready, s_ready, conv_ready, zs_ready = sem("col_ready"), sem("s_ready"), sem("conv_ready"), sem("zs_ready")
            cin_ready, acc_ready, th_ready, conv_step = sem("cin_ready"), sem("acc_ready"), sem("th_ready"), sem("conv_step")
            conv_in, const_ready, nw_ready, oz_stored = sem("conv_in"), sem("const_ready"), sem("nw_ready"), sem("oz_stored")

            class Turn:

                def __init__(self, eng, i):
                    self.eng, self.i = eng, i

                def need(self, name, g):
                    self.eng.wait_ge(R_[name], self.i * NQ + (g + 1))

                def fill(self, name):
                    b, n = use_out[name]
                    self.eng.wait_ge(evicted[b], self.i * per_out[b] + (n + 1))
                    return work[:, b, :]

                def filled(self, name):
                    b, n = use[name]
                    self.eng.wait_ge(full[b], self.i * per_bank[b] + (n + 1))
                    return work[:, b, :]

                def out(self, name):
                    b, n = use_out[name]
                    self.eng.wait_ge(evicted[b], self.i * per_out[b] + (n + 2))

            def full_of(name):
                return full[use[name][0]]

            def evicted_of(name):
                return evicted[use[name][0]]

            def proj_units(pe, base, it, u0, u1):
                for u in range(u0, u1):
                    s, n, k = u // 16, u // 8 % 2, u % 8
                    t = base + s
                    if u % 16 == 0:
                        pe.wait_ge(w_lo, it * 4 + (t + 1))
                        if s == 1:
                            pe.wait_ge(zs_ready, it + 1)
                        else:
                            pe.wait_ge(cin_ready, it * 3 + (3, 0, 4, 5)[s])
                    mm = product3(pe, pair[s % 2][:, n, :], wH[:, t % 2, k * P:(k + 1) * P], wL[:, t % 2, k * P:(k + 1) * P],
                                  hH[:, k, n * HALF:(n + 1) * HALF], hL[:, k, n * HALF:(n + 1) * HALF], k == 0, k == KT - 1)
                    if u % 16 == 15:
                        mm.then_inc(w_used, 1)

            def act_copy(act, base, it, s):
                act.wait_ge(w_used, it * 4 + (base + s + 1))
                act.wait_ge(conv_step, it * 12 + (4 * s + 13))
                act.activation(cin[:, CONV_K - 1:], pair[s % 2][:, :, :].rearrange("p a b -> p (a b)"), ACT.Copy).then_inc(cin_ready, 1)

            def act_tanh(act, it, s):
                act.wait_ge(conv_step, it * 12 + (4 * s + 17))
                if s == 0:
                    act.wait_ge(zs_ready, it + 1)
                else:
                    act.wait_ge(conv_ready, it * 3 + (3 + s))
                act.activation(th[:, :], acc[:, :], ACT.Tanh, scale=0.5).then_inc(th_ready, 1)

            def dve_conv(dve, it, s, tap):
                if tap == 0:
                    dve.wait_ge(cin_ready, it * 3 + (s + 4))
                    dve.wait_ge(conv_ready, it * 3 + (3 + s))
                    dve.tensor_scalar(acc[:, :], cin[:, 0:T], cw[:, CONV_K * s:CONV_K * s + 1], None, ALU.mult).then_inc(conv_step, 1)
                else:
                    dve.wait_ge(conv_step, it * 12 + (4 * s + tap + 13))
                    dve.scalar_tensor_tensor(acc[:, :], cin[:, tap:tap + T], cw[:, CONV_K * s + tap:CONV_K * s + tap + 1], acc[:, :],
                                             ALU.mult, ALU.add).then_inc(conv_step, 1)

            def dve_silu(dve, it, s):
                dve.wait_ge(th_ready, it * 4 + (s + 5))
                dve.scalar_tensor_tensor((qc, kc, vc)[s][:, :], th[:, :], 1.0, acc[:, :], ALU.add, ALU.mult).then_inc(conv_ready, 1)

            def act_z(act, base, it):
                act.wait_ge(w_used, it * 4 + (base + 4))
                act.wait_ge(conv_ready, it * 3 + 6)
                act.activation(th[:, :], pair[1][:, :, :].rearrange("p a b -> p (a b)"), ACT.Tanh, scale=0.5).then_inc(th_ready, 1)

            def dve_z(dve, it):
                dve.wait_ge(th_ready, it * 4 + 8)
                dve.scalar_tensor_tensor(zs[:, :], th[:, :], 1.0, pair[1][:, :, :].rearrange("p a b -> p (a b)"), ALU.add,
                                         ALU.mult).then_inc(zs_ready, 1)

            def dve_cw(dve, head):
                dve.tensor_copy(cw[:, :], cw_all[:, head, :]).then_inc(const_ready, 1)

            def pe_turn(pe, i, proj):
                t = Turn(pe, i)
                base = TILE_HEAD + 4

                def units(u0, u1):
                    if proj:
                        proj_units(pe, base, i, u0, u1)

                def trans(name, src, g):
                    bank = t.fill(name)
                    for n in range(GT):
                        tr = pe.transpose(bank[:, n * P:(n + 1) * P], src(GT * g + n), ident)
                    tr.then_inc(full_of(name), 1)

                def prod(name, lhs, rhs, g):
                    bank = t.fill(name)
                    for n in range(GT):
                        mm = pe.matmul(bank[:, n * P:(n + 1) * P], lhs(GT * g + n), rhs(GT * g + n), start=True, stop=True)
                    mm.then_inc(full_of(name), 1)
                ch = lambda tile: (lambda n: tile[:, n * P:(n + 1) * P])
                bf = lambda name: (lambda n: B[name][:, n, :])
                pe.wait_ge(conv_ready, i * 3 + 3)
                for g in range(NQ):
                    trans(f"nq{g}", ch(qc), g)
                    trans(f"nk{g}", ch(kc), g)
                    trans(f"nv{g}", ch(vc), g)
                    units(4 * g, 4 * g + 4)
                for g in range(NQ):
                    t.need("rg", g)
                    bank = t.fill(f"D{g}")
                    pe.matmul(bank, cst[:, LE, :], flat("rg", g), start=True, stop=True).then_inc(full_of(f"D{g}"), 1)
                    units(8 + 4 * g, 12 + 4 * g)
                for g in range(NQ):
                    t.need("kh", g)
                    trans(f"kh{g}", bf("kh"), g)
                    t.need("qd", g)
                    trans(f"qd{g}", bf("qd"), g)
                    units(16 + 4 * g, 20 + 4 * g)
                for g in range(NQ):
                    t.out(f"kh{g}")
                    prod(f"kk{g}", bf("khT"), bf("khT"), g)
                    prod(f"qk{g}", ch(qc), bf("khT"), g)
                    units(24 + 2 * g, 26 + 2 * g)
                for g in range(NQ):
                    t.out(f"qk{g}")
                    trans(f"at{g}", bf("attn"), g)
                    pe.wait_ge(mb_done, i * (NQ * NL) + (g + 1))
                    trans(f"m1{g}", bf("mb"), g)
                    units(28 + 2 * g, 30 + 2 * g)
                for l in range(1, NL):
                    for g in range(NQ):
                        t.out(f"m1{g}" if l == 1 else f"Y{g}_{l - 1}")
                        pe.wait_ge(mb_done, i * (NQ * NL) + (NQ * l + g + 1))
                        prod(f"R{g}_{l}", bf("mb"), bf("Y"), g)
                    units(30 + 2 * l, 31 + 2 * l)
                    for g in range(NQ):
                        t.out(f"R{g}_{l}")
                        if l > 1:
                            t.out(f"X{g}_{l - 1}")
                        else:
                            t.need("X1", g)
                        if l < NL - 1:
                            prod(f"X{g}_{l}", bf("R"), bf("X"), g)
                        prod(f"Y{g}_{l}", bf("X"), bf("R"), g)
                    units(31 + 2 * l, 32 + 2 * l)
                for g in range(NQ):
                    t.need("kbg", g)
                    t.out(f"Y{g}_{NL - 1}")
                    prod(f"w{g}", bf("kbg"), bf("Y"), g)
                    units(44 + g, 45 + g)
                t.need("kd", 1)
                t.out("w1")
                t.out("at1")
                t.out("qd1")
                t.out("nv1")
                for n in range(NT):
                    g = n // GT
                    bank = t.fill(f"vn{n}")[:, 0:P]
                    pe.wait_ge(s_ready, i * (NT + 1) + (n + 1))
                    pe.matmul(bank, B["Y"][:, n, :], B["vb"][:, n, :], start=True, stop=False)
                    pe.matmul(bank, B["wT"][:, n, :], st[:, :], start=False, stop=True).then_inc(full_of(f"vn{n}"), 1)
                    units(46 + 2 * n, 47 + 2 * n)
                    if n % GT == 0:
                        obank = t.fill(f"o{g}")
                    o = obank[:, n % GT * P:(n % GT + 1) * P]
                    pe.matmul(o, B["qdT"][:, n, :], st[:, :], start=True, stop=False)
                    sbank = t.fill(f"s{n}")[:, 0:P]
                    t.out(f"vn{n}")
                    pe.matmul(sbank, B["kd"][:, n, :], vnew[:, :], start=True, stop=True).then_inc(full_of(f"s{n}"), 1)
                    mm = pe.matmul(o, B["attnT"][:, n, :], vnew[:, :], start=False, stop=True)
                    if n % GT == GT - 1:
                        mm.then_inc(full_of(f"o{g}"), 1)
                    units(47 + 2 * n, 48 + 2 * n)
                units(62, 64)
                pe.wait_ge(s_ready, i * (NT + 1) + (NT + 1))
                for g in range(NQ):
                    t.need("onx", g)
                    trans(f"on{g}", bf("onx"), g)

            def act_turn(act, i, proj):
                t = Turn(act, i)
                base = TILE_HEAD + 4

                def copy(name, dst, g, scale=1.0):
                    act.activation(flat(dst, g), t.filled(name), ACT.Copy, scale=scale).then_inc(evicted_of(name), 1)

                def checkpoint(s):
                    if proj:
                        split_hi(act, base + s + 2, i, 4)
                        if s < 3:
                            act_copy(act, base, i, s)
                copy("nq0", "qn", 0)
                copy("nq1", "qn", 1)
                for g in range(NQ):
                    act.activation(flat("dec", g), t.filled(f"D{g}"), ACT.Exp).then_inc(evicted_of(f"D{g}"), 1)
                copy("kh0", "khT", 0)
                checkpoint(0)
                copy("kh1", "khT", 1)
                for g in range(NQ):
                    copy(f"at{g}", "attnT", g)
                if proj:
                    act_tanh(act, i, 0)
                for l in range(1, NL):
                    for g in range(NQ):
                        copy(f"R{g}_{l}", "R", g)
                    if l == 1:
                        checkpoint(1)
                    if l == NL - 2 and proj:
                        act_tanh(act, i, 1)
                for g in range(NQ):
                    copy(f"w{g}", "wT", g, -1.0)
                for n in range(NT):
                    act.activation(vnew[:, :], t.filled(f"vn{n}")[:, 0:P], ACT.Copy).then_inc(evicted_of(f"vn{n}"), 1)
                    if n == 1:
                        checkpoint(2)
                    if n == GT:
                        copy("o0", "on", 0)
                    if n == NT - 1 and proj:
                        act_tanh(act, i, 2)
                copy("o1", "on", 1)
                checkpoint(3)
                if proj:
                    act_z(act, base, i)

            def dve_turn(dve, i, proj):
                t = Turn(dve, i)
                tt = dve.tensor_tensor

                def conv(s, tap):
                    if proj:
                        dve_conv(dve, i, s, tap)
                dve.tensor_copy(col[:, :, :], cols[:, i, :, :]).then_inc(col_ready, 1)
                dve.memset(st[:, :], 0.0).then_inc(s_ready, 1)
                dve.wait_ge(col_ready, i + 1)
                for g in range(NQ):
                    dve.tensor_copy(flat("kn", g), t.filled(f"nk{g}")).then_inc(evicted_of(f"nk{g}"), 1)
                    t.filled(f"nv{g}")
                    tt(tiles4("vb", g), bank4(use[f"nv{g}"][0]), rows(C_HB, g), ALU.mult).then_inc(evicted_of(f"nv{g}"), 1)
                for g in range(NQ):
                    t.need("sqq", g)
                    t.need("sqk", g)
                    dve.tensor_reduce(ssq[:, g, 0:2, :], SQ[g][:, :, :].rearrange("p (a n) d -> p a n d", a=2), AX, ALU.add).then_inc(R_["ssq"], 1)
                    dve.wait_ge(R_["ssq"], i * (3 * NQ) + (3 * g + 1))
                    dve.tensor_scalar(ssq[:, g, 0, :], ssq[:, g, 0, :], 4 * EPS, float(HD), ALU.add, ALU.mult).then_inc(R_["ssq"], 1)
                    dve.tensor_scalar(ssq[:, g, 1, :], ssq[:, g, 1, :], 4 * EPS, None, ALU.add).then_inc(R_["ssq"], 1)
                for g in range(NQ):
                    t.need("rr", g)
                    tt(tiles4("kh", g), tiles4("kn", g), rsq[:, g, 1, :].unsqueeze(2).to_broadcast([P, GT, P]), ALU.mult).then_inc(R_["kh"], 1)
                for g in range(NQ):
                    dve.tensor_copy(flat("qdT", g), t.filled(f"qd{g}")).then_inc(evicted_of(f"qd{g}"), 1)
                if proj:
                    dve.wait_ge(conv_step, i * 12 + 13)
                    dve_cw(dve, i + 1)
                    dve.wait_ge(const_ready, i + 3)
                for g in range(NQ):
                    t.need("decB", g)
                    tt(flat("mm_", g), t.filled(f"kk{g}"), flat("decS", g), ALU.mult).then_inc(evicted_of(f"kk{g}"), 1)
                    t.need("decA", g)
                    tt(flat("attn", g), t.filled(f"qk{g}"), flat("decA", g), ALU.mult).then_inc(evicted_of(f"qk{g}"), 1)
                    conv(0, 2 * g)
                    conv(0, 2 * g + 1)
                for g in range(NQ):
                    dve.wait_ge(mb_done, i * (NQ * NL) + (g + 1))
                    tt(tiles4("X", g), mat4(IDENT), tiles4("mb", g), ALU.subtract).then_inc(R_["X1"], 1)
                    t.filled(f"m1{g}")
                    tt(tiles4("Y", g), mat4(IDENT), bank4(use[f"m1{g}"][0]), ALU.subtract).then_inc(evicted_of(f"m1{g}"), 1)
                if proj:
                    dve_silu(dve, i, 0)
                for l in range(1, NL):
                    for g in range(NQ):
                        t.filled(f"Y{g}_{l}")
                        if l < NL - 1:
                            tt(flat("X", g), flat("X", g), t.filled(f"X{g}_{l}"), ALU.subtract).then_inc(evicted_of(f"X{g}_{l}"), 1)
                        t.out(f"m1{g}" if l == 1 else f"Y{g}_{l - 1}")
                        tt(flat("Y", g), flat("Y", g), t.filled(f"Y{g}_{l}"), ALU.subtract).then_inc(evicted_of(f"Y{g}_{l}"), 1)
                    if 2 <= l < 6:
                        conv(1, l - 2)
                for n in range(NT):
                    dve.wait_ge(s_ready, i * (NT + 1) + (n + 1))
                    bank = t.filled(f"s{n}")[:, 0:P]
                    dve.scalar_tensor_tensor(st[:, :], st[:, :], col[:, C_EGL, n:n + 1], bank, ALU.mult, ALU.add).then_inc(s_ready, 1)
                    if n == 0 and proj:
                        dve_silu(dve, i, 1)
                    if 2 <= n < 6:
                        conv(2, n - 2)

                def norm(g):
                    t.need("sqo", g)
                    dve.tensor_reduce(ssq[:, g, 2, :], tiles4("onx", g), AX, ALU.add).then_inc(R_["sso"], 1)
                    dve.wait_ge(R_["sso"], i * (2 * NQ) + (2 * g + 1))
                    dve.tensor_scalar(ssq[:, g, 2, :], ssq[:, g, 2, :], 1.0 / HD, EPS, ALU.mult, ALU.add).then_inc(R_["sso"], 1)
                    t.need("ro", g)
                    tt(tiles4("onx", g), tiles4("on", g), rsq[:, g, 2, :].unsqueeze(2).to_broadcast([P, GT, P]), ALU.mult).then_inc(R_["onx"], 1)
                norm(0)
                if proj:
                    dve_silu(dve, i, 2)
                norm(1)
                for g in range(NQ):
                    dve.wait_ge(zs_ready, i + 1)
                    bank = t.filled(f"on{g}")
                    dve.scalar_tensor_tensor(flat("oz", g), bank, nw[:, 0:1], zs[:, g * HALF:(g + 1) * HALF], ALU.mult, ALU.mult).then_inc(R_["oz"], 1)
                    dve.wait_ge(R_["oz"], i * NQ + (g + 1))
                    dve.sem_inc(evicted_of(f"on{g}"), 1)
                if proj:
                    dve_z(dve, i)

            def pool_turn(pool, i, proj):
                t = Turn(pool, i)
                tt = pool.tensor_tensor
                pool.wait_ge(col_ready, i + 1)
                for g in range(NQ):
                    tt(tiles4("rg", g), mat4(GT_), rows(C_G, g), ALU.mult).then_inc(R_["rg"], 1)
                for g in range(NQ):
                    t.out(f"nq{g}")
                    tt(SQ[g][:, 0:GT, :], tiles4("qn", g), tiles4("qn", g), ALU.mult).then_inc(R_["sqq"], 1)
                    t.out(f"nk{g}")
                    tt(SQ[g][:, GT:NT, :], tiles4("kn", g), tiles4("kn", g), ALU.mult).then_inc(R_["sqk"], 1)
                for g in range(NQ):
                    pool.wait_ge(R_["ssq"], i * (3 * NQ) + (3 * g + 3))
                    tt(rsq[:, g, 0:2, :], ssq[:, g, 0:2, :], mh[:, :].rearrange("p (a n) -> p a n", a=2), ALU.pow).then_inc(R_["rr"], 1)
                    t.need("rr", g)
                    tt(cqd[:, g, :], rsq[:, g, 0, :], col[:, C_EG, GT * g:GT * g + GT], ALU.mult).then_inc(R_["cq"], 1)
                    t.need("cq", g)
                    tt(tiles4("qd", g), tiles4("qn", g), cqd[:, g, :].unsqueeze(2).to_broadcast([P, GT, P]), ALU.mult).then_inc(R_["qd"], 1)
                pool.wait_ge(oz_stored, i * (16 * NQ) + 16)
                for g in range(NQ):
                    t.out(f"D{g}")
                    tt(tiles4("decA", g), tiles4("dec", g), mat4(GE), ALU.mult).then_inc(R_["decI"], 1)
                    tt(tiles4("decS", g), tiles4("dec", g), mat4(GT_), ALU.mult).then_inc(R_["decS"], 1)
                    t.need("decS", g)
                    tt(tiles4("decS", g), tiles4("decS", g), rows(C_BETA, g), ALU.mult).then_inc(R_["decB"], 1)
                    t.need("decI", g)
                    tt(tiles4("decA", g), tiles4("decA", g), rsq[:, g, 0, :].unsqueeze(2).to_broadcast([P, GT, P]), ALU.mult).then_inc(R_["decA"], 1)
                if proj:
                    split_lo(pool, TILE_HEAD + 6, i, 4)

                def level(l):
                    for g in range(NQ):
                        if l == 0:
                            t.out(f"kk{g}")
                            t.filled(f"at{g}")
                        elif l == 1:
                            t.filled(f"m1{g}")
                            t.need("X1", g)
                        else:
                            t.filled(f"R{g}_{l - 1}")
                        tt(tiles4("mb", g), tiles4("mm_", g), mat4(LEVEL0 + l), ALU.mult).then_inc(mb_done, 1)
                level(0)
                level(1)
                for g in range(NQ):
                    t.need("kh", g)
                    tt(tiles4("kbg", g), tiles4("kh", g), rows(C_BEG, g), ALU.mult).then_inc(R_["kbg"], 1)
                level(2)
                for g in range(NQ):
                    tt(tiles4("kd", g), tiles4("kh", g), rows(C_ES, g), ALU.mult).then_inc(R_["kd"], 1)
                if proj:
                    split_lo(pool, TILE_HEAD + 7, i, 4)
                for l in range(3, NL):
                    level(l)
                if proj:
                    split_lo(pool, TILE_HEAD + 8, i, 4)
                for g in range(NQ):
                    t.out(f"o{g}")
                    tt(tiles4("onx", g), tiles4("on", g), tiles4("on", g), ALU.mult).then_inc(R_["sqo"], 1)
                    pool.wait_ge(R_["sso"], i * (2 * NQ) + (2 * g + 2))
                    tt(rsq[:, g, 2, :], ssq[:, g, 2, :], mh[:, 0:GT], ALU.pow).then_inc(R_["ro"], 1)
                if proj:
                    split_lo(pool, TILE_HEAD + 9, i, 4)

            def sp_turn(sp, i, proj):
                if proj:
                    for s in range(4):
                        load_w(sp, TILE_HEAD + 7 + s, i, 4)
                for g in range(NQ):
                    sp.wait_ge(R_["oz"], i * NQ + (g + 1))
                    sp.dma_start(oz_dram[i][:, g * HALF:(g + 1) * HALF], flat("oz", g)).then_inc(oz_stored, 16)

            with nc.Block() as block:
                @block.sync
                def _(sp):
                    sp.dma_start(cw_all[:, :, :], a["conv"]).then_inc(conv_in, 16)
                    sp.dma_start(nw[:, :], a["normw"]).then_inc(conv_in, 16)
                    sp.sem_inc(oz_stored, 16)
                    load_w(sp, TILE_HEAD + 3)
                    for s in range(3):
                        load_w(sp, TILE_HEAD + 4 + s)
                    with sp.Fori(0, HEADS - 1) as i:
                        sp_turn(sp, i, True)
                    sp_turn(sp, HEADS - 1, False)
                    sp.wait_ge(oz_stored, 16 * NQ * HEADS + 16)

                @block.tensor
                def _(pe):
                    for u in range(64):
                        s, n, k = u // 16, u // 8 % 2, u % 8
                        t = TILE_HEAD + s
                        if u % 16 == 0:
                            pe.wait_ge(w_lo, t + 1)
                            if s >= 2:
                                pe.wait_ge(cin_ready, 1 + s - 2)
                        mm = product3(pe, pair[s % 2][:, n, :], wH[:, t % 2, k * P:(k + 1) * P], wL[:, t % 2, k * P:(k + 1) * P],
                                      hH[:, k, n * HALF:(n + 1) * HALF], hL[:, k, n * HALF:(n + 1) * HALF], k == 0, k == KT - 1)
                        if u % 16 == 15:
                            mm.then_inc(w_used, 1)
                    for b in range(4):
                        pe.sem_inc(evicted[b], 1)
                    with pe.Fori(0, HEADS - 1) as i:
                        pe_turn(pe, i, True)
                    pe_turn(pe, HEADS - 1, False)

                @block.scalar
                def _(act):
                    for s in range(4):
                        if s < 3:
                            act.wait_ge(w_used, TILE_HEAD + s + 1)
                            act.wait_ge(conv_step, 4 * s + 1)
                            act.activation(cin[:, CONV_K - 1:], pair[s % 2][:, :, :].rearrange("p a b -> p (a b)"), ACT.Copy).then_inc(cin_ready, 1)
                            split_hi(act, TILE_HEAD + 2 + s)
                            act.wait_ge(conv_step, 4 * s + 5)
                            if s:
                                act.wait_ge(conv_ready, s)
                            act.activation(th[:, :], acc[:, :], ACT.Tanh, scale=0.5).then_inc(th_ready, 1)
                        else:
                            act.wait_ge(w_used, TILE_HEAD + 4)
                            split_hi(act, TILE_HEAD + 5)
                            act.wait_ge(conv_ready, 3)
                            act.activation(th[:, :], pair[1][:, :, :].rearrange("p a b -> p (a b)"), ACT.Tanh, scale=0.5).then_inc(th_ready, 1)
                    with act.Fori(0, HEADS - 1) as i:
                        act_turn(act, i, True)
                    act_turn(act, HEADS - 1, False)

                @block.gpsimd
                def _(pool):
                    pool.memset(mh[:, :], -0.5).then_inc(mh_ready, 1)
                    pool.wait_ge(mh_ready, 1)
                    for s in range(4):
                        split_lo(pool, TILE_HEAD + 2 + s)
                    with pool.Fori(0, HEADS - 1) as i:
                        pool_turn(pool, i, True)
                    pool_turn(pool, HEADS - 1, False)

                @block.vector
                def _(dve):
                    dve.memset(cin[:, 0:CONV_K - 1], 0.0).then_inc(const_ready, 1)
                    dve.sem_inc(conv_step, 1)
                    dve.wait_ge(conv_in, 32)
                    dve_cw(dve, 0)
                    dve.wait_ge(const_ready, 2)
                    dve.tensor_scalar(nw[:, :], nw[:, :], 0.5, None, ALU.mult).then_inc(nw_ready, 1)
                    dve.wait_ge(nw_ready, 1)
                    for s in range(3):
                        dve.wait_ge(cin_ready, s + 1)
                        if s:
                            dve.wait_ge(conv_ready, s)
                        dve.tensor_scalar(acc[:, :], cin[:, 0:T], cw[:, CONV_K * s:CONV_K * s + 1], None, ALU.mult).then_inc(conv_step, 1)
                        for tap in range(1, CONV_K):
                            dve.wait_ge(conv_step, 4 * s + tap + 1)
                            dve.scalar_tensor_tensor(acc[:, :], cin[:, tap:tap + T], cw[:, CONV_K * s + tap:CONV_K * s + tap + 1], acc[:, :],
                                                     ALU.mult, ALU.add).then_inc(conv_step, 1)
                        dve.wait_ge(th_ready, s + 1)
                        dve.scalar_tensor_tensor((qc, kc, vc)[s][:, :], th[:, :], 1.0, acc[:, :], ALU.add, ALU.mult).then_inc(conv_ready, 1)
                    dve.wait_ge(th_ready, 4)
                    dve.scalar_tensor_tensor(zs[:, :], th[:, :], 1.0, pair[1][:, :, :].rearrange("p a b -> p (a b)"), ALU.add,
                                             ALU.mult).then_inc(zs_ready, 1)
                    with dve.Fori(0, HEADS - 1) as i:
                        dve_turn(dve, i, True)
                    dve_turn(dve, HEADS - 1, False)

        dstack.close()

        with ExitStack() as c6:
            s6 = sb_in(c6)
            ozH, ozL = s6("ozH", [P, HEADS, T], F32R), s6("ozL", [P, HEADS, T], F32R)
            ygH, ygL = s6("ygH", [P, CT, T], F32R), s6("ygL", [P, CT, T], F32R)
            stg = s6("stg", [P, 4, T])
            TA, TB, M1, MG = range(4)
            NB = HEADS + CT
            b_landed = [sem(f"b_landed{n}") for n in range(4)]
            bH_done, bL_pool, bL_dve = sem("bH_done"), sem("bL_pool"), sem("bL_dve")
            gate_act = sem("gate_act")
            merge_dve = sem("merge_dve")
            mg_stored = sem("mg_stored")
            hi_of = lambda j: ozH[:, j, :] if j < HEADS else ygH[:, j - HEADS, :]
            lo_of = lambda j: ozL[:, j, :] if j < HEADS else ygL[:, j - HEADS, :]

            def branch_lo(eng, j, done):
                eng.wait_ge(bH_done, j + 1)
                eng.tensor_tensor(lo_of(j), stg[:, j % 4, :], hi_of(j).bitcast(F32), ALU.subtract).then_inc(done, 1)

            def merge_pe(pe, i):
                for s, (dst, xh, xl, kt) in enumerate(((pair[0], hH, hL, KT), (pair[1], hH, hL, KT),
                                                       (work[:, 0:2, :], ozH, ozL, HEADS), (work[:, 2:4, :], ygH, ygL, CT))):
                    t = TILE_MERGE + s
                    pe.wait_ge(w_lo, i * 4 + (t + 1))
                    if s < 2:
                        pe.wait_ge(gate_act, i * 2 + (s + 1))
                    else:
                        pe.wait_ge(merge_dve, i * 4 + (2 * s - 3))
                    if s == 2:
                        pe.wait_ge(bL_pool, NB // 2)
                        pe.wait_ge(bL_dve, NB // 2)
                    for n in range(2):
                        for k in range(kt):
                            mm = product3(pe, dst[:, n, :], wH[:, t % 2, k * P:(k + 1) * P], wL[:, t % 2, k * P:(k + 1) * P],
                                          xh[:, k, n * HALF:(n + 1) * HALF], xl[:, k, n * HALF:(n + 1) * HALF], k == 0, k == kt - 1)
                    mm.then_inc(w_used, 1)

            def merge_act(act, i, last):
                for s in range(4):
                    act.wait_ge(w_used, i * 4 + (TILE_MERGE + s + 1))
                    if not (last and s >= 2):
                        split_hi(act, TILE_MERGE + 2 + s, i, 4)
                    if s < 2:
                        act.wait_ge(merge_dve, i * 4 + (2 * s + 1))
                        act.activation(stg[:, (TA, TB)[s], :], pair[s][:, :, :].rearrange("p a b -> p (a b)"), ACT.Tanh,
                                       scale=0.5).then_inc(gate_act, 1)

            def merge_dve_turn(dve, i):
                dve.wait_ge(gate_act, i * 2 + 4)
                dve.wait_ge(w_used, i * 4 + (TILE_MERGE + 3))
                dve.wait_ge(merge_dve, i * 4 + 4)
                dve.scalar_tensor_tensor(stg[:, M1, :], stg[:, TA, :], 1.0, work[:, 0:2, :].rearrange("p a b -> p (a b)"),
                                         ALU.add, ALU.mult).then_inc(merge_dve, 1)
                dve.tensor_scalar(stg[:, TB, :], stg[:, TB, :], 1.0, 0.125, ALU.add, ALU.mult).then_inc(merge_dve, 1)
                dve.wait_ge(w_used, i * 4 + (TILE_MERGE + 4))
                dve.wait_ge(merge_dve, i * 4 + 6)
                dve.wait_ge(mg_stored, i * 16 + 16)
                dve.tensor_tensor(stg[:, MG, :], stg[:, TB, :], work[:, 2:4, :].rearrange("p a b -> p (a b)"), ALU.mult).then_inc(merge_dve, 1)
                dve.wait_ge(merge_dve, i * 4 + 7)
                dve.tensor_tensor(stg[:, MG, :], stg[:, M1, :], stg[:, MG, :], ALU.add).then_inc(merge_dve, 1)

            def merge_sp(sp, i, last):
                for s in range(1 if last else 4):
                    load_w(sp, TILE_MERGE + 3 + s, i, 4)
                sp.wait_ge(merge_dve, i * 4 + 8)
                sp.dma_start(mg_dram[i], stg[:, MG, :]).then_inc(mg_stored, 16)

            with nc.Block() as block:
                @block.sync
                def _(sp):
                    for j in range(NB):
                        if j >= 4:
                            sp.wait_ge((bL_pool, bL_dve)[j % 2], (j - 4) // 2 + 1)
                        sp.dma_start(stg[:, j % 4, :], oz_dram[j] if j < HEADS else yg_dram[j - HEADS]).then_inc(b_landed[j % 4], 16)
                    sp.sem_inc(mg_stored, 16)
                    with sp.Fori(0, KT - 1) as i:
                        merge_sp(sp, i, False)
                    merge_sp(sp, KT - 1, True)
                    sp.wait_ge(mg_stored, 16 * KT + 16)

                @block.tensor
                def _(pe):
                    with pe.Fori(0, KT) as i:
                        merge_pe(pe, i)

                @block.scalar
                def _(act):
                    act.sem_inc(gate_act, 2)
                    for j in range(NB):
                        act.wait_ge(b_landed[j % 4], 16 * (j // 4 + 1))
                        act.activation(hi_of(j), stg[:, j % 4, :], ACT.Copy).then_inc(bH_done, 1)
                    act.wait_ge(bL_pool, NB // 2)
                    act.wait_ge(bL_dve, NB // 2)
                    with act.Fori(0, KT - 1) as i:
                        merge_act(act, i, False)
                    merge_act(act, KT - 1, True)

                @block.gpsimd
                def _(pool):
                    for j in range(0, NB, 2):
                        branch_lo(pool, j, bL_pool)
                    with pool.Fori(0, KT - 1) as i:
                        for s in range(4):
                            split_lo(pool, TILE_MERGE + 2 + s, i, 4)
                    for s in range(2):
                        split_lo(pool, TILE_MERGE + 2 + s, KT - 1, 4)

                @block.vector
                def _(dve):
                    for j in range(1, NB, 2):
                        branch_lo(dve, j, bL_dve)
                    dve.wait_ge(bL_pool, NB // 2)
                    dve.sem_inc(merge_dve, 4)
                    with dve.Fori(0, KT) as i:
                        merge_dve_turn(dve, i)
        hstack.close()

        with ExitStack() as c7:
            s7 = sb_in(c7)
            wo = s7("wo", [P, KT, D])
            woH, woL = s7("woH", [P, KT, D], F32R), s7("woL", [P, KT, D], F32R)
            wg = s7("wg", [P, KT, D // 2])
            cT7 = s7("cT7", [P, KT])
            cTb = s7("cTb", [P, KT, P])
            gate = s7("gate", [P, D])
            fnw = s7("fnw", [P, D])
            xt = s7("xt", [P, 2, D])
            y = s7("y", [P, 2, D])
            ss = s7("ss7", [P, 2])
            rs = s7("rs7", [P, 2])
            mh = s7("mh7", [P, 1])
            wo_in = [sem(f"wo_in{k}") for k in range(KT)]
            woH_done, woL_pool, woL_dve = sem("woH_done"), sem("woL_pool"), sem("woL_dve")
            c7_in, bg_in, fn_in, wg_in = sem("c7_in"), sem("bg_in"), sem("fn_in"), sem("wg_in")
            cTb_done, gate_full, gate_done = sem("cTb_done"), sem("gate_full"), sem("gate_done")
            x7_in, out_stored = [sem("x7_in0"), sem("x7_in1")], [sem("out_stored0"), sem("out_stored1")]
            out_dve = sem("out_dve")
            sq7_done, rs_done, mh7_done = sem("sq7_done"), sem("rs_done"), sem("mh7_done")
            mgv = mg_dram.rearrange("m p (n t) -> n p m t", n=NT)
            with nc.Block() as block:
                @block.sync
                def _(sp):
                    def load_merged(i, s):
                        t = TILE_OUT + s
                        sp.wait_ge(w_lo, i * 2 + (t - 1))
                        sp.dma_start(raw[:, t % 2, :].rearrange("p (m t) -> p m t", m=KT), mgv[i * 2 + s]).then_inc(w_landed[t % 2], 16)
                    for k in range(KT):
                        sp.dma_start(wo[:, k, :], a["wout"][:, k, :]).then_inc(wo_in[k], 16)
                    for s in range(2):
                        sp.sem_inc(out_stored[s], 16)
                    with sp.Fori(0, NT // 2) as i:
                        for s in range(2):
                            load_merged(i, s)
                        for s in range(2):
                            sp.wait_ge(out_dve, i * 8 + (4 * s + 2))
                            sp.dma_start(xt[:, s, :], a["x"][i * 2 + s]).then_inc(x7_in[s], 16)
                        for s in range(2):
                            sp.wait_ge(out_dve, i * 8 + (4 * s + 12))
                            sp.dma_start(out[0].rearrange("(n p) d -> n p d", p=P)[i * 2 + s], y[:, s, :]).then_inc(out_stored[s], 16)
                    for s in range(2):
                        sp.wait_ge(out_stored[s], 16 * (NT // 2) + 16)

                @block.tensor
                def _(pe):
                    pe.wait_ge(cTb_done, 1)
                    for n in range(2):
                        pe.wait_ge(wg_in, 16 * n + 16)
                        for k in range(KT):
                            mm = pe.matmul(work[:, n, :], cTb[:, k, :], wg[:, k, :], start=(k == 0), stop=(k == KT - 1))
                        mm.then_inc(gate_full, 1)
                    pe.wait_ge(woL_pool, KT // 2)
                    pe.wait_ge(woL_dve, KT // 2)
                    with pe.Fori(0, NT // 2) as i:
                        for s in range(2):
                            t = TILE_OUT + s
                            pe.wait_ge(w_lo, i * 2 + (t + 1))
                            pe.wait_ge(out_dve, i * 8 + (4 * s + 1))
                            for n in range(2):
                                for k in range(KT):
                                    mm = product3(pe, pair[s][:, n, :], wH[:, t % 2, k * P:(k + 1) * P], wL[:, t % 2, k * P:(k + 1) * P],
                                                  woH[:, k, n * HALF:(n + 1) * HALF], woL[:, k, n * HALF:(n + 1) * HALF], k == 0, k == KT - 1)
                            mm.then_inc(w_used, 1)

                @block.scalar
                def _(act):
                    act.dma_start(cT7[:, :], a["cT"]).then_inc(c7_in, 16)
                    act.dma_start(gate[:, :], a["bgate"]).then_inc(bg_in, 16)
                    act.dma_start(fnw[:, :], a["fnw"]).then_inc(fn_in, 16)
                    act.dma_start(wg[:, :, :], a["wada"][2][:, :, 0:HALF]).then_inc(wg_in, 16)
                    for k in range(KT):
                        act.wait_ge(wo_in[k], 16)
                        act.activation(woH[:, k, :], wo[:, k, :], ACT.Copy).then_inc(woH_done, 1)
                    act.wait_ge(gate_full, 1)
                    act.dma_start(wg[:, :, :], a["wada"][2][:, :, HALF:D]).then_inc(wg_in, 16)
                    act.sem_inc(sq7_done, 1)
                    with act.Fori(0, NT // 2) as i:
                        for s in range(2):
                            split_hi(act, TILE_OUT + s, i, 2)
                        for s in range(2):
                            act.wait_ge(out_dve, i * 8 + (4 * s + 10))
                            act.wait_ge(sq7_done, i * 2 + (s + 1))
                            act.activation(wo[:, 0, :], y[:, s, :], ACT.Square, accum_out=ss[:, s:s + 1]).then_inc(sq7_done, 1)

                @block.gpsimd
                def _(pool):
                    pool.memset(mh[:, :], -0.5).then_inc(mh7_done, 1)
                    pool.wait_ge(mh7_done, 1)
                    for k in range(0, KT, 2):
                        pool.wait_ge(woH_done, k + 1)
                        pool.tensor_tensor(woL[:, k, :], wo[:, k, :], woH[:, k, :].bitcast(F32), ALU.subtract).then_inc(woL_pool, 1)
                    with pool.Fori(0, NT // 2) as i:
                        for s in range(2):
                            split_lo(pool, TILE_OUT + s, i, 2)
                        for s in range(2):
                            pool.wait_ge(out_dve, i * 8 + (4 * s + 11))
                            pool.tensor_tensor(rs[:, s:s + 1], ss[:, s:s + 1], mh[:, :], ALU.pow).then_inc(rs_done, 1)

                @block.vector
                def _(dve):
                    dve.wait_ge(c7_in, 16)
                    dve.tensor_copy(cTb[:, :, :], cT7[:, :].unsqueeze(2).to_broadcast([P, KT, P])).then_inc(cTb_done, 1)
                    for k in range(1, KT, 2):
                        dve.wait_ge(woH_done, k + 1)
                        dve.tensor_tensor(woL[:, k, :], wo[:, k, :], woH[:, k, :].bitcast(F32), ALU.subtract).then_inc(woL_dve, 1)
                    dve.wait_ge(woL_pool, KT // 2)
                    dve.wait_ge(bg_in, 16)
                    dve.wait_ge(gate_full, 2)
                    dve.tensor_tensor(gate[:, :], gate[:, :], work[:, 0:2, :].rearrange("p a b -> p (a b)"), ALU.add).then_inc(gate_done, 1)
                    dve.wait_ge(gate_done, 1)
                    dve.tensor_scalar(gate[:, :], gate[:, :], 0.5, None, ALU.mult).then_inc(gate_done, 1)
                    dve.wait_ge(gate_done, 2)
                    dve.wait_ge(fn_in, 16)
                    dve.sem_inc(out_dve, 8)
                    with dve.Fori(0, NT // 2) as i:
                        for s in range(2):
                            dve.wait_ge(w_used, i * 2 + (TILE_OUT + s + 1))
                            dve.wait_ge(out_stored[s], i * 16 + 16)
                            dve.tensor_tensor(y[:, s, :], pair[s][:, :, :].rearrange("p a b -> p (a b)"), gate[:, :], ALU.mult).then_inc(out_dve, 1)
                            dve.wait_ge(out_dve, i * 8 + (4 * s + 9))
                            dve.wait_ge(x7_in[s], i * 16 + 16)
                            dve.tensor_tensor(y[:, s, :], y[:, s, :], xt[:, s, :], ALU.add).then_inc(out_dve, 1)
                            dve.wait_ge(sq7_done, i * 2 + (s + 2))
                            dve.tensor_scalar(ss[:, s:s + 1], ss[:, s:s + 1], 1.0 / D, EPS, ALU.mult, ALU.add).then_inc(out_dve, 1)
                            dve.wait_ge(rs_done, i * 2 + (s + 1))
                            dve.scalar_tensor_tensor(y[:, s, :], y[:, s, :], rs[:, s:s + 1], fnw[:, :], ALU.mult, ALU.mult).then_inc(out_dve, 1)


_OUTS = [((1, T, D), 'float32')]


def _layout(i):
    import numpy as np
    f = lambda n: np.asarray(i[n])
    w_in = f('w_in')[0]
    qkvz = 4 * HEADS * HD
    u0 = qkvz + 2 * HEADS

    def tiles(w, col, n=1):
        k = w.shape[0] // P
        return np.concatenate([w[:, col + P * m:col + P * (m + 1)].reshape(k, P, P).transpose(1, 0, 2).reshape(P, k * P)[None]
                               for m in range(n)])
    glu, wa, wb = f('s5_glu_w')[0], f('w_proj_a')[0], f('w_proj_b')[0]
    parts = [tiles(w_in, qkvz)]
    for m in range(CT):
        parts += [tiles(w_in, u0 + m * P), tiles(w_in, u0 + S5W + m * P)]
    gt = tiles(glu, 0, CT)
    parts.append(np.stack([np.concatenate([gt[2 * m], gt[2 * m + 1]], 1) for m in range(2)]))
    for h in range(HEADS):
        for s in range(4):
            parts.append(tiles(w_in, s * HEADS * HD + h * HD))
    for m in range(KT):
        parts.append(tiles(w_in, u0 + 2 * S5W + m * P))
        parts.append(tiles(w_in, u0 + 2 * S5W + D + m * P))
        parts.append(tiles(wa, m * P))
        b = tiles(wb, m * P)
        parts.append(np.concatenate([b, b], 2))
    col = lambda v: v.reshape(-1, P).T
    ada = f('w_ada')[0].reshape(KT, P, 3, D).transpose(2, 1, 0, 3)
    dup = lambda v: np.concatenate([v, v], 0)
    p_, f_ = np.arange(P)[:, None], np.arange(P)[None, :]
    cst = [p_ == f_, p_ <= f_, p_ > f_, p_ >= f_, p_ >= 0 * f_]
    cst += [(p_ // (2 * b) == f_ // (2 * b)) & (p_ % (2 * b) >= b) & (f_ % (2 * b) < b) for b in LEVELS]
    conv = f('dn_conv_w')[0].reshape(CONV_K, 3, HEADS, P).transpose(3, 2, 1, 0)
    d = {
        'w': np.concatenate(parts),
        'x': f('x')[0].reshape(NT, P, D),
        'cT': col(f('c')[0]),
        'bada': col(f('b_ada')[0])[:, 0:2 * KT],
        'bgate': np.broadcast_to(f('b_ada')[0][2 * D:], (P, D)),
        'wada': ada,
        'cst': np.stack([np.broadcast_to(m, (P, P)).astype(np.float32) for m in cst], 1),
        'dtb': np.broadcast_to(f('dn_dt_bias')[0], (P, HEADS)),
        'alog': np.broadcast_to(f('dn_a_log')[0], (P, HEADS)),
        'conv': conv.reshape(P, HEADS, 3 * CONV_K),
        'normw': f('dn_norm_w')[0].reshape(P, 1),
        's5p': np.stack([dup(f('s5_lambda_re')[0].T), dup(f('s5_lambda_im')[0].T),
                         np.broadcast_to(f('s5_log_dt')[0], (P, GROUPS))], 1),
        's5b': np.stack([dup(f('s5_b_re')[0].transpose(1, 0, 2)), dup(f('s5_b_im')[0].transpose(1, 0, 2))], 1),
        's5c': np.stack([dup(f('s5_c_re')[0].transpose(2, 0, 1)), dup(f('s5_c_im')[0].transpose(2, 0, 1))], 1),
        's5d': col(f('s5_d')[0]),
        'glub': col(f('s5_glu_b')[0]),
        'wout': f('w_out')[0].reshape(KT, P, D).transpose(1, 0, 2),
        'fnw': np.broadcast_to(f('final_norm_w'), (P, D)),
    }
    return {k: np.ascontiguousarray(v) for k, v in d.items()}


def kernel(**inputs):
    import numpy as _np
    import concourse.bacc as _bacc
    from concourse.bass_utils import run_bass_kernel_spmd as _run

    nc = _bacc.Bacc("TRN2", target_bir_lowering=False, num_devices=1)
    arrays, aps = {}, {}
    for name, v in _layout(inputs).items():
        arrays[f"in_{name}_dram"] = v
        aps[name] = nc.dram_tensor(f"in_{name}_dram", v.shape, mybir.dt.from_np(v.dtype), kind="ExternalInput").ap()
    out = nc.dram_tensor("out_0_dram", (1, T, D), F32, kind="ExternalOutput").ap()
    oz = nc.dram_tensor("oz_scratch", (HEADS, P, T), F32, kind="Internal").ap()
    yg = nc.dram_tensor("yg_scratch", (CT, P, T), F32, kind="Internal").ap()
    mg = nc.dram_tensor("mg_scratch", (KT, P, T), F32, kind="Internal").ap()
    build_program(nc, aps, out, oz, yg, mg)
    r = _run(nc, [arrays], core_ids=[0])
    return r.results[0]["out_0_dram"]
```

```python
from contextlib import ExitStack
import concourse.bass as bass
from concourse import mybir

P = 128
D = 1024
T = 1024
HEADS, HD = 8, 128
KT = D // P
NT = T // P
HALF = T // 2
CONV_K = 4
S5W, GROUPS, GI, PS = 512, 32, 16, 64
CT = S5W // P
CG = P // GI
STEP = 8
NCH = T // STEP
EPS = 1e-6
CW = 256
CK = D // CW
NQ = 2
GT = NT // NQ

TILE_BA, TILE_UZ, TILE_GLU, TILE_HEAD = 0, 1, 9, 11
TILE_MERGE = TILE_HEAD + 4 * HEADS
TILE_OUT = TILE_MERGE + 4 * KT
LEVELS = (1, 2, 4, 8, 16, 32, 64)
IDENT, LE, GT_, GE, ONES, LEVEL0 = 0, 1, 2, 3, 4, 5
NCONST = LEVEL0 + len(LEVELS)
C_G, C_BETA, C_EG, C_ES, C_EGL, C_BEG, C_HB = range(7)
NCOL = 7

F32, F32R = mybir.dt.float32, mybir.dt.float32r
I32 = mybir.dt.int32
ACT = mybir.ActivationFunctionType
ALU = mybir.AluOpType
AX = mybir.AxisListType.X


def bc(ap, shape):
    return ap.to_broadcast(shape)


def build_program(nc, a, out, oz_dram, yg_dram, mg_dram):
    ctx = ExitStack()
    with ctx:
        def sb_in(c):
            return lambda name, shape, dt=F32: c.enter_context(nc.sbuf_tensor(name, shape, dt))

        def sem(name):
            return ctx.enter_context(nc.semaphore(name))

        sb = sb_in(ctx)
        cst = sb("cst", [P, NCONST, P])
        cT = sb("cT", [P, KT])
        bada = sb("bada", [P, 3 * KT])
        modT = sb("modT", [P, 3 * KT])
        raw = sb("raw", [P, 2, D])
        wH = sb("wH", [P, 2, D], F32R)
        wL = sb("wL", [P, 2, D], F32R)
        pair = [ctx.enter_context(nc.psum_tensor(f"pair{n}", [P, 2, HALF], F32)) for n in range(2)]
        work = ctx.enter_context(nc.psum_tensor("work", [P, 4, 512], F32))
        ident = cst[:, IDENT, :]

        w_landed = [sem("w_landed0"), sem("w_landed1")]
        w_hi = sem("w_hi")
        w_lo = sem("w_lo")
        w_used = sem("w_used")

        def load_w(sp, base, it=0, per=0, width=D, src=None):
            t0 = base
            if t0 >= 2:
                sp.wait_ge(w_lo, it * per + (t0 - 1))
            if src is None:
                src = a["w"][it * per + t0]
            sp.dma_start(raw[:, t0 % 2, 0:width], src[:, 0:width]).then_inc(w_landed[t0 % 2], 16)

        def split_hi(act, base, it=0, per=0, width=D):
            act.wait_ge(w_landed[base % 2], it * (8 * per) + 16 * (base // 2 + 1))
            if base >= 2:
                act.wait_ge(w_used, it * per + (base - 1))
            act.activation(wH[:, base % 2, 0:width], raw[:, base % 2, 0:width], ACT.Copy).then_inc(w_hi, 1)

        def split_lo(pool, base, it=0, per=0, width=D):
            pool.wait_ge(w_hi, it * per + (base + 1))
            pool.tensor_tensor(wL[:, base % 2, 0:width], raw[:, base % 2, 0:width],
                               wH[:, base % 2, 0:width].bitcast(F32), ALU.subtract).then_inc(w_lo, 1)

        def product3(pe, dst, wh, wl, xh, xl, first, last):
            pe.matmul(dst, wh, xh, start=first, stop=False)
            pe.matmul(dst, wh, xl, start=False, stop=False)
            return pe.matmul(dst, wl, xh, start=False, stop=last)

        def ada_columns(pe, chunk, c):
            for q in range(CW // P):
                col = c % CK * (CW // P) + q
                for k in range(KT):
                    mm = pe.matmul(work[:, c // CK, col:col + 1], chunk[:, k, q * P:(q + 1) * P], cT[:, k:k + 1],
                                   start=(k == 0), stop=(k == KT - 1))
            return mm

        hstack = ExitStack()
        hsb = sb_in(hstack)
        hH = hsb("hH", [P, KT, T], F32R)
        hL = hsb("hL", [P, KT, T], F32R)
        dstack = ExitStack()
        dsb = sb_in(dstack)
        cols = dsb("cols", [P, HEADS, NCOL, NT])
        gstack = ExitStack()
        psb = sb_in(gstack)
        s5p = psb("s5p", [P, 3, GROUPS])
        s5b = psb("s5b", [P, 2, GROUPS, GI])
        s5c = psb("s5c", [P, 2, GROUPS, GI])
        s5d = psb("s5d", [P, CT])
        q = psb("q", [P, 14, GROUPS])
        are = psb("are", [P, STEP + 1, GROUPS])
        aim = psb("aim", [P, STEP + 1, GROUPS])
        pw = psb("pw", [P, 2, 4, GROUPS])
        ua = psb("ua", [P, STEP, GROUPS])
        va = psb("va", [P, STEP, GROUPS])
        ca = psb("ca", [P, STEP + 1, GROUPS])
        cb = psb("cb", [P, STEP + 1, GROUPS])
        bbst = psb("bbst", [P, GROUPS, GI])
        LR, LI, DTT, TH, LDT, NN, SN, SH, CC, MAG, MG8, T_A, T_B, DEN = range(14)
        Q = lambda n: q[:, n, :]
        s5_in = sem("s5_in")
        par = sem("par")
        par_act = sem("par_act")
        bb_done = sem("bb_done")
        PAR_DONE = 68

        def s5_params_act(act):
            act.wait_ge(s5_in, 64)
            act.activation(Q(DTT), s5p[:, 2, :], ACT.Exp).then_inc(par_act, 1)
            act.wait_ge(par, 11)
            act.activation(Q(MAG), Q(LDT), ACT.Exp).then_inc(par_act, 1)
            act.activation(Q(MG8), Q(LDT), ACT.Exp, scale=float(STEP)).then_inc(par_act, 1)
            act.activation(Q(SN), Q(TH), ACT.Sin).then_inc(par_act, 1)
            act.activation(Q(SH), Q(TH), ACT.Sin, scale=0.5).then_inc(par_act, 1)

        def s5_params_pool(pool, bscr):
            pool.wait_ge(par, 30)
            pool.wait_ge(s5_in, 64)
            br, bi = s5b[:, 0, :, :], s5b[:, 1, :, :]
            fr = Q(T_A).unsqueeze(2).to_broadcast([P, GROUPS, GI])
            fi = Q(T_B).unsqueeze(2).to_broadcast([P, GROUPS, GI])
            r_, i_ = bscr[:, 0, :, :], bscr[:, 1, :, :]
            n = [0]

            def link(ins):
                n[0] += 1
                ins.then_inc(bb_done, 1)
                pool.wait_ge(bb_done, n[0])
            link(pool.tensor_tensor(bbst[:, :, :], fi, bi, ALU.mult))
            link(pool.tensor_tensor(r_, fr, br, ALU.mult))
            link(pool.tensor_tensor(r_, r_, bbst[:, :, :], ALU.subtract))
            link(pool.tensor_tensor(i_, fr, bi, ALU.mult))
            link(pool.tensor_tensor(bbst[:, :, :], fi, br, ALU.mult))
            link(pool.tensor_tensor(s5b[:, 1, :, :], i_, bbst[:, :, :], ALU.add))
            link(pool.tensor_copy(s5b[:, 0, :, :], r_))
            link(pool.tensor_copy(bbst[0:PS, :, :], s5b[0:PS, 0, :, :]))
            link(pool.tensor_copy(bbst[PS:P, :, :], s5b[PS:P, 1, :, :]))

        def s5_params_dve(dve):
            n = [0]

            def link(ins):
                n[0] += 1
                ins.then_inc(par, 1)
                dve.wait_ge(par, n[0])
            tt = dve.tensor_tensor
            MAGIC = 1.5 * 2.0 ** 23
            TWO_PI = (6.28125, 1.9350051879882812e-3, 3.0199159819567e-07)
            dve.wait_ge(s5_in, 64)
            link(dve.tensor_scalar(Q(LR), s5p[:, 0, :], -1e-4, None, ALU.min))
            link(dve.tensor_copy(Q(LI), s5p[:, 1, :]))
            dve.wait_ge(par_act, 1)
            link(tt(Q(TH), Q(LI), Q(DTT), ALU.mult))
            link(tt(Q(LDT), Q(LR), Q(DTT), ALU.mult))
            link(dve.tensor_scalar(Q(NN), Q(TH), 0.15915494309189535, None, ALU.mult))
            link(dve.tensor_scalar(Q(NN), Q(NN), MAGIC, None, ALU.add))
            link(dve.tensor_scalar(Q(NN), Q(NN), MAGIC, None, ALU.subtract))
            for c in TWO_PI:
                link(dve.scalar_tensor_tensor(Q(TH), Q(NN), -c, Q(TH), ALU.mult, ALU.add))
            link(dve.tensor_scalar(Q(TH), Q(TH), 3.1415925, -3.1415925, ALU.min, ALU.max))
            assert n[0] == 11
            dve.wait_ge(par_act, 5)
            link(tt(Q(T_A), Q(SH), Q(SH), ALU.mult))
            link(dve.tensor_scalar(Q(CC), Q(T_A), -2.0, 1.0, ALU.mult, ALU.add))
            link(tt(are[:, 1, :], Q(MAG), Q(CC), ALU.mult))
            link(tt(aim[:, 1, :], Q(MAG), Q(SN), ALU.mult))
            link(dve.memset(are[:, 0, :], 1.0))
            link(dve.memset(aim[:, 0, :], 0.0))
            link(tt(Q(T_A), Q(LR), Q(LR), ALU.mult))
            link(tt(Q(T_B), Q(LI), Q(LI), ALU.mult))
            link(tt(Q(DEN), Q(T_A), Q(T_B), ALU.add))
            link(dve.reciprocal(Q(DEN), Q(DEN)))
            link(dve.tensor_scalar(Q(NN), are[:, 1, :], 1.0, None, ALU.subtract))
            link(tt(Q(T_A), Q(NN), Q(LR), ALU.mult))
            link(tt(Q(T_B), aim[:, 1, :], Q(LI), ALU.mult))
            link(tt(Q(T_A), Q(T_A), Q(T_B), ALU.add))
            link(tt(Q(T_A), Q(T_A), Q(DEN), ALU.mult))
            link(tt(Q(T_B), aim[:, 1, :], Q(LR), ALU.mult))
            link(tt(Q(TH), Q(NN), Q(LI), ALU.mult))
            link(tt(Q(T_B), Q(T_B), Q(TH), ALU.subtract))
            link(tt(Q(T_B), Q(T_B), Q(DEN), ALU.mult))
            assert n[0] == 30
            for _r in range(3):
                link(tt(Q(LDT), Q(CC), Q(CC), ALU.mult))
                link(tt(Q(NN), Q(SN), Q(SN), ALU.mult))
                link(dve.scalar_tensor_tensor(Q(SN), Q(CC), 2.0, Q(SN), ALU.mult, ALU.mult))
                link(tt(Q(CC), Q(LDT), Q(NN), ALU.subtract))
            for m in (1, 2, 4):
                sr, si = are[:, 1:m + 1, :], aim[:, 1:m + 1, :]
                br = are[:, m:m + 1, :].to_broadcast([P, m, GROUPS])
                bi = aim[:, m:m + 1, :].to_broadcast([P, m, GROUPS])
                x0, x1 = pw[:, 0, 0:m, :], pw[:, 1, 0:m, :]
                link(tt(x0, sr, br, ALU.mult))
                link(tt(x1, si, bi, ALU.mult))
                link(tt(are[:, m + 1:2 * m + 1, :], x0, x1, ALU.subtract))
                link(tt(x0, sr, bi, ALU.mult))
                link(tt(x1, si, br, ALU.mult))
                link(tt(aim[:, m + 1:2 * m + 1, :], x0, x1, ALU.add))
            lo_, hi_ = slice(0, PS), slice(PS, P)
            for dst, rows, src, sgn in ((ua, lo_, are, 1.0), (ua, hi_, aim, 1.0), (va, lo_, aim, -1.0), (va, hi_, are, 1.0),
                                        (ca, lo_, are, 1.0), (ca, hi_, aim, -1.0), (cb, lo_, aim, -1.0), (cb, hi_, are, -1.0)):
                m = dst.shape[1]
                link(dve.tensor_scalar(dst[rows, :, :], src[rows, 0:m, :], sgn, None, ALU.mult))
            assert n[0] == PAR_DONE, n[0]

        with ExitStack() as c1:
            s1 = sb_in(c1)
            xr = s1("xr", [P, 4, D])
            xT = s1("xT", [P, KT, T])
            wada = s1("wada", [P, 2, KT, CW])
            ss = s1("ss", [P, NT])
            rstd = s1("rstd", [P, NT])
            mhalf = s1("mhalf", [P, 1])
            hf = s1("hf", [P, 4, HALF])
            bscr = s1("bscr", [P, 2, GROUPS, GI])
            baT = s1("baT", [2 * HEADS, T])
            ba = s1("ba", [P, NT, 2 * HEADS])
            dtb = s1("dtb", [P, HEADS])
            alog = s1("alog", [P, HEADS])
            ea = s1("ea", [P, HEADS])
            z = s1("z", [P, HEADS, NT])
            az = s1("az", [P, HEADS, NT])
            g = s1("g", [P, HEADS, NT])
            ex3 = s1("ex3", [P, 3, HEADS * NT])
            x_in = [sem(f"x_in{n}") for n in range(4)]
            c_in, b_in, k_in = sem("c_in"), sem("b_in"), sem("k_in")
            ada_in = [sem("ada_in0"), sem("ada_in1")]
            ada_used = sem("ada_used")
            sq_done, ms_done, rstd_done, xn_done = sem("sq_done"), sem("ms_done"), sem("rstd_done"), sem("xn_done")
            x_t, xT_done, mod_done = sem("x_t"), sem("xT_done"), sem("mod_done")
            hf_done, hH_done, hL_pool, hL_dve = sem("hf_done"), sem("hH_done"), sem("hL_pool"), sem("hL_dve")
            par_in = sem("par_in")
            ba_copied, ba_t, ba_nat = sem("ba_copied"), sem("ba_t"), sem("ba_nat")
            col_act, col_dve, col_pe = sem("col_act"), sem("col_dve"), sem("col_pe")
            hs = lambda u: (slice(None), u // 2, slice(u % 2 * HALF, (u % 2 + 1) * HALF))

            def h_lo(eng, u, done):
                eng.wait_ge(hH_done, u + 1)
                eng.tensor_tensor(hL[hs(u)], hf[:, u % 4, :], hH[hs(u)].bitcast(F32), ALU.subtract).then_inc(done, 1)

            with nc.Block() as block:
                @block.sync
                def _(sp):
                    def load_x(n):
                        if n >= 4:
                            sp.wait_ge(x_t, n - 3)
                        sp.dma_start(xr[:, n % 4, :], a["x"][n]).then_inc(x_in[n % 4], 16)

                    def load_ada(c):
                        if c >= 2:
                            sp.wait_ge(ada_used, c - 1)
                        m, q0 = c // 4, c % 4 * CW
                        sp.dma_start(wada[:, c % 2, :, :], a["wada"][m][:, :, q0:q0 + CW]).then_inc(ada_in[c % 2], 16)
                    load_x(0)
                    load_x(1)
                    for dst, n in ((s5p, "s5p"), (s5b, "s5b"), (s5c, "s5c"), (s5d, "s5d")):
                        ap = dst[tuple([slice(None)] * len(a[n].shape))]
                        sp.dma_start(ap, a[n]).then_inc(s5_in, 16)
                    load_x(2)
                    load_x(3)
                    sp.dma_start(cst[:, :, :], a["cst"]).then_inc(k_in, 16)
                    load_ada(0)
                    load_ada(1)
                    for n in range(4, NT):
                        load_x(n)
                    for c in range(2, 6):
                        load_ada(c)
                    load_w(sp, 0)
                    load_w(sp, 1)
                    for c in range(6, 2 * CK):
                        load_ada(c)
                    load_w(sp, 2)
                    load_w(sp, 3)

                @block.scalar
                def _(act):
                    act.dma_start(cT[:, :], a["cT"]).then_inc(c_in, 16)
                    act.dma_start(bada[:, :], a["bada"]).then_inc(b_in, 16)
                    act.dma_start(dtb[:, :], a["dtb"]).then_inc(par_in, 16)
                    act.dma_start(alog[:, :], a["alog"]).then_inc(par_in, 16)

                    def evict_x(n):
                        act.wait_ge(x_t, n + 1)
                        act.activation(xT[:, :, n * P:(n + 1) * P], pair[n % 2][:, :, :].rearrange("p a (k t) -> p (a k) t", k=4),
                                       ACT.Copy).then_inc(xT_done, 1)
                    for n in range(NT):
                        act.wait_ge(x_in[n % 4], 16 * (n // 4 + 1))
                        if n >= 2:
                            act.wait_ge(sq_done, n - 1)
                        act.activation(hf[:, n % 2 * 2:n % 2 * 2 + 2, :].rearrange("p a b -> p (a b)"), xr[:, n % 4, :], ACT.Square,
                                       accum_out=ss[:, n:n + 1]).then_inc(sq_done, 1)
                        if n >= 1:
                            evict_x(n - 1)
                    evict_x(NT - 1)
                    s5_params_act(act)
                    split_hi(act, 0)
                    split_hi(act, 1)
                    for u in range(2 * KT):
                        act.wait_ge(hf_done, u + 1)
                        act.activation(hH[hs(u)], hf[:, u % 4, :], ACT.Copy).then_inc(hH_done, 1)
                    act.wait_ge(w_used, 1)
                    act.activation(baT[:, :], pair[0][0:16, :, :].rearrange("p a b -> p (a b)"), ACT.Copy).then_inc(ba_copied, 1)
                    act.wait_ge(ba_nat, 1)
                    act.wait_ge(par_in, 32)
                    act.activation(cols[:, :, C_BETA, :], ba[:, :, 0:HEADS].rearrange("p n h -> p h n"), ACT.Tanh,
                                   scale=0.5).then_inc(col_act, 1)
                    act.activation(ea[:, :], alog[:, :], ACT.Exp).then_inc(col_act, 1)
                    act.wait_ge(col_dve, 1)
                    act.activation(az[:, :, :], az[:, :, :], ACT.Exp, scale=-1.0).then_inc(col_act, 1)
                    act.wait_ge(col_act, 3)
                    act.activation(az[:, :, :], az[:, :, :], ACT.Ln, bias=1.0).then_inc(col_act, 1)
                    act.wait_ge(col_pe, 1)
                    act.activation(ex3[:, :, :].rearrange("p a b -> p (a b)"), work[:, 1, 0:192], ACT.Exp).then_inc(col_act, 1)
                    split_hi(act, 2)

                @block.gpsimd
                def _(pool):
                    pool.memset(mhalf[:, :], -0.5).then_inc(rstd_done, 1)
                    pool.wait_ge(rstd_done, 1)
                    for n in range(NT):
                        pool.wait_ge(ms_done, n + 1)
                        pool.tensor_tensor(rstd[:, n:n + 1], ss[:, n:n + 1], mhalf[:, :], ALU.pow).then_inc(rstd_done, 1)
                    s5_params_pool(pool, bscr)
                    split_lo(pool, 0)
                    split_lo(pool, 1)
                    for u in range(0, 2 * KT, 2):
                        h_lo(pool, u, hL_pool)
                    split_lo(pool, 2)

                @block.tensor
                def _(pe):
                    def transpose_x(n):
                        pe.wait_ge(xn_done, n + 1)
                        if n >= 2:
                            pe.wait_ge(xT_done, n - 1)
                        for k in range(KT):
                            tr = pe.transpose(pair[n % 2][:, k // 4, k % 4 * P:(k % 4 + 1) * P], xr[:, n % 4, k * P:(k + 1) * P], ident)
                        tr.then_inc(x_t, 1)

                    def adaln(c):
                        pe.wait_ge(ada_in[c % 2], 16 * (c // 2 + 1))
                        ada_columns(pe, wada[:, c % 2, :, :], c).then_inc(ada_used, 1)
                    pe.wait_ge(k_in, 16)
                    for n in range(4):
                        transpose_x(n)
                    pe.wait_ge(c_in, 16)
                    adaln(0)
                    adaln(1)
                    for n in range(4, NT):
                        transpose_x(n)
                    for c in range(2, 8):
                        adaln(c)
                    pe.wait_ge(w_lo, 1)
                    pe.wait_ge(xT_done, NT)
                    for k in range(KT):
                        pe.wait_ge(hL_pool, k + 1)
                        pe.wait_ge(hL_dve, k + 1)
                        for n in range(2):
                            mm = product3(pe, pair[0][:, n, :], wH[:, 0, k * P:(k + 1) * P], wL[:, 0, k * P:(k + 1) * P],
                                          hH[hs(2 * k + n)], hL[hs(2 * k + n)], k == 0, k == KT - 1)
                    mm.then_inc(w_used, 1)
                    pe.wait_ge(ba_copied, 1)
                    for n in range(NT):
                        tr = pe.transpose(work[:, 0, n * 16:(n + 1) * 16], baT[:, n * P:(n + 1) * P], cst[0:16, IDENT, 0:16])
                    tr.then_inc(ba_t, 1)
                    pe.wait_ge(col_dve, 3)
                    gg = g[:, :, :].rearrange("p h n -> p (h n)")
                    pe.matmul(work[:, 1, 0:64], cst[:, LE, :], gg, start=True, stop=True)
                    pe.matmul(work[:, 1, 64:128], cst[:, GT_, :], gg, start=True, stop=True)
                    pe.matmul(work[:, 1, 128:192], cst[:, ONES, :], gg, start=True, stop=True).then_inc(col_pe, 1)

                @block.vector
                def _(dve):
                    for n in range(NT):
                        dve.wait_ge(sq_done, n + 1)
                        dve.tensor_scalar(ss[:, n:n + 1], ss[:, n:n + 1], 1.0 / D, EPS, ALU.mult, ALU.add).then_inc(ms_done, 1)
                        dve.wait_ge(rstd_done, n + 2)
                        dve.tensor_scalar(xr[:, n % 4, :], xr[:, n % 4, :], rstd[:, n:n + 1], None, ALU.mult).then_inc(xn_done, 1)
                    s5_params_dve(dve)
                    dve.wait_ge(b_in, 16)
                    for m in range(2):
                        dve.wait_ge(ada_used, 4 * m + 4)
                        dve.tensor_tensor(modT[:, m * KT:(m + 1) * KT], work[:, m, 0:KT], bada[:, m * KT:(m + 1) * KT],
                                          ALU.add).then_inc(mod_done, 1)
                    dve.wait_ge(mod_done, 2)
                    dve.tensor_scalar(modT[:, KT:2 * KT], modT[:, KT:2 * KT], 1.0, None, ALU.add).then_inc(mod_done, 1)
                    dve.wait_ge(mod_done, 3)
                    dve.wait_ge(xT_done, NT)
                    for k in range(KT):
                        for u in (2 * k, 2 * k + 1):
                            if u >= 4:
                                dve.wait_ge((hL_pool, hL_dve)[u % 2], u // 2 - 1)
                            dve.tensor_scalar(hf[:, u % 4, :], xT[hs(u)], modT[:, KT + k:KT + k + 1], modT[:, k:k + 1],
                                              ALU.mult, ALU.add).then_inc(hf_done, 1)
                        if k >= 1:
                            h_lo(dve, 2 * k - 1, hL_dve)
                    h_lo(dve, 2 * KT - 1, hL_dve)
                    dve.wait_ge(ba_t, 1)
                    dve.tensor_copy(ba[:, :, :].rearrange("p n c -> p (n c)"), work[:, 0, 0:16 * NT]).then_inc(ba_nat, 1)
                    dve.wait_ge(ba_nat, 1)
                    dve.wait_ge(par_in, 32)
                    dve.tensor_tensor(z[:, :, :], ba[:, :, HEADS:2 * HEADS].rearrange("p n h -> p h n"),
                                      dtb[:, :].unsqueeze(2).to_broadcast([P, HEADS, NT]), ALU.add).then_inc(ba_nat, 1)
                    dve.wait_ge(ba_nat, 2)
                    dve.scalar_tensor_tensor(az[:, :, :].rearrange("p h n -> p (h n)"), z[:, :, :].rearrange("p h n -> p (h n)"), -1.0,
                                             z[:, :, :].rearrange("p h n -> p (h n)"), ALU.mult, ALU.max).then_inc(col_dve, 1)
                    dve.wait_ge(col_act, 4)
                    dve.scalar_tensor_tensor(az[:, :, :].rearrange("p h n -> p (h n)"), z[:, :, :].rearrange("p h n -> p (h n)"), 0.0,
                                             az[:, :, :].rearrange("p h n -> p (h n)"), ALU.max, ALU.add).then_inc(col_dve, 1)
                    dve.wait_ge(col_dve, 2)
                    dve.scalar_tensor_tensor(g[:, :, :], az[:, :, :], -1.0,
                                             ea[:, :].unsqueeze(2).to_broadcast([P, HEADS, NT]), ALU.mult, ALU.mult).then_inc(col_dve, 1)
                    dve.wait_ge(col_dve, 3)
                    dve.tensor_copy(cols[:, :, C_G, :], g[:, :, :]).then_inc(col_dve, 1)
                    dve.tensor_scalar(cols[:, :, C_BETA, :], cols[:, :, C_BETA, :], 1.0, 0.5, ALU.add, ALU.mult).then_inc(col_dve, 1)
                    dve.wait_ge(col_dve, 5)
                    dve.tensor_scalar(cols[:, :, C_HB, :], cols[:, :, C_BETA, :], 0.5, None, ALU.mult).then_inc(col_dve, 1)
                    dve.wait_ge(col_act, 5)
                    for n, c in enumerate((C_EG, C_ES, C_EGL)):
                        dve.tensor_copy(cols[:, :, c, :], ex3[:, n, :].rearrange("p (h n) -> p h n", n=NT)).then_inc(col_dve, 1)
                    dve.wait_ge(col_dve, 9)
                    dve.tensor_tensor(cols[:, :, C_BEG, :], cols[:, :, C_BETA, :], cols[:, :, C_EG, :], ALU.mult).then_inc(col_dve, 1)

        gy = psb("gy", [P, CT, T])
        with ExitStack() as c3:
            s3 = sb_in(c3)
            bbs = s3("bbs", [P, CG, GI])
            pt9 = s3("pt9", [P, CG, STEP + 1, GI])
            mg8 = s3("mg8", [P, CG])
            dsk = s3("dsk", [P, 1])
            rot = s3("rot", [P, 4, CG])
            uT = s3("uT", [P, T])
            un = s3("un", [P, CG, STEP, GI])
            ug = s3("ug", [P, CG, NCH])
            dg = s3("dg", [P, CG, P])
            w1 = s3("w1", [P, CG, P])
            w2 = s3("w2", [P, CG, P])
            p1 = s3("p1", [P, CG, STEP + 1, GI])
            p2 = s3("p2", [P, CG, STEP, GI])
            ctab = s3("ctab", [P, CG, NCH])
            stab = s3("stab", [P, CG, NCH])
            yin = s3("yin", [P, CG, NCH])
            tmp = s3("tmp", [P, CG, NCH])
            t1 = s3("t1", [P, CG, NCH + 1])
            t2 = s3("t2", [P, CG, NCH + 1])
            yT, th = s3("yT", [P, T])[:, :], s3("th3", [P, T])[:, :]
            zs = yin[:, :, :].rearrange("p a b -> p (a b)")
            ksb = w1[0:GI, :, :]
            w_done, w_t, w12_done = sem("s5_w_done"), sem("s5_w_t"), sem("s5_w12_done")
            p_done, tab = sem("s5_p_done"), sem("s5_tab")
            uT_done, u_t, un_done, u_tt, ug_done = (sem(n) for n in ("uT_done", "u_t", "un_done", "u_tt", "ug_done"))
            s_full, state = sem("s_full"), sem("s5_state")
            z_act, z_dve = sem("z_act"), sem("z_dve")
            k_full, k_done, dg_zero = sem("k_full"), sem("k_done"), sem("dg_zero")
            dg_in = sem("dg_in")
            y_full, yn_done, y_t = sem("y_full"), sem("yn_done"), sem("y_t")
            tail_dve, tail_act = sem("tail_dve"), sem("tail_act")
            turn_end = sem("turn_end")
            pz_done, pz_stored = sem("pz_done"), sem("pz_stored")
            NTAB = 8 + 10 * 6
            t_zero = sem("t_zero")
            with nc.Block() as block:
                @block.sync
                def _(sp):
                    sp.sem_inc(pz_stored, 16)
                    with sp.Fori(0, CT) as i:
                        for jr in range(STEP):
                            if jr == 0:
                                sp.wait_ge(dg_zero, i + 1)
                                sp.wait_ge(k_done, i * 2 + 4)
                            sp.dma_start(dg[jr * GI:(jr + 1) * GI, :, (STEP - 1 - jr) * GI:P],
                                         ksb[:, :, 0:(jr + 1) * GI]).then_inc(dg_in, 16)
                        load_w(sp, 4, i, 2)
                        load_w(sp, 5, i, 2)
                        sp.wait_ge(pz_done, i + 1)
                        sp.dma_start(yg_dram[i], zs).then_inc(pz_stored, 16)
                    sp.wait_ge(pz_stored, 16 * CT + 16)

                @block.tensor
                def _(pe):
                    pe.sem_inc(y_full, 1)
                    with pe.Fori(0, CT) as i:
                        pe.wait_ge(w_lo, i * 2 + 2)
                        pe.wait_ge(yn_done, i * 2 + 2)
                        for n in range(2):
                            for k in range(KT):
                                mm = product3(pe, pair[0][:, n, :], wH[:, 1, k * P:(k + 1) * P], wL[:, 1, k * P:(k + 1) * P],
                                              hH[:, k, n * HALF:(n + 1) * HALF], hL[:, k, n * HALF:(n + 1) * HALF], k == 0, k == KT - 1)
                        mm.then_inc(w_used, 1)
                        pe.wait_ge(w_done, i * 3 + 3)
                        pe.wait_ge(z_dve, i + 1)
                        for gr in range(CG):
                            tr = pe.transpose(work[:, gr // 4, gr % 4 * P:(gr % 4 + 1) * P], dg[:, gr, :], ident)
                        tr.then_inc(w_t, 1)
                        pe.wait_ge(uT_done, i + 1)
                        pe.wait_ge(k_done, i * 2 + 2)
                        for jr in range(STEP):
                            tr = pe.transpose(work[:, 2 + jr // 4, jr % 4 * P:(jr % 4 + 1) * P],
                                              uT[:, STEP - 1 - jr::STEP], ident)
                        tr.then_inc(u_t, 1)
                        pe.wait_ge(un_done, i * 2 + 2)
                        pe.wait_ge(w12_done, i * 6 + 6)
                        for gr in range(CG):
                            tr = pe.transpose(work[:, gr // 4, gr % 4 * P:(gr % 4 + 1) * P],
                                              un[:, gr, :, :].rearrange("p j i -> p (j i)"), ident)
                        tr.then_inc(u_tt, 1)
                        pe.wait_ge(p_done, i * 7 + 7)
                        for gr in range(CG):
                            mm = pe.matmul(work[0:GI, 2 + gr // 4, gr % 4 * P:(gr % 4 + 1) * P], bbs[:, gr, :],
                                           p1[:, gr, 0:STEP, :].rearrange("p k i -> p (k i)"), start=True, stop=True)
                        mm.then_inc(k_full, 1)
                        pe.wait_ge(ug_done, i * 2 + 2)
                        pe.wait_ge(tail_dve, i * 4 + 2)
                        for gr in range(CG):
                            pe.matmul(pair[1][:, gr // 4, gr % 4 * P:(gr % 4 + 1) * P], w1[:, gr, :], ug[:, gr, :], start=True, stop=True)
                            mm = pe.matmul(pair[0][:, gr // 4, gr % 4 * P:(gr % 4 + 1) * P], w2[:, gr, :], ug[:, gr, :], start=True, stop=True)
                        mm.then_inc(s_full, 1)
                        pe.wait_ge(w_lo, i * 2 + 3)
                        for n in range(2):
                            for k in range(KT):
                                mm = product3(pe, work[:, n, :], wH[:, 0, k * P:(k + 1) * P], wL[:, 0, k * P:(k + 1) * P],
                                              hH[:, k, n * HALF:(n + 1) * HALF], hL[:, k, n * HALF:(n + 1) * HALF], k == 0, k == KT - 1)
                        mm.then_inc(w_used, 1)
                        pe.wait_ge(dg_in, i * (16 * STEP) + 16 * STEP)
                        pe.wait_ge(state, i * 13 + 13)
                        for gr in range(CG):
                            dst = pair[0][:, gr // 4, gr % 4 * P:(gr % 4 + 1) * P]
                            pe.matmul(dst, ug[:, gr, :], dg[:, gr, :], start=True, stop=False)
                            pe.matmul(dst, t1[:, gr, 0:NCH], p1[:, gr, 1:STEP + 1, :].rearrange("p k i -> p (k i)"), start=False, stop=False)
                            mm = pe.matmul(dst, t2[:, gr, 0:NCH], p2[:, gr, :, :].rearrange("p k i -> p (k i)"), start=False, stop=True)
                        mm.then_inc(y_full, 1)
                        pe.wait_ge(yn_done, i * 2 + 4)
                        yn = un[:, :, :, :].rearrange("p g j i -> p (g j i)").rearrange("p (j c) -> p j c", j=STEP)
                        for j in range(STEP):
                            tr = pe.transpose(pair[1][:, j // 4, j % 4 * P:(j % 4 + 1) * P], yn[:, j, :], ident)
                        tr.then_inc(y_t, 1)

                @block.scalar
                def _(act):
                    act.sem_inc(yn_done, 2)
                    act.sem_inc(k_done, 2)
                    with act.Fori(0, CT) as i:
                        act.wait_ge(w_used, i * 2 + 2)
                        act.wait_ge(tail_dve, i * 4 + 2)
                        act.activation(uT[:, :], pair[0][:, :, :].rearrange("p a b -> p (a b)"), ACT.Copy).then_inc(uT_done, 1)
                        act.wait_ge(w_t, i + 1)
                        for n in range(2):
                            src = work[:, n, :].rearrange("p (g s) -> p g s", g=4)
                            act.activation(w1[:, 4 * n:4 * n + 4, :], src, ACT.Copy).then_inc(w12_done, 1)
                        for n in range(2):
                            src = work[:, n, :].rearrange("p (g s) -> p g s", g=4)
                            act.activation(w2[:, 4 * n:4 * n + 4, 0:PS], src[:, :, PS:P], ACT.Copy).then_inc(w12_done, 1)
                            act.activation(w2[:, 4 * n:4 * n + 4, PS:P], src[:, :, 0:PS], ACT.Copy, scale=-1.0).then_inc(w12_done, 1)
                        act.wait_ge(u_t, i + 1)
                        act.wait_ge(y_t, i + 1)
                        for n in range(2):
                            act.activation(un[:, :, 4 * n:4 * n + 4, :], work[:, 2 + n, :].rearrange("p (j g i) -> p g j i", j=4, g=CG),
                                           ACT.Copy).then_inc(un_done, 1)
                        act.wait_ge(u_tt, i + 1)
                        for n in range(2):
                            act.activation(ug[:, 4 * n:4 * n + 4, :], work[:, n, :].rearrange("p (g c) -> p g c", g=4), ACT.Copy).then_inc(ug_done, 1)
                        act.wait_ge(k_full, i + 1)
                        act.wait_ge(s_full, i + 1)
                        for n in range(2):
                            act.activation(ksb[:, 4 * n:4 * n + 4, :], work[0:GI, 2 + n, :].rearrange("p (g c) -> p g c", g=4), ACT.Copy).then_inc(k_done, 1)
                        split_hi(act, 3, i, 2)
                        act.wait_ge(w_used, i * 2 + 3)
                        split_hi(act, 4, i, 2)
                        act.activation(th, work[:, 0:2, :].rearrange("p a b -> p (a b)"), ACT.Tanh, scale=0.5).then_inc(z_act, 1)
                        act.wait_ge(y_full, i + 2)
                        for n in range(2):
                            act.activation(un[:, :, :, :].rearrange("p g j i -> p (g j i)").rearrange("p (j g i) -> p g j i", j=STEP, g=CG)[:, 4 * n:4 * n + 4, :, :],
                                           pair[0][:, n, :].rearrange("p (g j i) -> p g j i", g=4, j=STEP), ACT.Copy).then_inc(yn_done, 1)
                        act.wait_ge(tail_dve, i * 4 + 4)
                        act.activation(th, yT, ACT.Square).then_inc(tail_act, 1)
                        act.wait_ge(tail_dve, i * 4 + 6)
                        act.activation(th, th, ACT.Tanh, scale=0.7978845608028654).then_inc(tail_act, 1)

                @block.gpsimd
                def _(pool):
                    with pool.Fori(0, CT) as i:
                        pool.wait_ge(y_full, i + 1)
                        g8 = bass.ds(i * CG, CG)
                        cre = s5c[:, 0, g8, :].unsqueeze(2)
                        cim = s5c[:, 1, g8, :].unsqueeze(2)
                        A = lambda t, k0, k1: t[:, k0:k1, g8].rearrange("p k g -> p g k").unsqueeze(3).to_broadcast([P, CG, k1 - k0, GI])
                        C = lambda t, n: t.to_broadcast([P, CG, n, GI])
                        t9 = pt9[:, :, :, :]
                        t8 = pt9[:, :, 0:STEP, :]
                        m = [0]

                        def step(ins):
                            m[0] += 1
                            ins.then_inc(p_done, 1)
                            pool.wait_ge(p_done, i * 7 + m[0])
                        step(pool.tensor_tensor(p1[:, :, :, :], C(cre, STEP + 1), A(ca, 0, STEP + 1), ALU.mult))
                        step(pool.tensor_tensor(t9, C(cim, STEP + 1), A(cb, 0, STEP + 1), ALU.mult))
                        step(pool.tensor_tensor(p1[:, :, :, :], p1[:, :, :, :], t9, ALU.add))
                        step(pool.tensor_tensor(p2[:, :, :, :], C(cre, STEP), A(cb, 1, STEP + 1), ALU.mult))
                        step(pool.tensor_tensor(t8, C(cim, STEP), A(ca, 1, STEP + 1), ALU.mult))
                        step(pool.tensor_tensor(p2[:, :, :, :], p2[:, :, :, :], t8, ALU.subtract))
                        step(pool.tensor_copy(bbs[:, :, :], bbst[:, g8, :]))
                        split_lo(pool, 3, i, 2)
                        split_lo(pool, 4, i, 2)

                @block.vector
                def _(dve):
                    tt = dve.tensor_tensor
                    dve.memset(t1[:, :, 0:1], 0.0).then_inc(t_zero, 1)
                    dve.memset(t2[:, :, 0:1], 0.0).then_inc(t_zero, 1)
                    dve.wait_ge(t_zero, 2)
                    v4 = lambda t: t[:, :, :].rearrange("p g (k i) -> p g k i", i=GI)

                    def powers(i, j):
                        g8 = bass.ds(j * CG, CG)
                        B = lambda c: s5b[:, c, g8, :].unsqueeze(2).to_broadcast([P, CG, STEP, GI])
                        A = lambda t: t[:, :, g8].rearrange("p k g -> p g k").unsqueeze(3).to_broadcast([P, CG, STEP, GI])
                        tt(v4(dg), B(0), A(ua), ALU.mult).then_inc(w_done, 1)
                        tt(v4(tmp), B(1), A(va), ALU.mult).then_inc(w_done, 1)
                        dve.wait_ge(w_done, i * 3 + 2)
                        tt(v4(dg), v4(dg), v4(tmp), ALU.add).then_inc(w_done, 1)
                        dve.wait_ge(w_done, i * 3 + 3)

                    def turn(i, last):
                        g8 = bass.ds(i * CG, CG)
                        m = [0]

                        def step(ins):
                            m[0] += 1
                            ins.then_inc(tab, 1)
                            dve.wait_ge(tab, i * NTAB + m[0])
                        step(dve.memset(ctab[:, :, 0:1], 1.0))
                        step(dve.memset(stab[:, :, 0:1], 0.0))
                        step(dve.tensor_copy(rot[:, 0, :], q[:, CC, g8]))
                        step(dve.tensor_copy(rot[:, 1, :], q[:, SN, g8]))
                        step(dve.tensor_copy(ctab[:, :, 1:2], rot[:, 0, :].unsqueeze(2)))
                        step(dve.tensor_copy(stab[:, :, 1:2], rot[:, 1, :].unsqueeze(2)))
                        step(dve.tensor_copy(mg8[:, :], q[:, MG8, g8]))
                        step(dve.tensor_copy(dsk[:, :], s5d[:, bass.ds(i, 1)]))
                        k = 2
                        while k < NCH:
                            step(tt(rot[:, 2, :], rot[:, 0, :], rot[:, 0, :], ALU.mult))
                            step(tt(rot[:, 3, :], rot[:, 1, :], rot[:, 1, :], ALU.mult))
                            step(dve.scalar_tensor_tensor(rot[:, 1, :], rot[:, 0, :], 2.0, rot[:, 1, :], ALU.mult, ALU.mult))
                            step(tt(rot[:, 0, :], rot[:, 2, :], rot[:, 3, :], ALU.subtract))
                            cr = rot[:, 0, :].unsqueeze(2).to_broadcast([P, CG, k])
                            sr = rot[:, 1, :].unsqueeze(2).to_broadcast([P, CG, k])
                            x0, x1 = tmp[:, :, 0:k], yin[:, :, 0:k]
                            if k == 2:
                                dve.wait_ge(pz_stored, i * 16 + 16)
                            step(tt(x0, ctab[:, :, 0:k], cr, ALU.mult))
                            step(tt(x1, stab[:, :, 0:k], sr, ALU.mult))
                            step(tt(ctab[:, :, k:2 * k], x0, x1, ALU.subtract))
                            step(tt(x0, ctab[:, :, 0:k], sr, ALU.mult))
                            step(tt(x1, stab[:, :, 0:k], cr, ALU.mult))
                            step(tt(stab[:, :, k:2 * k], x0, x1, ALU.add))
                            k *= 2
                        assert m[0] == NTAB, m[0]
                        dve.wait_ge(w_t, i + 1)
                        dve.memset(dg[:, :, :], 0.0).then_inc(dg_zero, 1)
                        dve.wait_ge(s_full, i + 1)
                        m8 = lambda pp: pp[:, :, :].rearrange("p a (g c) -> p (a g) c", g=4)
                        tt(yin[:, :, :], m8(pair[1]), ctab[:, :, :], ALU.mult).then_inc(state, 1)
                        tt(tmp[:, :, :], m8(pair[0]), stab[:, :, :], ALU.mult).then_inc(state, 1)
                        dve.wait_ge(state, i * 13 + 2)
                        tt(yin[:, :, :], yin[:, :, :], tmp[:, :, :], ALU.add).then_inc(state, 1)
                        dve.wait_ge(state, i * 13 + 3)
                        for gr in range(CG):
                            dve.tensor_tensor_scan(tmp[:, gr, :], mg8[:, gr:gr + 1].to_broadcast([P, NCH]), yin[:, gr, :], 0.0,
                                                   ALU.mult, ALU.add).then_inc(state, 1)
                        dve.wait_ge(state, i * 13 + 11)
                        tt(t1[:, :, 1:NCH + 1], tmp[:, :, :], ctab[:, :, :], ALU.mult).then_inc(state, 1)
                        tt(t2[:, :, 1:NCH + 1], tmp[:, :, :], stab[:, :, :], ALU.mult).then_inc(state, 1)
                        dve.wait_ge(z_act, i + 1)
                        dve.scalar_tensor_tensor(zs, th, 1.0, work[:, 0:2, :].rearrange("p a b -> p (a b)"), ALU.add, ALU.mult).then_inc(z_dve, 1)
                        if not last:
                            dve.wait_ge(y_full, i + 2)
                            dve.wait_ge(state, i * 13 + 13)
                            powers(i + 1, i + 1)
                        dve.wait_ge(y_t, i + 2)
                        jc = lambda t, b: t.rearrange("p (c j) -> p j c", j=STEP)[:, 4 * b:4 * b + 4, :]
                        for b in range(2):
                            dve.scalar_tensor_tensor(jc(yT, b), jc(uT[:, :], b), dsk[:, 0:1],
                                                     pair[1][:, b, :].rearrange("p (j c) -> p j c", j=4), ALU.mult, ALU.add).then_inc(tail_dve, 1)
                        dve.wait_ge(tail_act, i * 2 + 1)
                        tt(th, th, yT, ALU.mult).then_inc(tail_dve, 1)
                        dve.wait_ge(tail_dve, i * 4 + 5)
                        dve.scalar_tensor_tensor(th, th, 0.044715, yT, ALU.mult, ALU.add).then_inc(tail_dve, 1)
                        dve.wait_ge(tail_act, i * 2 + 2)
                        dve.scalar_tensor_tensor(gy[:, i, :], th, 1.0, yT, ALU.add, ALU.mult).then_inc(turn_end, 1)
                        dve.wait_ge(turn_end, i + 1)
                        tt(zs, zs, gy[:, i, :], ALU.mult).then_inc(pz_done, 1)
                    powers(0, 0)
                    dve.sem_inc(tail_dve, 2)
                    dve.sem_inc(z_dve, 1)
                    dve.sem_inc(y_t, 1)
                    with dve.Fori(0, CT - 1) as i:
                        turn(i, False)
                    turn(CT - 1, True)

        with ExitStack() as c4:
            s4 = sb_in(c4)
            pz = s4("pz", [P, CT, T])
            gH = s4("gH", [P, CT, T], F32R)
            gL = s4("gL", [P, CT, T], F32R)
            tg = s4("tg", [P, 2, T])
            glub = s4("glub", [P, CT])
            wgate = s4("wgate", [P, 2, KT, CW])
            wg_in, wg_used, gate_col = [sem("wg_in0"), sem("wg_in1")], sem("wg_used"), sem("gate_col")
            pz_in, gb_in, gH_done, gL_done, hb_done = sem("pz_in"), sem("gb_in"), sem("gH_done"), sem("gL_done"), sem("hb_done")
            glu_full, glu_act, yg_done, yg_stored = sem("glu_full"), sem("glu_act"), sem("yg_done"), sem("yg_stored")
            with nc.Block() as block:
                @block.sync
                def _(sp):
                    sp.dma_start(glub[:, :], a["glub"]).then_inc(gb_in, 16)
                    sp.dma_start(pz[:, :, :], yg_dram.rearrange("m p t -> p m t")).then_inc(pz_in, 16)
                    load_w(sp, 12)
                    for c in range(CK):
                        if c >= 2:
                            sp.wait_ge(wg_used, c - 1)
                        sp.dma_start(wgate[:, c % 2, :, :], a["wada"][2][:, :, c * CW:(c + 1) * CW]).then_inc(wg_in[c % 2], 16)
                    for m in range(CT):
                        sp.wait_ge(yg_done, m + 1)
                        sp.dma_start(yg_dram[m], pz[:, m, :]).then_inc(yg_stored, 16)
                    load_w(sp, 13)
                    sp.wait_ge(yg_stored, 16 * CT)

                @block.gpsimd
                def _(pool):
                    for m in range(CT):
                        pool.wait_ge(gH_done, m + 1)
                        pool.tensor_tensor(gL[:, m, :], gy[:, m, :], gH[:, m, :].bitcast(F32), ALU.subtract).then_inc(gL_done, 1)
                    split_lo(pool, 11)
                    split_lo(pool, 12)

                @block.tensor
                def _(pe):
                    pe.wait_ge(gL_done, CT)
                    for m in range(CT):
                        if m % 2 == 0:
                            pe.wait_ge(w_lo, 10 + m // 2)
                        if m >= 2:
                            pe.wait_ge(glu_act, m - 1)
                        sl = (TILE_GLU + m // 2) % 2
                        for n in range(2):
                            for k in range(CT):
                                o = (m % 2) * HALF + k * P
                                mm = product3(pe, pair[m % 2][:, n, :], wH[:, sl, o:o + P], wL[:, sl, o:o + P],
                                              gH[:, k, n * HALF:(n + 1) * HALF], gL[:, k, n * HALF:(n + 1) * HALF], k == 0, k == CT - 1)
                        mm.then_inc(glu_full, 1)
                        pe.wait_ge(wg_in[m % 2], 16 * (m // 2 + 1))
                        ada_columns(pe, wgate[:, m % 2, :, :], 2 * CK + m).then_inc(wg_used, 1)
                        if m % 2:
                            pe.wait_ge(glu_full, m + 1)
                            pe.sem_inc(w_used, 1)

                @block.scalar
                def _(act):
                    for m in range(CT):
                        act.activation(gH[:, m, :], gy[:, m, :], ACT.Copy).then_inc(gH_done, 1)
                    act.wait_ge(hb_done, 1)
                    for m in range(CT):
                        act.wait_ge(glu_full, m + 1)
                        if m >= 2:
                            act.wait_ge(yg_done, m - 1)
                        act.activation(tg[:, m % 2, :], pair[m % 2][:, :, :].rearrange("p a b -> p (a b)"), ACT.Tanh,
                                       scale=0.25, bias=glub[:, m:m + 1]).then_inc(glu_act, 1)
                        if m % 2:
                            split_hi(act, 11 + m // 2)

                @block.vector
                def _(dve):
                    dve.wait_ge(gb_in, 16)
                    dve.tensor_scalar(glub[:, :], glub[:, :], 0.5, None, ALU.mult).then_inc(hb_done, 1)
                    dve.wait_ge(pz_in, 16)
                    for m in range(CT):
                        dve.wait_ge(glu_act, m + 1)
                        dve.scalar_tensor_tensor(pz[:, m, :], tg[:, m % 2, :], 1.0, pz[:, m, :], ALU.add, ALU.mult).then_inc(yg_done, 1)
                    dve.wait_ge(wg_used, CK)
                    dve.tensor_tensor(modT[:, 2 * KT:3 * KT], work[:, 2, 0:KT], bada[:, 2 * KT:3 * KT], ALU.add).then_inc(gate_col, 1)
        gstack.close()

        with ExitStack() as c5:
            s5 = sb_in(c5)
            qc, kc, vc = s5("qc", [P, T]), s5("kc", [P, T]), s5("vc", [P, T])
            zs = s5("zs5", [P, T])
            cin = s5("cin", [P, CONV_K - 1 + T])
            acc = s5("acc", [P, T])
            th = s5("th5", [P, T])
            cw_all = s5("cw_all", [P, HEADS, 3 * CONV_K])
            cw = s5("cw", [P, 3 * CONV_K])
            nw = s5("nw", [P, 1])
            col = s5("col", [P, NCOL, NT])
            ssq = s5("ssq", [P, NQ, 3, GT])
            rsq = s5("rsq", [P, NQ, 3, GT])
            cqd = s5("cqd", [P, NQ, GT])
            mh = s5("mh", [P, 2 * GT])
            st = s5("state", [P, P])
            vnew = s5("vnew", [P, P])
            names = ("vb", "kh", "kbg", "kd", "khT", "qd", "qdT", "dec", "decA", "decS", "mm_", "attnT", "mb", "X", "Y", "R", "wT")
            B = {n: s5("d_" + n, [P, NT, P]) for n in names}
            B["qn"], B["kn"], B["rg"], B["attn"], B["on"], B["onx"], B["oz"] = B["X"], B["Y"], B["R"], B["mb"], B["dec"], B["decA"], B["decS"]
            SQ = [B["wT"], B["mb"]]
            tiles4 = lambda n, g: B[n][:, GT * g:GT * g + GT, :]
            flat = lambda n, g: tiles4(n, g).rearrange("p n d -> p (n d)")
            bank4 = lambda b: work[:, b, :].rearrange("p (n d) -> p n d", n=GT)
            rows = lambda c, g: col[:, c, GT * g:GT * g + GT].unsqueeze(2).to_broadcast([P, GT, P])
            mat4 = lambda m: cst[:, m:m + 1, :].to_broadcast([P, GT, P])

            order = ["nq0", "nk0", "nv0", "nq1", "nk1", "nv1", "D0", "D1", "kh0", "qd0", "kh1", "qd1", "kk0", "qk0", "kk1", "qk1",
                     "at0", "m10", "at1", "m11"]
            NL = len(LEVELS)
            for l in range(1, NL):
                order += [f"R0_{l}", f"R1_{l}"]
                order += [f"X0_{l}", f"Y0_{l}", f"X1_{l}", f"Y1_{l}"] if l < NL - 1 else [f"Y0_{l}", f"Y1_{l}"]
            order += ["w0", "w1"]
            banks = [(n, i % 4) for i, n in enumerate(order)]
            for n in range(NT):
                banks += [(f"vn{n}", 0), (f"s{n}", 1)]
            banks += [("o0", 2), ("o1", 3), ("on0", 0), ("on1", 1)]
            per_bank = [sum(b == k for _, b in banks) for k in range(4)]
            use = {n: (b, sum(bb == b for _, bb in banks[:i])) for i, (n, b) in enumerate(banks)}
            per_out = [per_bank[k] - (NT if k == 1 else 0) for k in range(4)]
            use_out = {n: (b, sum(bb == b and m[0] != "s" for m, bb in banks[:i])) for i, (n, b) in enumerate(banks)}
            full = [sem(f"bank_full{b}") for b in range(4)]
            evicted = [sem(f"bank_evicted{b}") for b in range(4)]
            R_ = {n: sem("r_" + n) for n in ("rg", "sqq", "sqk", "ssq", "rr", "kh", "qd", "kbg", "kd", "decI", "decS", "decB", "decA", "cq", "X1",
                                              "sqo", "sso", "ro", "onx", "oz")}
            mb_done, mh_ready = sem("mb_done"), sem("mh_ready")
            col_ready, s_ready, conv_ready, zs_ready = sem("col_ready"), sem("s_ready"), sem("conv_ready"), sem("zs_ready")
            cin_ready, acc_ready, th_ready, conv_step = sem("cin_ready"), sem("acc_ready"), sem("th_ready"), sem("conv_step")
            conv_in, const_ready, nw_ready, oz_stored = sem("conv_in"), sem("const_ready"), sem("nw_ready"), sem("oz_stored")

            class Turn:

                def __init__(self, eng, i):
                    self.eng, self.i = eng, i

                def need(self, name, g):
                    self.eng.wait_ge(R_[name], self.i * NQ + (g + 1))

                def fill(self, name):
                    b, n = use_out[name]
                    self.eng.wait_ge(evicted[b], self.i * per_out[b] + (n + 1))
                    return work[:, b, :]

                def filled(self, name):
                    b, n = use[name]
                    self.eng.wait_ge(full[b], self.i * per_bank[b] + (n + 1))
                    return work[:, b, :]

                def out(self, name):
                    b, n = use_out[name]
                    self.eng.wait_ge(evicted[b], self.i * per_out[b] + (n + 2))

            def full_of(name):
                return full[use[name][0]]

            def evicted_of(name):
                return evicted[use[name][0]]

            def proj_units(pe, base, it, u0, u1):
                for u in range(u0, u1):
                    s, n, k = u // 16, u // 8 % 2, u % 8
                    t = base + s
                    if u % 16 == 0:
                        pe.wait_ge(w_lo, it * 4 + (t + 1))
                        if s == 1:
                            pe.wait_ge(zs_ready, it + 1)
                        else:
                            pe.wait_ge(cin_ready, it * 3 + (3, 0, 4, 5)[s])
                    mm = product3(pe, pair[s % 2][:, n, :], wH[:, t % 2, k * P:(k + 1) * P], wL[:, t % 2, k * P:(k + 1) * P],
                                  hH[:, k, n * HALF:(n + 1) * HALF], hL[:, k, n * HALF:(n + 1) * HALF], k == 0, k == KT - 1)
                    if u % 16 == 15:
                        mm.then_inc(w_used, 1)

            def act_copy(act, base, it, s):
                act.wait_ge(w_used, it * 4 + (base + s + 1))
                act.wait_ge(conv_step, it * 12 + (4 * s + 13))
                act.activation(cin[:, CONV_K - 1:], pair[s % 2][:, :, :].rearrange("p a b -> p (a b)"), ACT.Copy).then_inc(cin_ready, 1)

            def act_tanh(act, it, s):
                act.wait_ge(conv_step, it * 12 + (4 * s + 17))
                if s == 0:
                    act.wait_ge(zs_ready, it + 1)
                else:
                    act.wait_ge(conv_ready, it * 3 + (3 + s))
                act.activation(th[:, :], acc[:, :], ACT.Tanh, scale=0.5).then_inc(th_ready, 1)

            def dve_conv(dve, it, s, tap):
                if tap == 0:
                    dve.wait_ge(cin_ready, it * 3 + (s + 4))
                    dve.wait_ge(conv_ready, it * 3 + (3 + s))
                    dve.tensor_scalar(acc[:, :], cin[:, 0:T], cw[:, CONV_K * s:CONV_K * s + 1], None, ALU.mult).then_inc(conv_step, 1)
                else:
                    dve.wait_ge(conv_step, it * 12 + (4 * s + tap + 13))
                    dve.scalar_tensor_tensor(acc[:, :], cin[:, tap:tap + T], cw[:, CONV_K * s + tap:CONV_K * s + tap + 1], acc[:, :],
                                             ALU.mult, ALU.add).then_inc(conv_step, 1)

            def dve_silu(dve, it, s):
                dve.wait_ge(th_ready, it * 4 + (s + 5))
                dve.scalar_tensor_tensor((qc, kc, vc)[s][:, :], th[:, :], 1.0, acc[:, :], ALU.add, ALU.mult).then_inc(conv_ready, 1)

            def act_z(act, base, it):
                act.wait_ge(w_used, it * 4 + (base + 4))
                act.wait_ge(conv_ready, it * 3 + 6)
                act.activation(th[:, :], pair[1][:, :, :].rearrange("p a b -> p (a b)"), ACT.Tanh, scale=0.5).then_inc(th_ready, 1)

            def dve_z(dve, it):
                dve.wait_ge(th_ready, it * 4 + 8)
                dve.scalar_tensor_tensor(zs[:, :], th[:, :], 1.0, pair[1][:, :, :].rearrange("p a b -> p (a b)"), ALU.add,
                                         ALU.mult).then_inc(zs_ready, 1)

            def dve_cw(dve, head):
                dve.tensor_copy(cw[:, :], cw_all[:, head, :]).then_inc(const_ready, 1)

            def pe_turn(pe, i, proj):
                t = Turn(pe, i)
                base = TILE_HEAD + 4

                def units(u0, u1):
                    if proj:
                        proj_units(pe, base, i, u0, u1)

                def trans(name, src, g):
                    bank = t.fill(name)
                    for n in range(GT):
                        tr = pe.transpose(bank[:, n * P:(n + 1) * P], src(GT * g + n), ident)
                    tr.then_inc(full_of(name), 1)

                def prod(name, lhs, rhs, g):
                    bank = t.fill(name)
                    for n in range(GT):
                        mm = pe.matmul(bank[:, n * P:(n + 1) * P], lhs(GT * g + n), rhs(GT * g + n), start=True, stop=True)
                    mm.then_inc(full_of(name), 1)
                ch = lambda tile: (lambda n: tile[:, n * P:(n + 1) * P])
                bf = lambda name: (lambda n: B[name][:, n, :])
                pe.wait_ge(conv_ready, i * 3 + 3)
                for g in range(NQ):
                    trans(f"nq{g}", ch(qc), g)
                    trans(f"nk{g}", ch(kc), g)
                    trans(f"nv{g}", ch(vc), g)
                    units(4 * g, 4 * g + 4)
                for g in range(NQ):
                    t.need("rg", g)
                    bank = t.fill(f"D{g}")
                    pe.matmul(bank, cst[:, LE, :], flat("rg", g), start=True, stop=True).then_inc(full_of(f"D{g}"), 1)
                    units(8 + 4 * g, 12 + 4 * g)
                for g in range(NQ):
                    t.need("kh", g)
                    trans(f"kh{g}", bf("kh"), g)
                    t.need("qd", g)
                    trans(f"qd{g}", bf("qd"), g)
                    units(16 + 4 * g, 20 + 4 * g)
                for g in range(NQ):
                    t.out(f"kh{g}")
                    prod(f"kk{g}", bf("khT"), bf("khT"), g)
                    prod(f"qk{g}", ch(qc), bf("khT"), g)
                    units(24 + 2 * g, 26 + 2 * g)
                for g in range(NQ):
                    t.out(f"qk{g}")
                    trans(f"at{g}", bf("attn"), g)
                    pe.wait_ge(mb_done, i * (NQ * NL) + (g + 1))
                    trans(f"m1{g}", bf("mb"), g)
                    units(28 + 2 * g, 30 + 2 * g)
                for l in range(1, NL):
                    for g in range(NQ):
                        t.out(f"m1{g}" if l == 1 else f"Y{g}_{l - 1}")
                        pe.wait_ge(mb_done, i * (NQ * NL) + (NQ * l + g + 1))
                        prod(f"R{g}_{l}", bf("mb"), bf("Y"), g)
                    units(30 + 2 * l, 31 + 2 * l)
                    for g in range(NQ):
                        t.out(f"R{g}_{l}")
                        if l > 1:
                            t.out(f"X{g}_{l - 1}")
                        else:
                            t.need("X1", g)
                        if l < NL - 1:
                            prod(f"X{g}_{l}", bf("R"), bf("X"), g)
                        prod(f"Y{g}_{l}", bf("X"), bf("R"), g)
                    units(31 + 2 * l, 32 + 2 * l)
                for g in range(NQ):
                    t.need("kbg", g)
                    t.out(f"Y{g}_{NL - 1}")
                    prod(f"w{g}", bf("kbg"), bf("Y"), g)
                    units(44 + g, 45 + g)
                t.need("kd", 1)
                t.out("w1")
                t.out("at1")
                t.out("qd1")
                t.out("nv1")
                for n in range(NT):
                    g = n // GT
                    bank = t.fill(f"vn{n}")[:, 0:P]
                    pe.wait_ge(s_ready, i * (NT + 1) + (n + 1))
                    pe.matmul(bank, B["Y"][:, n, :], B["vb"][:, n, :], start=True, stop=False)
                    pe.matmul(bank, B["wT"][:, n, :], st[:, :], start=False, stop=True).then_inc(full_of(f"vn{n}"), 1)
                    units(46 + 2 * n, 47 + 2 * n)
                    if n % GT == 0:
                        obank = t.fill(f"o{g}")
                    o = obank[:, n % GT * P:(n % GT + 1) * P]
                    pe.matmul(o, B["qdT"][:, n, :], st[:, :], start=True, stop=False)
                    sbank = t.fill(f"s{n}")[:, 0:P]
                    t.out(f"vn{n}")
                    pe.matmul(sbank, B["kd"][:, n, :], vnew[:, :], start=True, stop=True).then_inc(full_of(f"s{n}"), 1)
                    mm = pe.matmul(o, B["attnT"][:, n, :], vnew[:, :], start=False, stop=True)
                    if n % GT == GT - 1:
                        mm.then_inc(full_of(f"o{g}"), 1)
                    units(47 + 2 * n, 48 + 2 * n)
                units(62, 64)
                pe.wait_ge(s_ready, i * (NT + 1) + (NT + 1))
                for g in range(NQ):
                    t.need("onx", g)
                    trans(f"on{g}", bf("onx"), g)

            def act_turn(act, i, proj):
                t = Turn(act, i)
                base = TILE_HEAD + 4

                def copy(name, dst, g, scale=1.0):
                    act.activation(flat(dst, g), t.filled(name), ACT.Copy, scale=scale).then_inc(evicted_of(name), 1)

                def checkpoint(s):
                    if proj:
                        split_hi(act, base + s + 2, i, 4)
                        if s < 3:
                            act_copy(act, base, i, s)
                copy("nq0", "qn", 0)
                copy("nq1", "qn", 1)
                for g in range(NQ):
                    act.activation(flat("dec", g), t.filled(f"D{g}"), ACT.Exp).then_inc(evicted_of(f"D{g}"), 1)
                copy("kh0", "khT", 0)
                checkpoint(0)
                copy("kh1", "khT", 1)
                for g in range(NQ):
                    copy(f"at{g}", "attnT", g)
                if proj:
                    act_tanh(act, i, 0)
                for l in range(1, NL):
                    for g in range(NQ):
                        copy(f"R{g}_{l}", "R", g)
                    if l == 1:
                        checkpoint(1)
                    if l == NL - 2 and proj:
                        act_tanh(act, i, 1)
                for g in range(NQ):
                    copy(f"w{g}", "wT", g, -1.0)
                for n in range(NT):
                    act.activation(vnew[:, :], t.filled(f"vn{n}")[:, 0:P], ACT.Copy).then_inc(evicted_of(f"vn{n}"), 1)
                    if n == 1:
                        checkpoint(2)
                    if n == GT:
                        copy("o0", "on", 0)
                    if n == NT - 1 and proj:
                        act_tanh(act, i, 2)
                copy("o1", "on", 1)
                checkpoint(3)
                if proj:
                    act_z(act, base, i)

            def dve_turn(dve, i, proj):
                t = Turn(dve, i)
                tt = dve.tensor_tensor

                def conv(s, tap):
                    if proj:
                        dve_conv(dve, i, s, tap)
                dve.tensor_copy(col[:, :, :], cols[:, i, :, :]).then_inc(col_ready, 1)
                dve.memset(st[:, :], 0.0).then_inc(s_ready, 1)
                dve.wait_ge(col_ready, i + 1)
                for g in range(NQ):
                    dve.tensor_copy(flat("kn", g), t.filled(f"nk{g}")).then_inc(evicted_of(f"nk{g}"), 1)
                    t.filled(f"nv{g}")
                    tt(tiles4("vb", g), bank4(use[f"nv{g}"][0]), rows(C_HB, g), ALU.mult).then_inc(evicted_of(f"nv{g}"), 1)
                for g in range(NQ):
                    t.need("sqq", g)
                    t.need("sqk", g)
                    dve.tensor_reduce(ssq[:, g, 0:2, :], SQ[g][:, :, :].rearrange("p (a n) d -> p a n d", a=2), AX, ALU.add).then_inc(R_["ssq"], 1)
                    dve.wait_ge(R_["ssq"], i * (3 * NQ) + (3 * g + 1))
                    dve.tensor_scalar(ssq[:, g, 0, :], ssq[:, g, 0, :], 4 * EPS, float(HD), ALU.add, ALU.mult).then_inc(R_["ssq"], 1)
                    dve.tensor_scalar(ssq[:, g, 1, :], ssq[:, g, 1, :], 4 * EPS, None, ALU.add).then_inc(R_["ssq"], 1)
                for g in range(NQ):
                    t.need("rr", g)
                    tt(tiles4("kh", g), tiles4("kn", g), rsq[:, g, 1, :].unsqueeze(2).to_broadcast([P, GT, P]), ALU.mult).then_inc(R_["kh"], 1)
                for g in range(NQ):
                    dve.tensor_copy(flat("qdT", g), t.filled(f"qd{g}")).then_inc(evicted_of(f"qd{g}"), 1)
                if proj:
                    dve.wait_ge(conv_step, i * 12 + 13)
                    dve_cw(dve, i + 1)
                    dve.wait_ge(const_ready, i + 3)
                for g in range(NQ):
                    t.need("decB", g)
                    tt(flat("mm_", g), t.filled(f"kk{g}"), flat("decS", g), ALU.mult).then_inc(evicted_of(f"kk{g}"), 1)
                    t.need("decA", g)
                    tt(flat("attn", g), t.filled(f"qk{g}"), flat("decA", g), ALU.mult).then_inc(evicted_of(f"qk{g}"), 1)
                    conv(0, 2 * g)
                    conv(0, 2 * g + 1)
                for g in range(NQ):
                    dve.wait_ge(mb_done, i * (NQ * NL) + (g + 1))
                    tt(tiles4("X", g), mat4(IDENT), tiles4("mb", g), ALU.subtract).then_inc(R_["X1"], 1)
                    t.filled(f"m1{g}")
                    tt(tiles4("Y", g), mat4(IDENT), bank4(use[f"m1{g}"][0]), ALU.subtract).then_inc(evicted_of(f"m1{g}"), 1)
                if proj:
                    dve_silu(dve, i, 0)
                for l in range(1, NL):
                    for g in range(NQ):
                        t.filled(f"Y{g}_{l}")
                        if l < NL - 1:
                            tt(flat("X", g), flat("X", g), t.filled(f"X{g}_{l}"), ALU.subtract).then_inc(evicted_of(f"X{g}_{l}"), 1)
                        t.out(f"m1{g}" if l == 1 else f"Y{g}_{l - 1}")
                        tt(flat("Y", g), flat("Y", g), t.filled(f"Y{g}_{l}"), ALU.subtract).then_inc(evicted_of(f"Y{g}_{l}"), 1)
                    if 2 <= l < 6:
                        conv(1, l - 2)
                for n in range(NT):
                    dve.wait_ge(s_ready, i * (NT + 1) + (n + 1))
                    bank = t.filled(f"s{n}")[:, 0:P]
                    dve.scalar_tensor_tensor(st[:, :], st[:, :], col[:, C_EGL, n:n + 1], bank, ALU.mult, ALU.add).then_inc(s_ready, 1)
                    if n == 0 and proj:
                        dve_silu(dve, i, 1)
                    if 2 <= n < 6:
                        conv(2, n - 2)

                def norm(g):
                    t.need("sqo", g)
                    dve.tensor_reduce(ssq[:, g, 2, :], tiles4("onx", g), AX, ALU.add).then_inc(R_["sso"], 1)
                    dve.wait_ge(R_["sso"], i * (2 * NQ) + (2 * g + 1))
                    dve.tensor_scalar(ssq[:, g, 2, :], ssq[:, g, 2, :], 1.0 / HD, EPS, ALU.mult, ALU.add).then_inc(R_["sso"], 1)
                    t.need("ro", g)
                    tt(tiles4("onx", g), tiles4("on", g), rsq[:, g, 2, :].unsqueeze(2).to_broadcast([P, GT, P]), ALU.mult).then_inc(R_["onx"], 1)
                norm(0)
                if proj:
                    dve_silu(dve, i, 2)
                norm(1)
                for g in range(NQ):
                    dve.wait_ge(zs_ready, i + 1)
                    bank = t.filled(f"on{g}")
                    dve.scalar_tensor_tensor(flat("oz", g), bank, nw[:, 0:1], zs[:, g * HALF:(g + 1) * HALF], ALU.mult, ALU.mult).then_inc(R_["oz"], 1)
                    dve.wait_ge(R_["oz"], i * NQ + (g + 1))
                    dve.sem_inc(evicted_of(f"on{g}"), 1)
                if proj:
                    dve_z(dve, i)

            def pool_turn(pool, i, proj):
                t = Turn(pool, i)
                tt = pool.tensor_tensor
                pool.wait_ge(col_ready, i + 1)
                for g in range(NQ):
                    tt(tiles4("rg", g), mat4(GT_), rows(C_G, g), ALU.mult).then_inc(R_["rg"], 1)
                for g in range(NQ):
                    t.out(f"nq{g}")
                    tt(SQ[g][:, 0:GT, :], tiles4("qn", g), tiles4("qn", g), ALU.mult).then_inc(R_["sqq"], 1)
                    t.out(f"nk{g}")
                    tt(SQ[g][:, GT:NT, :], tiles4("kn", g), tiles4("kn", g), ALU.mult).then_inc(R_["sqk"], 1)
                for g in range(NQ):
                    pool.wait_ge(R_["ssq"], i * (3 * NQ) + (3 * g + 3))
                    tt(rsq[:, g, 0:2, :], ssq[:, g, 0:2, :], mh[:, :].rearrange("p (a n) -> p a n", a=2), ALU.pow).then_inc(R_["rr"], 1)
                    t.need("rr", g)
                    tt(cqd[:, g, :], rsq[:, g, 0, :], col[:, C_EG, GT * g:GT * g + GT], ALU.mult).then_inc(R_["cq"], 1)
                    t.need("cq", g)
                    tt(tiles4("qd", g), tiles4("qn", g), cqd[:, g, :].unsqueeze(2).to_broadcast([P, GT, P]), ALU.mult).then_inc(R_["qd"], 1)
                pool.wait_ge(oz_stored, i * (16 * NQ) + 16)
                for g in range(NQ):
                    t.out(f"D{g}")
                    tt(tiles4("decA", g), tiles4("dec", g), mat4(GE), ALU.mult).then_inc(R_["decI"], 1)
                    tt(tiles4("decS", g), tiles4("dec", g), mat4(GT_), ALU.mult).then_inc(R_["decS"], 1)
                    t.need("decS", g)
                    tt(tiles4("decS", g), tiles4("decS", g), rows(C_BETA, g), ALU.mult).then_inc(R_["decB"], 1)
                    t.need("decI", g)
                    tt(tiles4("decA", g), tiles4("decA", g), rsq[:, g, 0, :].unsqueeze(2).to_broadcast([P, GT, P]), ALU.mult).then_inc(R_["decA"], 1)
                if proj:
                    split_lo(pool, TILE_HEAD + 6, i, 4)

                def level(l):
                    for g in range(NQ):
                        if l == 0:
                            t.out(f"kk{g}")
                            t.filled(f"at{g}")
                        elif l == 1:
                            t.filled(f"m1{g}")
                            t.need("X1", g)
                        else:
                            t.filled(f"R{g}_{l - 1}")
                        tt(tiles4("mb", g), tiles4("mm_", g), mat4(LEVEL0 + l), ALU.mult).then_inc(mb_done, 1)
                level(0)
                level(1)
                for g in range(NQ):
                    t.need("kh", g)
                    tt(tiles4("kbg", g), tiles4("kh", g), rows(C_BEG, g), ALU.mult).then_inc(R_["kbg"], 1)
                level(2)
                for g in range(NQ):
                    tt(tiles4("kd", g), tiles4("kh", g), rows(C_ES, g), ALU.mult).then_inc(R_["kd"], 1)
                if proj:
                    split_lo(pool, TILE_HEAD + 7, i, 4)
                for l in range(3, NL):
                    level(l)
                if proj:
                    split_lo(pool, TILE_HEAD + 8, i, 4)
                for g in range(NQ):
                    t.out(f"o{g}")
                    tt(tiles4("onx", g), tiles4("on", g), tiles4("on", g), ALU.mult).then_inc(R_["sqo"], 1)
                    pool.wait_ge(R_["sso"], i * (2 * NQ) + (2 * g + 2))
                    tt(rsq[:, g, 2, :], ssq[:, g, 2, :], mh[:, 0:GT], ALU.pow).then_inc(R_["ro"], 1)
                if proj:
                    split_lo(pool, TILE_HEAD + 9, i, 4)

            def sp_turn(sp, i, proj):
                if proj:
                    for s in range(4):
                        load_w(sp, TILE_HEAD + 7 + s, i, 4)
                for g in range(NQ):
                    sp.wait_ge(R_["oz"], i * NQ + (g + 1))
                    sp.dma_start(oz_dram[i][:, g * HALF:(g + 1) * HALF], flat("oz", g)).then_inc(oz_stored, 16)

            with nc.Block() as block:
                @block.sync
                def _(sp):
                    sp.dma_start(cw_all[:, :, :], a["conv"]).then_inc(conv_in, 16)
                    sp.dma_start(nw[:, :], a["normw"]).then_inc(conv_in, 16)
                    sp.sem_inc(oz_stored, 16)
                    load_w(sp, TILE_HEAD + 3)
                    for s in range(3):
                        load_w(sp, TILE_HEAD + 4 + s)
                    with sp.Fori(0, HEADS - 1) as i:
                        sp_turn(sp, i, True)
                    sp_turn(sp, HEADS - 1, False)
                    sp.wait_ge(oz_stored, 16 * NQ * HEADS + 16)

                @block.tensor
                def _(pe):
                    for u in range(64):
                        s, n, k = u // 16, u // 8 % 2, u % 8
                        t = TILE_HEAD + s
                        if u % 16 == 0:
                            pe.wait_ge(w_lo, t + 1)
                            if s >= 2:
                                pe.wait_ge(cin_ready, 1 + s - 2)
                        mm = product3(pe, pair[s % 2][:, n, :], wH[:, t % 2, k * P:(k + 1) * P], wL[:, t % 2, k * P:(k + 1) * P],
                                      hH[:, k, n * HALF:(n + 1) * HALF], hL[:, k, n * HALF:(n + 1) * HALF], k == 0, k == KT - 1)
                        if u % 16 == 15:
                            mm.then_inc(w_used, 1)
                    for b in range(4):
                        pe.sem_inc(evicted[b], 1)
                    with pe.Fori(0, HEADS - 1) as i:
                        pe_turn(pe, i, True)
                    pe_turn(pe, HEADS - 1, False)

                @block.scalar
                def _(act):
                    for s in range(4):
                        if s < 3:
                            act.wait_ge(w_used, TILE_HEAD + s + 1)
                            act.wait_ge(conv_step, 4 * s + 1)
                            act.activation(cin[:, CONV_K - 1:], pair[s % 2][:, :, :].rearrange("p a b -> p (a b)"), ACT.Copy).then_inc(cin_ready, 1)
                            split_hi(act, TILE_HEAD + 2 + s)
                            act.wait_ge(conv_step, 4 * s + 5)
                            if s:
                                act.wait_ge(conv_ready, s)
                            act.activation(th[:, :], acc[:, :], ACT.Tanh, scale=0.5).then_inc(th_ready, 1)
                        else:
                            act.wait_ge(w_used, TILE_HEAD + 4)
                            split_hi(act, TILE_HEAD + 5)
                            act.wait_ge(conv_ready, 3)
                            act.activation(th[:, :], pair[1][:, :, :].rearrange("p a b -> p (a b)"), ACT.Tanh, scale=0.5).then_inc(th_ready, 1)
                    with act.Fori(0, HEADS - 1) as i:
                        act_turn(act, i, True)
                    act_turn(act, HEADS - 1, False)

                @block.gpsimd
                def _(pool):
                    pool.memset(mh[:, :], -0.5).then_inc(mh_ready, 1)
                    pool.wait_ge(mh_ready, 1)
                    for s in range(4):
                        split_lo(pool, TILE_HEAD + 2 + s)
                    with pool.Fori(0, HEADS - 1) as i:
                        pool_turn(pool, i, True)
                    pool_turn(pool, HEADS - 1, False)

                @block.vector
                def _(dve):
                    dve.memset(cin[:, 0:CONV_K - 1], 0.0).then_inc(const_ready, 1)
                    dve.sem_inc(conv_step, 1)
                    dve.wait_ge(conv_in, 32)
                    dve_cw(dve, 0)
                    dve.wait_ge(const_ready, 2)
                    dve.tensor_scalar(nw[:, :], nw[:, :], 0.5, None, ALU.mult).then_inc(nw_ready, 1)
                    dve.wait_ge(nw_ready, 1)
                    for s in range(3):
                        dve.wait_ge(cin_ready, s + 1)
                        if s:
                            dve.wait_ge(conv_ready, s)
                        dve.tensor_scalar(acc[:, :], cin[:, 0:T], cw[:, CONV_K * s:CONV_K * s + 1], None, ALU.mult).then_inc(conv_step, 1)
                        for tap in range(1, CONV_K):
                            dve.wait_ge(conv_step, 4 * s + tap + 1)
                            dve.scalar_tensor_tensor(acc[:, :], cin[:, tap:tap + T], cw[:, CONV_K * s + tap:CONV_K * s + tap + 1], acc[:, :],
                                                     ALU.mult, ALU.add).then_inc(conv_step, 1)
                        dve.wait_ge(th_ready, s + 1)
                        dve.scalar_tensor_tensor((qc, kc, vc)[s][:, :], th[:, :], 1.0, acc[:, :], ALU.add, ALU.mult).then_inc(conv_ready, 1)
                    dve.wait_ge(th_ready, 4)
                    dve.scalar_tensor_tensor(zs[:, :], th[:, :], 1.0, pair[1][:, :, :].rearrange("p a b -> p (a b)"), ALU.add,
                                             ALU.mult).then_inc(zs_ready, 1)
                    with dve.Fori(0, HEADS - 1) as i:
                        dve_turn(dve, i, True)
                    dve_turn(dve, HEADS - 1, False)

        dstack.close()

        with ExitStack() as c6:
            s6 = sb_in(c6)
            ozH, ozL = s6("ozH", [P, HEADS, T], F32R), s6("ozL", [P, HEADS, T], F32R)
            ygH, ygL = s6("ygH", [P, CT, T], F32R), s6("ygL", [P, CT, T], F32R)
            stg = s6("stg", [P, 4, T])
            TA, TB, M1, MG = range(4)
            NB = HEADS + CT
            b_landed = [sem(f"b_landed{n}") for n in range(4)]
            bH_done, bL_pool, bL_dve = sem("bH_done"), sem("bL_pool"), sem("bL_dve")
            gate_act = sem("gate_act")
            merge_dve = sem("merge_dve")
            mg_stored = sem("mg_stored")
            hi_of = lambda j: ozH[:, j, :] if j < HEADS else ygH[:, j - HEADS, :]
            lo_of = lambda j: ozL[:, j, :] if j < HEADS else ygL[:, j - HEADS, :]

            def branch_lo(eng, j, done):
                eng.wait_ge(bH_done, j + 1)
                eng.tensor_tensor(lo_of(j), stg[:, j % 4, :], hi_of(j).bitcast(F32), ALU.subtract).then_inc(done, 1)

            def merge_pe(pe, i):
                for s, (dst, xh, xl, kt) in enumerate(((pair[0], hH, hL, KT), (pair[1], hH, hL, KT),
                                                       (work[:, 0:2, :], ozH, ozL, HEADS), (work[:, 2:4, :], ygH, ygL, CT))):
                    t = TILE_MERGE + s
                    pe.wait_ge(w_lo, i * 4 + (t + 1))
                    if s < 2:
                        pe.wait_ge(gate_act, i * 2 + (s + 1))
                    else:
                        pe.wait_ge(merge_dve, i * 4 + (2 * s - 3))
                    if s == 2:
                        pe.wait_ge(bL_pool, NB // 2)
                        pe.wait_ge(bL_dve, NB // 2)
                    for n in range(2):
                        for k in range(kt):
                            mm = product3(pe, dst[:, n, :], wH[:, t % 2, k * P:(k + 1) * P], wL[:, t % 2, k * P:(k + 1) * P],
                                          xh[:, k, n * HALF:(n + 1) * HALF], xl[:, k, n * HALF:(n + 1) * HALF], k == 0, k == kt - 1)
                    mm.then_inc(w_used, 1)

            def merge_act(act, i, last):
                for s in range(4):
                    act.wait_ge(w_used, i * 4 + (TILE_MERGE + s + 1))
                    if not (last and s >= 2):
                        split_hi(act, TILE_MERGE + 2 + s, i, 4)
                    if s < 2:
                        act.wait_ge(merge_dve, i * 4 + (2 * s + 1))
                        act.activation(stg[:, (TA, TB)[s], :], pair[s][:, :, :].rearrange("p a b -> p (a b)"), ACT.Tanh,
                                       scale=0.5).then_inc(gate_act, 1)

            def merge_dve_turn(dve, i):
                dve.wait_ge(gate_act, i * 2 + 4)
                dve.wait_ge(w_used, i * 4 + (TILE_MERGE + 3))
                dve.wait_ge(merge_dve, i * 4 + 4)
                dve.scalar_tensor_tensor(stg[:, M1, :], stg[:, TA, :], 1.0, work[:, 0:2, :].rearrange("p a b -> p (a b)"),
                                         ALU.add, ALU.mult).then_inc(merge_dve, 1)
                dve.tensor_scalar(stg[:, TB, :], stg[:, TB, :], 1.0, 0.125, ALU.add, ALU.mult).then_inc(merge_dve, 1)
                dve.wait_ge(w_used, i * 4 + (TILE_MERGE + 4))
                dve.wait_ge(merge_dve, i * 4 + 6)
                dve.wait_ge(mg_stored, i * 16 + 16)
                dve.tensor_tensor(stg[:, MG, :], stg[:, TB, :], work[:, 2:4, :].rearrange("p a b -> p (a b)"), ALU.mult).then_inc(merge_dve, 1)
                dve.wait_ge(merge_dve, i * 4 + 7)
                dve.tensor_tensor(stg[:, MG, :], stg[:, M1, :], stg[:, MG, :], ALU.add).then_inc(merge_dve, 1)

            def merge_sp(sp, i, last):
                for s in range(1 if last else 4):
                    load_w(sp, TILE_MERGE + 3 + s, i, 4)
                sp.wait_ge(merge_dve, i * 4 + 8)
                sp.dma_start(mg_dram[i], stg[:, MG, :]).then_inc(mg_stored, 16)

            with nc.Block() as block:
                @block.sync
                def _(sp):
                    for j in range(NB):
                        if j >= 4:
                            sp.wait_ge((bL_pool, bL_dve)[j % 2], (j - 4) // 2 + 1)
                        sp.dma_start(stg[:, j % 4, :], oz_dram[j] if j < HEADS else yg_dram[j - HEADS]).then_inc(b_landed[j % 4], 16)
                    sp.sem_inc(mg_stored, 16)
                    with sp.Fori(0, KT - 1) as i:
                        merge_sp(sp, i, False)
                    merge_sp(sp, KT - 1, True)
                    sp.wait_ge(mg_stored, 16 * KT + 16)

                @block.tensor
                def _(pe):
                    with pe.Fori(0, KT) as i:
                        merge_pe(pe, i)

                @block.scalar
                def _(act):
                    act.sem_inc(gate_act, 2)
                    for j in range(NB):
                        act.wait_ge(b_landed[j % 4], 16 * (j // 4 + 1))
                        act.activation(hi_of(j), stg[:, j % 4, :], ACT.Copy).then_inc(bH_done, 1)
                    act.wait_ge(bL_pool, NB // 2)
                    act.wait_ge(bL_dve, NB // 2)
                    with act.Fori(0, KT - 1) as i:
                        merge_act(act, i, False)
                    merge_act(act, KT - 1, True)

                @block.gpsimd
                def _(pool):
                    for j in range(0, NB, 2):
                        branch_lo(pool, j, bL_pool)
                    with pool.Fori(0, KT - 1) as i:
                        for s in range(4):
                            split_lo(pool, TILE_MERGE + 2 + s, i, 4)
                    for s in range(2):
                        split_lo(pool, TILE_MERGE + 2 + s, KT - 1, 4)

                @block.vector
                def _(dve):
                    for j in range(1, NB, 2):
                        branch_lo(dve, j, bL_dve)
                    dve.wait_ge(bL_pool, NB // 2)
                    dve.sem_inc(merge_dve, 4)
                    with dve.Fori(0, KT) as i:
                        merge_dve_turn(dve, i)
        hstack.close()

        with ExitStack() as c7:
            s7 = sb_in(c7)
            wo = s7("wo", [P, KT, D])
            woH, woL = s7("woH", [P, KT, D], F32R), s7("woL", [P, KT, D], F32R)
            diag = s7("diag", [P, KT, P])
            gate = s7("gate", [P, D])
            fnw = s7("fnw", [P, D])
            xt = s7("xt", [P, 2, D])
            y = s7("y", [P, 2, D])
            ss = s7("ss7", [P, 2])
            rs = s7("rs7", [P, 2])
            mh = s7("mh7", [P, 1])
            wo_in = [sem(f"wo_in{k}") for k in range(KT)]
            woH_done, woL_pool, woL_dve = sem("woH_done"), sem("woL_pool"), sem("woL_dve")
            fn_in, diag_done = sem("fn_in"), sem("diag_done")
            gate_full, gate_done = sem("gate_full"), sem("gate_done")
            x7_in, out_stored = [sem("x7_in0"), sem("x7_in1")], [sem("out_stored0"), sem("out_stored1")]
            out_dve = sem("out_dve")
            sq7_done, rs_done, mh7_done = sem("sq7_done"), sem("rs_done"), sem("mh7_done")
            mgv = mg_dram.rearrange("m p (n t) -> n p m t", n=NT)
            with nc.Block() as block:
                @block.sync
                def _(sp):
                    def load_merged(i, s):
                        t = TILE_OUT + s
                        sp.wait_ge(w_lo, i * 2 + (t - 1))
                        sp.dma_start(raw[:, t % 2, :].rearrange("p (m t) -> p m t", m=KT), mgv[i * 2 + s]).then_inc(w_landed[t % 2], 16)
                    for k in range(KT):
                        sp.dma_start(wo[:, k, :], a["wout"][:, k, :]).then_inc(wo_in[k], 16)
                    for s in range(2):
                        sp.sem_inc(out_stored[s], 16)
                    with sp.Fori(0, NT // 2) as i:
                        for s in range(2):
                            load_merged(i, s)
                        for s in range(2):
                            sp.wait_ge(out_dve, i * 8 + (4 * s + 2))
                            sp.dma_start(xt[:, s, :], a["x"][i * 2 + s]).then_inc(x7_in[s], 16)
                        for s in range(2):
                            sp.wait_ge(out_dve, i * 8 + (4 * s + 12))
                            sp.dma_start(out[0].rearrange("(n p) d -> n p d", p=P)[i * 2 + s], y[:, s, :]).then_inc(out_stored[s], 16)
                    for s in range(2):
                        sp.wait_ge(out_stored[s], 16 * (NT // 2) + 16)

                @block.tensor
                def _(pe):
                    pe.wait_ge(diag_done, KT)
                    for k in range(KT):
                        mm = pe.matmul(work[:, k // 4, k % 4 * P:(k % 4 + 1) * P], cst[:, ONES, :], diag[:, k, :], start=True, stop=True)
                    mm.then_inc(gate_full, 1)
                    pe.wait_ge(woL_pool, KT // 2)
                    pe.wait_ge(woL_dve, KT // 2)
                    with pe.Fori(0, NT // 2) as i:
                        for s in range(2):
                            t = TILE_OUT + s
                            pe.wait_ge(w_lo, i * 2 + (t + 1))
                            pe.wait_ge(out_dve, i * 8 + (4 * s + 1))
                            for n in range(2):
                                for k in range(KT):
                                    mm = product3(pe, pair[s][:, n, :], wH[:, t % 2, k * P:(k + 1) * P], wL[:, t % 2, k * P:(k + 1) * P],
                                                  woH[:, k, n * HALF:(n + 1) * HALF], woL[:, k, n * HALF:(n + 1) * HALF], k == 0, k == KT - 1)
                            mm.then_inc(w_used, 1)

                @block.scalar
                def _(act):
                    act.dma_start(fnw[:, :], a["fnw"]).then_inc(fn_in, 16)
                    for k in range(KT):
                        act.wait_ge(wo_in[k], 16)
                        act.activation(woH[:, k, :], wo[:, k, :], ACT.Copy).then_inc(woH_done, 1)
                    act.sem_inc(sq7_done, 1)
                    with act.Fori(0, NT // 2) as i:
                        for s in range(2):
                            split_hi(act, TILE_OUT + s, i, 2)
                        for s in range(2):
                            act.wait_ge(out_dve, i * 8 + (4 * s + 10))
                            act.wait_ge(sq7_done, i * 2 + (s + 1))
                            act.activation(wo[:, 0, :], y[:, s, :], ACT.Square, accum_out=ss[:, s:s + 1]).then_inc(sq7_done, 1)

                @block.gpsimd
                def _(pool):
                    pool.memset(mh[:, :], -0.5).then_inc(mh7_done, 1)
                    pool.wait_ge(mh7_done, 1)
                    for k in range(0, KT, 2):
                        pool.wait_ge(woH_done, k + 1)
                        pool.tensor_tensor(woL[:, k, :], wo[:, k, :], woH[:, k, :].bitcast(F32), ALU.subtract).then_inc(woL_pool, 1)
                    with pool.Fori(0, NT // 2) as i:
                        for s in range(2):
                            split_lo(pool, TILE_OUT + s, i, 2)
                        for s in range(2):
                            pool.wait_ge(out_dve, i * 8 + (4 * s + 11))
                            pool.tensor_tensor(rs[:, s:s + 1], ss[:, s:s + 1], mh[:, :], ALU.pow).then_inc(rs_done, 1)

                @block.vector
                def _(dve):
                    for k in range(KT):
                        dve.tensor_scalar(diag[:, k, :], ident, modT[:, 2 * KT + k:2 * KT + k + 1], 0.5, ALU.mult, ALU.mult).then_inc(diag_done, 1)
                    for k in range(1, KT, 2):
                        dve.wait_ge(woH_done, k + 1)
                        dve.tensor_tensor(woL[:, k, :], wo[:, k, :], woH[:, k, :].bitcast(F32), ALU.subtract).then_inc(woL_dve, 1)
                    dve.wait_ge(woL_pool, KT // 2)
                    dve.wait_ge(gate_full, 1)
                    dve.tensor_copy(gate[:, :], work[:, 0:2, :].rearrange("p a b -> p (a b)")).then_inc(gate_done, 1)
                    dve.wait_ge(gate_done, 1)
                    dve.wait_ge(fn_in, 16)
                    dve.sem_inc(out_dve, 8)
                    with dve.Fori(0, NT // 2) as i:
                        for s in range(2):
                            dve.wait_ge(w_used, i * 2 + (TILE_OUT + s + 1))
                            dve.wait_ge(out_stored[s], i * 16 + 16)
                            dve.tensor_tensor(y[:, s, :], pair[s][:, :, :].rearrange("p a b -> p (a b)"), gate[:, :], ALU.mult).then_inc(out_dve, 1)
                            dve.wait_ge(out_dve, i * 8 + (4 * s + 9))
                            dve.wait_ge(x7_in[s], i * 16 + 16)
                            dve.tensor_tensor(y[:, s, :], y[:, s, :], xt[:, s, :], ALU.add).then_inc(out_dve, 1)
                            dve.wait_ge(sq7_done, i * 2 + (s + 2))
                            dve.tensor_scalar(ss[:, s:s + 1], ss[:, s:s + 1], 1.0 / D, EPS, ALU.mult, ALU.add).then_inc(out_dve, 1)
                            dve.wait_ge(rs_done, i * 2 + (s + 1))
                            dve.scalar_tensor_tensor(y[:, s, :], y[:, s, :], rs[:, s:s + 1], fnw[:, :], ALU.mult, ALU.mult).then_inc(out_dve, 1)


_OUTS = [((1, T, D), 'float32')]


def _layout(i):
    import numpy as np
    f = lambda n: np.asarray(i[n])
    w_in = f('w_in')[0]
    qkvz = 4 * HEADS * HD
    u0 = qkvz + 2 * HEADS

    def tiles(w, col, n=1):
        k = w.shape[0] // P
        return np.concatenate([w[:, col + P * m:col + P * (m + 1)].reshape(k, P, P).transpose(1, 0, 2).reshape(P, k * P)[None]
                               for m in range(n)])
    glu, wa, wb = f('s5_glu_w')[0], f('w_proj_a')[0], f('w_proj_b')[0]
    parts = [tiles(w_in, qkvz)]
    for m in range(CT):
        parts += [tiles(w_in, u0 + m * P), tiles(w_in, u0 + S5W + m * P)]
    gt = tiles(glu, 0, CT)
    parts.append(np.stack([np.concatenate([gt[2 * m], gt[2 * m + 1]], 1) for m in range(2)]))
    for h in range(HEADS):
        for s in range(4):
            parts.append(tiles(w_in, s * HEADS * HD + h * HD))
    for m in range(KT):
        parts.append(tiles(w_in, u0 + 2 * S5W + m * P))
        parts.append(tiles(w_in, u0 + 2 * S5W + D + m * P))
        parts.append(tiles(wa, m * P))
        b = tiles(wb, m * P)
        parts.append(np.concatenate([b, b], 2))
    col = lambda v: v.reshape(-1, P).T
    ada = f('w_ada')[0].reshape(KT, P, 3, D).transpose(2, 1, 0, 3)
    dup = lambda v: np.concatenate([v, v], 0)
    p_, f_ = np.arange(P)[:, None], np.arange(P)[None, :]
    cst = [p_ == f_, p_ <= f_, p_ > f_, p_ >= f_, p_ >= 0 * f_]
    cst += [(p_ // (2 * b) == f_ // (2 * b)) & (p_ % (2 * b) >= b) & (f_ % (2 * b) < b) for b in LEVELS]
    conv = f('dn_conv_w')[0].reshape(CONV_K, 3, HEADS, P).transpose(3, 2, 1, 0)
    d = {
        'w': np.concatenate(parts),
        'x': f('x')[0].reshape(NT, P, D),
        'cT': col(f('c')[0]),
        'bada': col(f('b_ada')[0]),
        'wada': ada,
        'cst': np.stack([np.broadcast_to(m, (P, P)).astype(np.float32) for m in cst], 1),
        'dtb': np.broadcast_to(f('dn_dt_bias')[0], (P, HEADS)),
        'alog': np.broadcast_to(f('dn_a_log')[0], (P, HEADS)),
        'conv': conv.reshape(P, HEADS, 3 * CONV_K),
        'normw': f('dn_norm_w')[0].reshape(P, 1),
        's5p': np.stack([dup(f('s5_lambda_re')[0].T), dup(f('s5_lambda_im')[0].T),
                         np.broadcast_to(f('s5_log_dt')[0], (P, GROUPS))], 1),
        's5b': np.stack([dup(f('s5_b_re')[0].transpose(1, 0, 2)), dup(f('s5_b_im')[0].transpose(1, 0, 2))], 1),
        's5c': np.stack([dup(f('s5_c_re')[0].transpose(2, 0, 1)), dup(f('s5_c_im')[0].transpose(2, 0, 1))], 1),
        's5d': col(f('s5_d')[0]),
        'glub': col(f('s5_glu_b')[0]),
        'wout': f('w_out')[0].reshape(KT, P, D).transpose(1, 0, 2),
        'fnw': np.broadcast_to(f('final_norm_w'), (P, D)),
    }
    return {k: np.ascontiguousarray(v) for k, v in d.items()}


def kernel(**inputs):
    import numpy as _np
    import concourse.bacc as _bacc
    from concourse.bass_utils import run_bass_kernel_spmd as _run

    nc = _bacc.Bacc("TRN2", target_bir_lowering=False, num_devices=1)
    arrays, aps = {}, {}
    for name, v in _layout(inputs).items():
        arrays[f"in_{name}_dram"] = v
        aps[name] = nc.dram_tensor(f"in_{name}_dram", v.shape, mybir.dt.from_np(v.dtype), kind="ExternalInput").ap()
    out = nc.dram_tensor("out_0_dram", (1, T, D), F32, kind="ExternalOutput").ap()
    oz = nc.dram_tensor("oz_scratch", (HEADS, P, T), F32, kind="Internal").ap()
    yg = nc.dram_tensor("yg_scratch", (CT, P, T), F32, kind="Internal").ap()
    mg = nc.dram_tensor("mg_scratch", (KT, P, T), F32, kind="Internal").ap()
    build_program(nc, aps, out, oz, yg, mg)
    r = _run(nc, [arrays], core_ids=[0])
    return r.results[0]["out_0_dram"]
```

```python
from contextlib import ExitStack
import concourse.bass as bass
from concourse import mybir

P = 128
D = 1024
T = 1024
HEADS, HD = 8, 128
KT = D // P
NT = T // P
HALF = T // 2
CONV_K = 4
S5W, GROUPS, GI, PS = 512, 32, 16, 64
CT = S5W // P
CG = P // GI
STEP = 8
NCH = T // STEP
EPS = 1e-6
CW = 256
RING = 3
CK = D // CW
SHIFT, SCALE, GATE = range(3)
NQ = 2
GT = NT // NQ

TILE_BA, TILE_UZ, TILE_GLU, TILE_HEAD = 0, 1, 9, 11
TILE_MERGE = TILE_HEAD + 4 * HEADS
TILE_FIRST = TILE_MERGE + 4
TILE_LOOP = TILE_FIRST + 4
TILE_OUT = TILE_MERGE + 4 * KT
EARLY = 2
LEVELS = (1, 2, 4, 8, 16, 32, 64)
IDENT, LE, GT_, GE, ONES, LEVEL0 = 0, 1, 2, 3, 4, 5
NCONST = LEVEL0 + len(LEVELS)
C_G, C_BETA, C_EG, C_ES, C_EGL, C_BEG, C_HB = range(7)
NCOL = 7

F32, F32R = mybir.dt.float32, mybir.dt.float32r
I32 = mybir.dt.int32
ACT = mybir.ActivationFunctionType
ALU = mybir.AluOpType
AX = mybir.AxisListType.X


def bc(ap, shape):
    return ap.to_broadcast(shape)


def build_program(nc, a, out, oz_dram, yg_dram, mg_dram):
    ctx = ExitStack()
    with ctx:
        def sb_in(c):
            return lambda name, shape, dt=F32: c.enter_context(nc.sbuf_tensor(name, shape, dt))

        def sem(name):
            return ctx.enter_context(nc.semaphore(name))

        sb = sb_in(ctx)
        cst = sb("cst", [P, NCONST, P])
        cT = sb("cT", [P, KT])
        bada = sb("bada", [P, 3 * KT])
        modT = sb("modT", [P, 3 * KT])
        raw = sb("raw", [P, 2, D])
        wH = sb("wH", [P, 2, D], F32R)
        wL = sb("wL", [P, 2, D], F32R)
        pair = [ctx.enter_context(nc.psum_tensor(f"pair{n}", [P, 2, HALF], F32)) for n in range(2)]
        work = ctx.enter_context(nc.psum_tensor("work", [P, 4, 512], F32))
        ident = cst[:, IDENT, :]

        w_landed = [sem("w_landed0"), sem("w_landed1")]
        w_hi = sem("w_hi")
        w_lo = sem("w_lo")
        w_used = sem("w_used")

        def load_w(sp, base, it=0, per=0, width=D, src=None):
            t0 = base
            if t0 >= 2:
                sp.wait_ge(w_lo, it * per + (t0 - 1))
            if src is None:
                src = a["w"][it * per + t0]
            sp.dma_start(raw[:, t0 % 2, 0:width], src[:, 0:width]).then_inc(w_landed[t0 % 2], 16)

        def split_hi(act, base, it=0, per=0, width=D):
            act.wait_ge(w_landed[base % 2], it * (8 * per) + 16 * (base // 2 + 1))
            if base >= 2:
                act.wait_ge(w_used, it * per + (base - 1))
            act.activation(wH[:, base % 2, 0:width], raw[:, base % 2, 0:width], ACT.Copy).then_inc(w_hi, 1)

        def split_lo(pool, base, it=0, per=0, width=D):
            pool.wait_ge(w_hi, it * per + (base + 1))
            pool.tensor_tensor(wL[:, base % 2, 0:width], raw[:, base % 2, 0:width],
                               wH[:, base % 2, 0:width].bitcast(F32), ALU.subtract).then_inc(w_lo, 1)

        def product3(pe, dst, wh, wl, xh, xl, first, last):
            pe.matmul(dst, wh, xh, start=first, stop=False)
            pe.matmul(dst, wh, xl, start=False, stop=False)
            return pe.matmul(dst, wl, xh, start=False, stop=last)

        def ada_sum(dve, chunk, acc, c, step):
            dst = acc[:, c * CW:(c + 1) * CW]
            for k in range(KT):
                if k == 0:
                    dve.tensor_scalar(dst, chunk[:, 0, :], cT[:, 0:1], None, ALU.mult).then_inc(step, 1)
                else:
                    dve.scalar_tensor_tensor(dst, chunk[:, k, :], cT[:, k:k + 1], dst, ALU.mult, ALU.add).then_inc(step, 1)
                dve.wait_ge(step, KT * c + k + 1)

        def summed_columns(pe, m, acc, step):
            pe.wait_ge(step, KT * CK)
            for q in range(KT):
                mm = pe.matmul(work[:, m, q:q + 1], acc[:, q * P:(q + 1) * P], cst[:, ONES, 0:1], start=True, stop=True)
            return mm

        hstack = ExitStack()
        hsb = sb_in(hstack)
        hH = hsb("hH", [P, KT, T], F32R)
        hL = hsb("hL", [P, KT, T], F32R)
        dstack = ExitStack()
        dsb = sb_in(dstack)
        cols = dsb("cols", [P, HEADS, NCOL, NT])
        gstack = ExitStack()
        psb = sb_in(gstack)
        s5p = psb("s5p", [P, 3, GROUPS])
        s5b = psb("s5b", [P, 2, GROUPS, GI])
        s5c = psb("s5c", [P, 2, GROUPS, GI])
        s5d = psb("s5d", [P, CT])
        q = psb("q", [P, 14, GROUPS])
        are = psb("are", [P, STEP + 1, GROUPS])
        aim = psb("aim", [P, STEP + 1, GROUPS])
        pw = psb("pw", [P, 2, 4, GROUPS])
        ua = psb("ua", [P, STEP, GROUPS])
        va = psb("va", [P, STEP, GROUPS])
        ca = psb("ca", [P, STEP + 1, GROUPS])
        cb = psb("cb", [P, STEP + 1, GROUPS])
        bbst = psb("bbst", [P, GROUPS, GI])
        LR, LI, DTT, TH, LDT, NN, SN, SH, CC, MAG, MG8, T_A, T_B, DEN = range(14)
        Q = lambda n: q[:, n, :]
        s5_in = sem("s5_in")
        par = sem("par")
        par_act = sem("par_act")
        bb_done = sem("bb_done")
        PAR_DONE = 68

        def s5_params_act(act):
            act.wait_ge(s5_in, 64)
            act.activation(Q(DTT), s5p[:, 2, :], ACT.Exp).then_inc(par_act, 1)
            act.wait_ge(par, 11)
            act.activation(Q(MAG), Q(LDT), ACT.Exp).then_inc(par_act, 1)
            act.activation(Q(MG8), Q(LDT), ACT.Exp, scale=float(STEP)).then_inc(par_act, 1)
            act.activation(Q(SN), Q(TH), ACT.Sin).then_inc(par_act, 1)
            act.activation(Q(SH), Q(TH), ACT.Sin, scale=0.5).then_inc(par_act, 1)

        def s5_params_pool(pool, bscr):
            pool.wait_ge(par, 30)
            pool.wait_ge(s5_in, 64)
            br, bi = s5b[:, 0, :, :], s5b[:, 1, :, :]
            fr = Q(T_A).unsqueeze(2).to_broadcast([P, GROUPS, GI])
            fi = Q(T_B).unsqueeze(2).to_broadcast([P, GROUPS, GI])
            r_, i_ = bscr[:, 0, :, :], bscr[:, 1, :, :]
            n = [0]

            def link(ins):
                n[0] += 1
                ins.then_inc(bb_done, 1)
                pool.wait_ge(bb_done, n[0])
            link(pool.tensor_tensor(bbst[:, :, :], fi, bi, ALU.mult))
            link(pool.tensor_tensor(r_, fr, br, ALU.mult))
            link(pool.tensor_tensor(r_, r_, bbst[:, :, :], ALU.subtract))
            link(pool.tensor_tensor(i_, fr, bi, ALU.mult))
            link(pool.tensor_tensor(bbst[:, :, :], fi, br, ALU.mult))
            link(pool.tensor_tensor(s5b[:, 1, :, :], i_, bbst[:, :, :], ALU.add))
            link(pool.tensor_copy(s5b[:, 0, :, :], r_))
            link(pool.tensor_copy(bbst[0:PS, :, :], s5b[0:PS, 0, :, :]))
            link(pool.tensor_copy(bbst[PS:P, :, :], s5b[PS:P, 1, :, :]))

        def s5_params_dve(dve):
            n = [0]

            def link(ins):
                n[0] += 1
                ins.then_inc(par, 1)
                dve.wait_ge(par, n[0])
            tt = dve.tensor_tensor
            MAGIC = 1.5 * 2.0 ** 23
            TWO_PI = (6.28125, 1.9350051879882812e-3, 3.0199159819567e-07)
            dve.wait_ge(s5_in, 64)
            link(dve.tensor_scalar(Q(LR), s5p[:, 0, :], -1e-4, None, ALU.min))
            link(dve.tensor_copy(Q(LI), s5p[:, 1, :]))
            dve.wait_ge(par_act, 1)
            link(tt(Q(TH), Q(LI), Q(DTT), ALU.mult))
            link(tt(Q(LDT), Q(LR), Q(DTT), ALU.mult))
            link(dve.tensor_scalar(Q(NN), Q(TH), 0.15915494309189535, None, ALU.mult))
            link(dve.tensor_scalar(Q(NN), Q(NN), MAGIC, None, ALU.add))
            link(dve.tensor_scalar(Q(NN), Q(NN), MAGIC, None, ALU.subtract))
            for c in TWO_PI:
                link(dve.scalar_tensor_tensor(Q(TH), Q(NN), -c, Q(TH), ALU.mult, ALU.add))
            link(dve.tensor_scalar(Q(TH), Q(TH), 3.1415925, -3.1415925, ALU.min, ALU.max))
            assert n[0] == 11
            dve.wait_ge(par_act, 5)
            link(tt(Q(T_A), Q(SH), Q(SH), ALU.mult))
            link(dve.tensor_scalar(Q(CC), Q(T_A), -2.0, 1.0, ALU.mult, ALU.add))
            link(tt(are[:, 1, :], Q(MAG), Q(CC), ALU.mult))
            link(tt(aim[:, 1, :], Q(MAG), Q(SN), ALU.mult))
            link(dve.memset(are[:, 0, :], 1.0))
            link(dve.memset(aim[:, 0, :], 0.0))
            link(tt(Q(T_A), Q(LR), Q(LR), ALU.mult))
            link(tt(Q(T_B), Q(LI), Q(LI), ALU.mult))
            link(tt(Q(DEN), Q(T_A), Q(T_B), ALU.add))
            link(dve.reciprocal(Q(DEN), Q(DEN)))
            link(dve.tensor_scalar(Q(NN), are[:, 1, :], 1.0, None, ALU.subtract))
            link(tt(Q(T_A), Q(NN), Q(LR), ALU.mult))
            link(tt(Q(T_B), aim[:, 1, :], Q(LI), ALU.mult))
            link(tt(Q(T_A), Q(T_A), Q(T_B), ALU.add))
            link(tt(Q(T_A), Q(T_A), Q(DEN), ALU.mult))
            link(tt(Q(T_B), aim[:, 1, :], Q(LR), ALU.mult))
            link(tt(Q(TH), Q(NN), Q(LI), ALU.mult))
            link(tt(Q(T_B), Q(T_B), Q(TH), ALU.subtract))
            link(tt(Q(T_B), Q(T_B), Q(DEN), ALU.mult))
            assert n[0] == 30
            for _r in range(3):
                link(tt(Q(LDT), Q(CC), Q(CC), ALU.mult))
                link(tt(Q(NN), Q(SN), Q(SN), ALU.mult))
                link(dve.scalar_tensor_tensor(Q(SN), Q(CC), 2.0, Q(SN), ALU.mult, ALU.mult))
                link(tt(Q(CC), Q(LDT), Q(NN), ALU.subtract))
            for m in (1, 2, 4):
                sr, si = are[:, 1:m + 1, :], aim[:, 1:m + 1, :]
                br = are[:, m:m + 1, :].to_broadcast([P, m, GROUPS])
                bi = aim[:, m:m + 1, :].to_broadcast([P, m, GROUPS])
                x0, x1 = pw[:, 0, 0:m, :], pw[:, 1, 0:m, :]
                link(tt(x0, sr, br, ALU.mult))
                link(tt(x1, si, bi, ALU.mult))
                link(tt(are[:, m + 1:2 * m + 1, :], x0, x1, ALU.subtract))
                link(tt(x0, sr, bi, ALU.mult))
                link(tt(x1, si, br, ALU.mult))
                link(tt(aim[:, m + 1:2 * m + 1, :], x0, x1, ALU.add))
            lo_, hi_ = slice(0, PS), slice(PS, P)
            for dst, rows, src, sgn in ((ua, lo_, are, 1.0), (ua, hi_, aim, 1.0), (va, lo_, aim, -1.0), (va, hi_, are, 1.0),
                                        (ca, lo_, are, 1.0), (ca, hi_, aim, -1.0), (cb, lo_, aim, -1.0), (cb, hi_, are, -1.0)):
                m = dst.shape[1]
                link(dve.tensor_scalar(dst[rows, :, :], src[rows, 0:m, :], sgn, None, ALU.mult))
            assert n[0] == PAR_DONE, n[0]

        with ExitStack() as c1:
            s1 = sb_in(c1)
            xr = s1("xr", [P, 4, D])
            xT = s1("xT", [P, KT, T])
            CHUNKS = [(m, c) for c in range(CK) for m in (SHIFT, SCALE)]
            acc = s1("acc_ada", [P, D])
            wada = s1("wada", [P, RING, KT, CW])
            ss = s1("ss", [P, NT])
            rstd = s1("rstd", [P, NT])
            mhalf = s1("mhalf", [P, 1])
            hf = s1("hf", [P, 4, HALF])
            bscr = xr[:, 0, :].rearrange("p (a g i) -> p a g i", a=2, i=GI)
            baT = hf[0:2 * HEADS, 0:2, :].rearrange("p a b -> p (a b)")
            ba = s1("ba", [P, NT, 2 * HEADS])
            dtb = s1("dtb", [P, HEADS])
            alog = s1("alog", [P, HEADS])
            ea = s1("ea", [P, HEADS])
            z = s1("z", [P, HEADS, NT])
            az = s1("az", [P, HEADS, NT])
            g = s1("g", [P, HEADS, NT])
            ex3 = s1("ex3", [P, 3, HEADS * NT])
            x_in = [sem(f"x_in{n}") for n in range(4)]
            c_in, b_in, k_in = sem("c_in"), sem("b_in"), sem("k_in")
            ada_in = [sem(f"ada_in{n}") for n in range(RING)]
            ada_free = [sem(f"ada_free{n}") for n in range(RING)]
            acc_step = sem("acc_step")
            ada_cols = sem("ada_cols")
            sq_done, ms_done, rstd_done, xn_done = sem("sq_done"), sem("ms_done"), sem("rstd_done"), sem("xn_done")
            x_t, xT_done, mod_done = sem("x_t"), sem("xT_done"), sem("mod_done")
            hf_done, hH_done, hL_pool, hL_dve = sem("hf_done"), sem("hH_done"), sem("hL_pool"), sem("hL_dve")
            par_in = sem("par_in")
            ba_copied, ba_t, ba_nat = sem("ba_copied"), sem("ba_t"), sem("ba_nat")
            col_act, col_dve, col_pe = sem("col_act"), sem("col_dve"), sem("col_pe")
            hs = lambda u: (slice(None), u // 2, slice(u % 2 * HALF, (u % 2 + 1) * HALF))

            def h_lo(eng, u, done):
                eng.wait_ge(hH_done, u + 1)
                eng.tensor_tensor(hL[hs(u)], hf[:, u % 4, :], hH[hs(u)].bitcast(F32), ALU.subtract).then_inc(done, 1)

            with nc.Block() as block:
                @block.sync
                def _(sp):
                    def load_x(n):
                        if n >= 4:
                            sp.wait_ge(x_t, n - 3)
                        sp.dma_start(xr[:, n % 4, :], a["x"][n]).then_inc(x_in[n % 4], 16)

                    def load_ada(c):
                        if c >= RING:
                            sp.wait_ge(ada_free[c % RING], c // RING)
                        m, q = CHUNKS[c]
                        sp.dma_start(wada[:, c % RING, :, :], a["wada"][m][:, :, q * CW:(q + 1) * CW]).then_inc(ada_in[c % RING], 16)
                    load_x(0)
                    load_x(1)
                    for dst, n in ((s5p, "s5p"), (s5b, "s5b"), (s5c, "s5c"), (s5d, "s5d")):
                        ap = dst[tuple([slice(None)] * len(a[n].shape))]
                        sp.dma_start(ap, a[n]).then_inc(s5_in, 16)
                    load_x(2)
                    load_x(3)
                    sp.dma_start(cst[:, :, :], a["cst"]).then_inc(k_in, 16)
                    load_ada(0)
                    load_ada(1)
                    for n in range(4, NT):
                        load_x(n)
                    load_ada(2)
                    load_w(sp, 0)
                    load_w(sp, 1)
                    for c in range(3, len(CHUNKS)):
                        load_ada(c)
                    load_w(sp, 2)
                    load_w(sp, 3)

                @block.scalar
                def _(act):
                    act.dma_start(cT[:, :], a["cT"]).then_inc(c_in, 16)
                    act.dma_start(bada[:, :], a["bada"]).then_inc(b_in, 16)
                    act.dma_start(dtb[:, :], a["dtb"]).then_inc(par_in, 16)
                    act.dma_start(alog[:, :], a["alog"]).then_inc(par_in, 16)

                    def evict_x(n):
                        act.wait_ge(x_t, n + 1)
                        act.activation(xT[:, :, n * P:(n + 1) * P], pair[n % 2][:, :, :].rearrange("p a (k t) -> p (a k) t", k=4),
                                       ACT.Copy).then_inc(xT_done, 1)
                    for n in range(NT):
                        act.wait_ge(x_in[n % 4], 16 * (n // 4 + 1))
                        if n >= 2:
                            act.wait_ge(sq_done, n - 1)
                        act.activation(hf[:, n % 2 * 2:n % 2 * 2 + 2, :].rearrange("p a b -> p (a b)"), xr[:, n % 4, :], ACT.Square,
                                       accum_out=ss[:, n:n + 1]).then_inc(sq_done, 1)
                        if n >= 1:
                            evict_x(n - 1)
                    evict_x(NT - 1)
                    s5_params_act(act)
                    split_hi(act, 0)
                    split_hi(act, 1)
                    for u in range(2 * KT):
                        act.wait_ge(hf_done, u + 1)
                        act.activation(hH[hs(u)], hf[:, u % 4, :], ACT.Copy).then_inc(hH_done, 1)
                    act.wait_ge(w_used, 1)
                    act.activation(baT, pair[0][0:16, :, :].rearrange("p a b -> p (a b)"), ACT.Copy).then_inc(ba_copied, 1)
                    act.wait_ge(ba_nat, 1)
                    act.wait_ge(par_in, 32)
                    act.activation(cols[:, :, C_BETA, :], ba[:, :, 0:HEADS].rearrange("p n h -> p h n"), ACT.Tanh,
                                   scale=0.5).then_inc(col_act, 1)
                    act.activation(ea[:, :], alog[:, :], ACT.Exp).then_inc(col_act, 1)
                    act.wait_ge(col_dve, 1)
                    act.activation(az[:, :, :], az[:, :, :], ACT.Exp, scale=-1.0).then_inc(col_act, 1)
                    act.wait_ge(col_act, 3)
                    act.activation(az[:, :, :], az[:, :, :], ACT.Ln, bias=1.0).then_inc(col_act, 1)
                    act.wait_ge(col_pe, 1)
                    act.activation(ex3[:, :, :].rearrange("p a b -> p (a b)"), work[:, 1, 0:192], ACT.Exp).then_inc(col_act, 1)
                    split_hi(act, 2)

                @block.gpsimd
                def _(pool):
                    pool.memset(mhalf[:, :], -0.5).then_inc(rstd_done, 1)
                    pool.wait_ge(rstd_done, 1)
                    for n in range(NT):
                        pool.wait_ge(ms_done, n + 1)
                        pool.tensor_tensor(rstd[:, n:n + 1], ss[:, n:n + 1], mhalf[:, :], ALU.pow).then_inc(rstd_done, 1)
                    pool.wait_ge(x_t, NT)
                    s5_params_pool(pool, bscr)
                    split_lo(pool, 0)
                    split_lo(pool, 1)
                    for u in range(0, 2 * KT, 2):
                        h_lo(pool, u, hL_pool)
                    split_lo(pool, 2)

                @block.tensor
                def _(pe):
                    def transpose_x(n):
                        pe.wait_ge(xn_done, n + 1)
                        if n >= 2:
                            pe.wait_ge(xT_done, n - 1)
                        for k in range(KT):
                            tr = pe.transpose(pair[n % 2][:, k // 4, k % 4 * P:(k % 4 + 1) * P], xr[:, n % 4, k * P:(k + 1) * P], ident)
                        tr.then_inc(x_t, 1)

                    def shift_columns(c):
                        slot = 2 * c % RING
                        pe.wait_ge(ada_in[slot], 16 * (2 * c // RING + 1))
                        for q in range(CW // P):
                            col = c * (CW // P) + q
                            for k in range(KT):
                                mm = pe.matmul(work[:, SHIFT, col:col + 1], wada[:, slot, k, q * P:(q + 1) * P], cT[:, k:k + 1],
                                               start=(k == 0), stop=(k == KT - 1))
                        mm.then_inc(ada_free[slot], 1)

                    pe.wait_ge(k_in, 16)
                    for n in range(4):
                        transpose_x(n)
                    pe.wait_ge(c_in, 16)
                    shift_columns(0)
                    for n in range(4, NT):
                        transpose_x(n)
                    for c in range(1, CK):
                        shift_columns(c)
                    pe.wait_ge(ada_free[2 * (CK - 1) % RING], 2 * (CK - 1) // RING + 1)
                    pe.sem_inc(ada_cols, 1)
                    summed_columns(pe, SCALE, acc, acc_step).then_inc(ada_cols, 1)
                    pe.wait_ge(w_lo, 1)
                    pe.wait_ge(xT_done, NT)
                    for k in range(KT):
                        pe.wait_ge(hL_pool, k + 1)
                        pe.wait_ge(hL_dve, k + 1)
                        for n in range(2):
                            mm = product3(pe, pair[0][:, n, :], wH[:, 0, k * P:(k + 1) * P], wL[:, 0, k * P:(k + 1) * P],
                                          hH[hs(2 * k + n)], hL[hs(2 * k + n)], k == 0, k == KT - 1)
                    mm.then_inc(w_used, 1)
                    pe.wait_ge(ba_copied, 1)
                    for n in range(NT):
                        tr = pe.transpose(work[:, 0, n * 16:(n + 1) * 16], baT[:, n * P:(n + 1) * P], cst[0:16, IDENT, 0:16])
                    tr.then_inc(ba_t, 1)
                    pe.wait_ge(col_dve, 3)
                    gg = g[:, :, :].rearrange("p h n -> p (h n)")
                    pe.matmul(work[:, 1, 0:64], cst[:, LE, :], gg, start=True, stop=True)
                    pe.matmul(work[:, 1, 64:128], cst[:, GT_, :], gg, start=True, stop=True)
                    pe.matmul(work[:, 1, 128:192], cst[:, ONES, :], gg, start=True, stop=True).then_inc(col_pe, 1)

                @block.vector
                def _(dve):
                    def normalise(n):
                        dve.wait_ge(sq_done, n + 1)
                        dve.tensor_scalar(ss[:, n:n + 1], ss[:, n:n + 1], 1.0 / D, EPS, ALU.mult, ALU.add).then_inc(ms_done, 1)
                        dve.wait_ge(rstd_done, n + 2)
                        dve.tensor_scalar(xr[:, n % 4, :], xr[:, n % 4, :], rstd[:, n:n + 1], None, ALU.mult).then_inc(xn_done, 1)

                    def scale_sum(c):
                        slot, turn = (2 * c + 1) % RING, (2 * c + 1) // RING
                        dve.wait_ge(ada_in[slot], 16 * (turn + 1))
                        ada_sum(dve, wada[:, slot, :, :], acc, c, acc_step)
                        dve.sem_inc(ada_free[slot], 1)
                    for n in range(4):
                        normalise(n)
                    dve.wait_ge(c_in, 16)
                    scale_sum(0)
                    for n in range(4, NT):
                        normalise(n)
                    scale_sum(1)
                    s5_params_dve(dve)
                    scale_sum(2)
                    scale_sum(3)
                    dve.wait_ge(b_in, 16)
                    for m in range(2):
                        dve.wait_ge(ada_cols, m + 1)
                        dve.tensor_tensor(modT[:, m * KT:(m + 1) * KT], work[:, m, 0:KT], bada[:, m * KT:(m + 1) * KT],
                                          ALU.add).then_inc(mod_done, 1)
                    dve.wait_ge(mod_done, 2)
                    dve.tensor_scalar(modT[:, KT:2 * KT], modT[:, KT:2 * KT], 1.0, None, ALU.add).then_inc(mod_done, 1)
                    dve.wait_ge(mod_done, 3)
                    dve.wait_ge(xT_done, NT)
                    for k in range(KT):
                        for u in (2 * k, 2 * k + 1):
                            if u >= 4:
                                dve.wait_ge((hL_pool, hL_dve)[u % 2], u // 2 - 1)
                            dve.tensor_scalar(hf[:, u % 4, :], xT[hs(u)], modT[:, KT + k:KT + k + 1], modT[:, k:k + 1],
                                              ALU.mult, ALU.add).then_inc(hf_done, 1)
                        if k >= 1:
                            h_lo(dve, 2 * k - 1, hL_dve)
                    h_lo(dve, 2 * KT - 1, hL_dve)
                    dve.wait_ge(ba_t, 1)
                    dve.tensor_copy(ba[:, :, :].rearrange("p n c -> p (n c)"), work[:, 0, 0:16 * NT]).then_inc(ba_nat, 1)
                    dve.wait_ge(ba_nat, 1)
                    dve.wait_ge(par_in, 32)
                    dve.tensor_tensor(z[:, :, :], ba[:, :, HEADS:2 * HEADS].rearrange("p n h -> p h n"),
                                      dtb[:, :].unsqueeze(2).to_broadcast([P, HEADS, NT]), ALU.add).then_inc(ba_nat, 1)
                    dve.wait_ge(ba_nat, 2)
                    dve.scalar_tensor_tensor(az[:, :, :].rearrange("p h n -> p (h n)"), z[:, :, :].rearrange("p h n -> p (h n)"), -1.0,
                                             z[:, :, :].rearrange("p h n -> p (h n)"), ALU.mult, ALU.max).then_inc(col_dve, 1)
                    dve.wait_ge(col_act, 4)
                    dve.scalar_tensor_tensor(az[:, :, :].rearrange("p h n -> p (h n)"), z[:, :, :].rearrange("p h n -> p (h n)"), 0.0,
                                             az[:, :, :].rearrange("p h n -> p (h n)"), ALU.max, ALU.add).then_inc(col_dve, 1)
                    dve.wait_ge(col_dve, 2)
                    dve.scalar_tensor_tensor(g[:, :, :], az[:, :, :], -1.0,
                                             ea[:, :].unsqueeze(2).to_broadcast([P, HEADS, NT]), ALU.mult, ALU.mult).then_inc(col_dve, 1)
                    dve.wait_ge(col_dve, 3)
                    dve.tensor_copy(cols[:, :, C_G, :], g[:, :, :]).then_inc(col_dve, 1)
                    dve.tensor_scalar(cols[:, :, C_BETA, :], cols[:, :, C_BETA, :], 1.0, 0.5, ALU.add, ALU.mult).then_inc(col_dve, 1)
                    dve.wait_ge(col_dve, 5)
                    dve.tensor_scalar(cols[:, :, C_HB, :], cols[:, :, C_BETA, :], 0.5, None, ALU.mult).then_inc(col_dve, 1)
                    dve.wait_ge(col_act, 5)
                    for n, c in enumerate((C_EG, C_ES, C_EGL)):
                        dve.tensor_copy(cols[:, :, c, :], ex3[:, n, :].rearrange("p (h n) -> p h n", n=NT)).then_inc(col_dve, 1)
                    dve.wait_ge(col_dve, 9)
                    dve.tensor_tensor(cols[:, :, C_BEG, :], cols[:, :, C_BETA, :], cols[:, :, C_EG, :], ALU.mult).then_inc(col_dve, 1)

        gy = psb("gy", [P, CT, T])
        with ExitStack() as c3:
            s3 = sb_in(c3)
            bbs = s3("bbs", [P, CG, GI])
            pt9 = s3("pt9", [P, CG, STEP + 1, GI])
            mg8 = s3("mg8", [P, CG])
            dsk = s3("dsk", [P, 1])
            rot = s3("rot", [P, 4, CG])
            uT = s3("uT", [P, T])
            un = s3("un", [P, CG, STEP, GI])
            ug = s3("ug", [P, CG, NCH])
            dg = s3("dg", [P, CG, P])
            w1 = s3("w1", [P, CG, P])
            w2 = s3("w2", [P, CG, P])
            p1 = s3("p1", [P, CG, STEP + 1, GI])
            p2 = s3("p2", [P, CG, STEP, GI])
            ctab = s3("ctab", [P, CG, NCH])
            stab = s3("stab", [P, CG, NCH])
            yin = s3("yin", [P, CG, NCH])
            tmp = s3("tmp", [P, CG, NCH])
            t1 = s3("t1", [P, CG, NCH + 1])
            t2 = s3("t2", [P, CG, NCH + 1])
            yT, th = s3("yT", [P, T])[:, :], s3("th3", [P, T])[:, :]
            zs = yin[:, :, :].rearrange("p a b -> p (a b)")
            ksb = w1[0:GI, :, :]
            w_done, w_t, w12_done = sem("s5_w_done"), sem("s5_w_t"), sem("s5_w12_done")
            p_done, tab = sem("s5_p_done"), sem("s5_tab")
            uT_done, u_t, un_done, u_tt, ug_done = (sem(n) for n in ("uT_done", "u_t", "un_done", "u_tt", "ug_done"))
            s_full, state = sem("s_full"), sem("s5_state")
            z_act, z_dve = sem("z_act"), sem("z_dve")
            k_full, k_done, dg_zero = sem("k_full"), sem("k_done"), sem("dg_zero")
            dg_in = sem("dg_in")
            y_full, yn_done, y_t = sem("y_full"), sem("yn_done"), sem("y_t")
            tail_dve, tail_act = sem("tail_dve"), sem("tail_act")
            turn_end = sem("turn_end")
            pz_done, pz_stored = sem("pz_done"), sem("pz_stored")
            NTAB = 7 + 10 * 6
            t_zero = sem("t_zero")
            with nc.Block() as block:
                @block.sync
                def _(sp):
                    sp.sem_inc(pz_stored, 16)
                    with sp.Fori(0, CT) as i:
                        for jr in range(STEP):
                            if jr == 0:
                                sp.wait_ge(dg_zero, i + 1)
                                sp.wait_ge(k_done, i * 2 + 4)
                            sp.dma_start(dg[jr * GI:(jr + 1) * GI, :, (STEP - 1 - jr) * GI:P],
                                         ksb[:, :, 0:(jr + 1) * GI]).then_inc(dg_in, 16)
                        load_w(sp, 4, i, 2)
                        load_w(sp, 5, i, 2)
                        sp.wait_ge(pz_done, i + 1)
                        sp.dma_start(yg_dram[i], zs).then_inc(pz_stored, 16)
                    sp.wait_ge(pz_stored, 16 * CT + 16)

                @block.tensor
                def _(pe):
                    pe.sem_inc(y_full, 1)
                    with pe.Fori(0, CT) as i:
                        pe.wait_ge(w_lo, i * 2 + 2)
                        pe.wait_ge(yn_done, i * 2 + 2)
                        for n in range(2):
                            for k in range(KT):
                                mm = product3(pe, pair[0][:, n, :], wH[:, 1, k * P:(k + 1) * P], wL[:, 1, k * P:(k + 1) * P],
                                              hH[:, k, n * HALF:(n + 1) * HALF], hL[:, k, n * HALF:(n + 1) * HALF], k == 0, k == KT - 1)
                        mm.then_inc(w_used, 1)
                        pe.wait_ge(w_done, i * 3 + 3)
                        pe.wait_ge(z_dve, i + 1)
                        for gr in range(CG):
                            tr = pe.transpose(work[:, gr // 4, gr % 4 * P:(gr % 4 + 1) * P], dg[:, gr, :], ident)
                        tr.then_inc(w_t, 1)
                        pe.wait_ge(uT_done, i + 1)
                        pe.wait_ge(k_done, i * 2 + 2)
                        for jr in range(STEP):
                            tr = pe.transpose(work[:, 2 + jr // 4, jr % 4 * P:(jr % 4 + 1) * P],
                                              uT[:, STEP - 1 - jr::STEP], ident)
                        tr.then_inc(u_t, 1)
                        pe.wait_ge(un_done, i * 2 + 2)
                        pe.wait_ge(w12_done, i * 6 + 6)
                        for gr in range(CG):
                            tr = pe.transpose(work[:, gr // 4, gr % 4 * P:(gr % 4 + 1) * P],
                                              un[:, gr, :, :].rearrange("p j i -> p (j i)"), ident)
                        tr.then_inc(u_tt, 1)
                        pe.wait_ge(p_done, i * 7 + 7)
                        for gr in range(CG):
                            mm = pe.matmul(work[0:GI, 2 + gr // 4, gr % 4 * P:(gr % 4 + 1) * P], bbs[:, gr, :],
                                           p1[:, gr, 0:STEP, :].rearrange("p k i -> p (k i)"), start=True, stop=True)
                        mm.then_inc(k_full, 1)
                        pe.wait_ge(ug_done, i * 2 + 2)
                        pe.wait_ge(tail_dve, i * 4 + 2)
                        for gr in range(CG):
                            pe.matmul(pair[1][:, gr // 4, gr % 4 * P:(gr % 4 + 1) * P], w1[:, gr, :], ug[:, gr, :], start=True, stop=True)
                            mm = pe.matmul(pair[0][:, gr // 4, gr % 4 * P:(gr % 4 + 1) * P], w2[:, gr, :], ug[:, gr, :], start=True, stop=True)
                        mm.then_inc(s_full, 1)
                        pe.wait_ge(w_lo, i * 2 + 3)
                        for n in range(2):
                            for k in range(KT):
                                mm = product3(pe, work[:, n, :], wH[:, 0, k * P:(k + 1) * P], wL[:, 0, k * P:(k + 1) * P],
                                              hH[:, k, n * HALF:(n + 1) * HALF], hL[:, k, n * HALF:(n + 1) * HALF], k == 0, k == KT - 1)
                        mm.then_inc(w_used, 1)
                        pe.wait_ge(dg_in, i * (16 * STEP) + 16 * STEP)
                        pe.wait_ge(state, i * 13 + 13)
                        for gr in range(CG):
                            dst = pair[0][:, gr // 4, gr % 4 * P:(gr % 4 + 1) * P]
                            pe.matmul(dst, ug[:, gr, :], dg[:, gr, :], start=True, stop=False)
                            pe.matmul(dst, t1[:, gr, 0:NCH], p1[:, gr, 1:STEP + 1, :].rearrange("p k i -> p (k i)"), start=False, stop=False)
                            mm = pe.matmul(dst, t2[:, gr, 0:NCH], p2[:, gr, :, :].rearrange("p k i -> p (k i)"), start=False, stop=True)
                        mm.then_inc(y_full, 1)
                        pe.wait_ge(yn_done, i * 2 + 4)
                        yn = un[:, :, :, :].rearrange("p g j i -> p (g j i)").rearrange("p (j c) -> p j c", j=STEP)
                        for j in range(STEP):
                            tr = pe.transpose(pair[1][:, j // 4, j % 4 * P:(j % 4 + 1) * P], yn[:, j, :], ident)
                        tr.then_inc(y_t, 1)

                @block.scalar
                def _(act):
                    act.sem_inc(yn_done, 2)
                    act.sem_inc(k_done, 2)

                    def copy_u(i, it):
                        act.wait_ge(w_used, i * 2 + (2 * it + 2))
                        act.wait_ge(tail_dve, i * 4 + (2 * it + 2))
                        act.activation(uT[:, :], pair[0][:, :, :].rearrange("p a b -> p (a b)"), ACT.Copy).then_inc(uT_done, 1)

                    def turn(i, last):
                        act.wait_ge(w_t, i + 1)
                        for n in range(2):
                            src = work[:, n, :].rearrange("p (g s) -> p g s", g=4)
                            act.activation(w1[:, 4 * n:4 * n + 4, :], src, ACT.Copy).then_inc(w12_done, 1)
                        for n in range(2):
                            src = work[:, n, :].rearrange("p (g s) -> p g s", g=4)
                            act.activation(w2[:, 4 * n:4 * n + 4, 0:PS], src[:, :, PS:P], ACT.Copy).then_inc(w12_done, 1)
                            act.activation(w2[:, 4 * n:4 * n + 4, PS:P], src[:, :, 0:PS], ACT.Copy, scale=-1.0).then_inc(w12_done, 1)
                        act.wait_ge(u_t, i + 1)
                        act.wait_ge(y_t, i + 1)
                        for n in range(2):
                            act.activation(un[:, :, 4 * n:4 * n + 4, :], work[:, 2 + n, :].rearrange("p (j g i) -> p g j i", j=4, g=CG),
                                           ACT.Copy).then_inc(un_done, 1)
                        act.wait_ge(u_tt, i + 1)
                        for n in range(2):
                            act.activation(ug[:, 4 * n:4 * n + 4, :], work[:, n, :].rearrange("p (g c) -> p g c", g=4), ACT.Copy).then_inc(ug_done, 1)
                        act.wait_ge(k_full, i + 1)
                        act.wait_ge(s_full, i + 1)
                        for n in range(2):
                            act.activation(ksb[:, 4 * n:4 * n + 4, :], work[0:GI, 2 + n, :].rearrange("p (g c) -> p g c", g=4), ACT.Copy).then_inc(k_done, 1)
                        split_hi(act, 3, i, 2)
                        act.wait_ge(w_used, i * 2 + 3)
                        split_hi(act, 4, i, 2)
                        act.activation(th, work[:, 0:2, :].rearrange("p a b -> p (a b)"), ACT.Tanh, scale=0.5).then_inc(z_act, 1)
                        act.wait_ge(y_full, i + 2)
                        for n in range(2):
                            act.activation(un[:, :, :, :].rearrange("p g j i -> p (g j i)").rearrange("p (j g i) -> p g j i", j=STEP, g=CG)[:, 4 * n:4 * n + 4, :, :],
                                           pair[0][:, n, :].rearrange("p (g j i) -> p g j i", g=4, j=STEP), ACT.Copy).then_inc(yn_done, 1)
                        act.wait_ge(tail_dve, i * 4 + 4)
                        act.activation(th, yT, ACT.Square).then_inc(tail_act, 1)
                        if not last:
                            copy_u(i, 1)
                        act.wait_ge(tail_dve, i * 4 + 6)
                        act.activation(th, th, ACT.Tanh, scale=0.7978845608028654).then_inc(tail_act, 1)
                    copy_u(0, 0)
                    with act.Fori(0, CT - 1) as i:
                        turn(i, False)
                    turn(CT - 1, True)

                @block.gpsimd
                def _(pool):
                    with pool.Fori(0, CT) as i:
                        pool.wait_ge(y_full, i + 1)
                        g8 = bass.ds(i * CG, CG)
                        cre = s5c[:, 0, g8, :].unsqueeze(2)
                        cim = s5c[:, 1, g8, :].unsqueeze(2)
                        A = lambda t, k0, k1: t[:, k0:k1, g8].rearrange("p k g -> p g k").unsqueeze(3).to_broadcast([P, CG, k1 - k0, GI])
                        C = lambda t, n: t.to_broadcast([P, CG, n, GI])
                        t9 = pt9[:, :, :, :]
                        t8 = pt9[:, :, 0:STEP, :]
                        m = [0]

                        def step(ins):
                            m[0] += 1
                            ins.then_inc(p_done, 1)
                            pool.wait_ge(p_done, i * 7 + m[0])
                        step(pool.tensor_tensor(p1[:, :, :, :], C(cre, STEP + 1), A(ca, 0, STEP + 1), ALU.mult))
                        step(pool.tensor_tensor(t9, C(cim, STEP + 1), A(cb, 0, STEP + 1), ALU.mult))
                        step(pool.tensor_tensor(p1[:, :, :, :], p1[:, :, :, :], t9, ALU.add))
                        step(pool.tensor_tensor(p2[:, :, :, :], C(cre, STEP), A(cb, 1, STEP + 1), ALU.mult))
                        step(pool.tensor_tensor(t8, C(cim, STEP), A(ca, 1, STEP + 1), ALU.mult))
                        step(pool.tensor_tensor(p2[:, :, :, :], p2[:, :, :, :], t8, ALU.subtract))
                        step(pool.tensor_copy(bbs[:, :, :], bbst[:, g8, :]))
                        split_lo(pool, 3, i, 2)
                        split_lo(pool, 4, i, 2)

                @block.vector
                def _(dve):
                    tt = dve.tensor_tensor
                    dve.memset(t1[:, :, 0:1], 0.0).then_inc(t_zero, 1)
                    dve.memset(t2[:, :, 0:1], 0.0).then_inc(t_zero, 1)
                    dve.wait_ge(t_zero, 2)
                    v4 = lambda t: t[:, :, :].rearrange("p g (k i) -> p g k i", i=GI)

                    def powers(i, j):
                        g8 = bass.ds(j * CG, CG)
                        B = lambda c: s5b[:, c, g8, :].unsqueeze(2).to_broadcast([P, CG, STEP, GI])
                        A = lambda t: t[:, :, g8].rearrange("p k g -> p g k").unsqueeze(3).to_broadcast([P, CG, STEP, GI])
                        tt(v4(dg), B(0), A(ua), ALU.mult).then_inc(w_done, 1)
                        tt(v4(tmp), B(1), A(va), ALU.mult).then_inc(w_done, 1)
                        dve.wait_ge(w_done, i * 3 + 2)
                        tt(v4(dg), v4(dg), v4(tmp), ALU.add).then_inc(w_done, 1)
                        dve.wait_ge(w_done, i * 3 + 3)

                    def tables(i, late):
                        g8 = bass.ds(i * CG, CG)
                        m = [NTAB - 20 if late else 0]

                        def step(ins):
                            m[0] += 1
                            ins.then_inc(tab, 1)
                            dve.wait_ge(tab, i * NTAB + m[0])
                        if not late:
                            step(dve.memset(ctab[:, :, 0:1], 1.0))
                            step(dve.memset(stab[:, :, 0:1], 0.0))
                            step(dve.tensor_copy(rot[:, 0, :], q[:, CC, g8]))
                            step(dve.tensor_copy(rot[:, 1, :], q[:, SN, g8]))
                            step(dve.tensor_copy(ctab[:, :, 1:2], rot[:, 0, :].unsqueeze(2)))
                            step(dve.tensor_copy(stab[:, :, 1:2], rot[:, 1, :].unsqueeze(2)))
                            step(dve.tensor_copy(mg8[:, :], q[:, MG8, g8]))
                        k = 32 if late else 2
                        while k < (NCH if late else 32):
                            step(tt(rot[:, 2, :], rot[:, 0, :], rot[:, 0, :], ALU.mult))
                            step(tt(rot[:, 3, :], rot[:, 1, :], rot[:, 1, :], ALU.mult))
                            step(dve.scalar_tensor_tensor(rot[:, 1, :], rot[:, 0, :], 2.0, rot[:, 1, :], ALU.mult, ALU.mult))
                            step(tt(rot[:, 0, :], rot[:, 2, :], rot[:, 3, :], ALU.subtract))
                            cr = rot[:, 0, :].unsqueeze(2).to_broadcast([P, CG, k])
                            sr = rot[:, 1, :].unsqueeze(2).to_broadcast([P, CG, k])
                            x0, x1 = (t1[:, :, 1:k + 1], t2[:, :, 1:k + 1]) if late else (tmp[:, :, 0:k], yin[:, :, 0:k])
                            step(tt(x0, ctab[:, :, 0:k], cr, ALU.mult))
                            step(tt(x1, stab[:, :, 0:k], sr, ALU.mult))
                            step(tt(ctab[:, :, k:2 * k], x0, x1, ALU.subtract))
                            step(tt(x0, ctab[:, :, 0:k], sr, ALU.mult))
                            step(tt(x1, stab[:, :, 0:k], cr, ALU.mult))
                            step(tt(stab[:, :, k:2 * k], x0, x1, ALU.add))
                            k *= 2
                        assert m[0] == (NTAB if late else NTAB - 20), m[0]

                    def turn(i, last):
                        dve.wait_ge(w_t, i + 1)
                        dve.memset(dg[:, :, :], 0.0).then_inc(dg_zero, 1)
                        dve.wait_ge(s_full, i + 1)
                        m8 = lambda pp: pp[:, :, :].rearrange("p a (g c) -> p (a g) c", g=4)
                        dve.wait_ge(pz_stored, i * 16 + 16)
                        tt(yin[:, :, :], m8(pair[1]), ctab[:, :, :], ALU.mult).then_inc(state, 1)
                        tt(tmp[:, :, :], m8(pair[0]), stab[:, :, :], ALU.mult).then_inc(state, 1)
                        dve.wait_ge(state, i * 13 + 2)
                        tt(yin[:, :, :], yin[:, :, :], tmp[:, :, :], ALU.add).then_inc(state, 1)
                        dve.wait_ge(state, i * 13 + 3)
                        for gr in range(CG):
                            dve.tensor_tensor_scan(tmp[:, gr, :], mg8[:, gr:gr + 1].to_broadcast([P, NCH]), yin[:, gr, :], 0.0,
                                                   ALU.mult, ALU.add).then_inc(state, 1)
                        dve.wait_ge(state, i * 13 + 11)
                        tt(t1[:, :, 1:NCH + 1], tmp[:, :, :], ctab[:, :, :], ALU.mult).then_inc(state, 1)
                        tt(t2[:, :, 1:NCH + 1], tmp[:, :, :], stab[:, :, :], ALU.mult).then_inc(state, 1)
                        dve.tensor_copy(dsk[:, :], s5d[:, bass.ds(i, 1)]).then_inc(t_zero, 1)
                        dve.wait_ge(state, i * 13 + 13)
                        if not last:
                            tables(i + 1, False)
                        dve.wait_ge(z_act, i + 1)
                        dve.scalar_tensor_tensor(zs, th, 1.0, work[:, 0:2, :].rearrange("p a b -> p (a b)"), ALU.add, ALU.mult).then_inc(z_dve, 1)
                        if not last:
                            dve.wait_ge(y_full, i + 2)
                            powers(i + 1, i + 1)
                        dve.wait_ge(y_t, i + 2)
                        dve.wait_ge(t_zero, i + 3)
                        jc = lambda t, b: t.rearrange("p (c j) -> p j c", j=STEP)[:, 4 * b:4 * b + 4, :]
                        for b in range(2):
                            dve.scalar_tensor_tensor(jc(yT, b), jc(uT[:, :], b), dsk[:, 0:1],
                                                     pair[1][:, b, :].rearrange("p (j c) -> p j c", j=4), ALU.mult, ALU.add).then_inc(tail_dve, 1)
                        dve.wait_ge(tail_act, i * 2 + 1)
                        tt(th, th, yT, ALU.mult).then_inc(tail_dve, 1)
                        dve.wait_ge(tail_dve, i * 4 + 5)
                        dve.scalar_tensor_tensor(th, th, 0.044715, yT, ALU.mult, ALU.add).then_inc(tail_dve, 1)
                        dve.wait_ge(tail_act, i * 2 + 2)
                        dve.scalar_tensor_tensor(gy[:, i, :], th, 1.0, yT, ALU.add, ALU.mult).then_inc(turn_end, 1)
                        dve.wait_ge(turn_end, i + 1)
                        tt(zs, zs, gy[:, i, :], ALU.mult).then_inc(pz_done, 1)
                        if not last:
                            tables(i + 1, True)
                    dve.sem_inc(tail_dve, 2)
                    dve.sem_inc(z_dve, 1)
                    dve.sem_inc(y_t, 1)
                    powers(0, 0)
                    tables(0, False)
                    tables(0, True)
                    with dve.Fori(0, CT - 1) as i:
                        turn(i, False)
                    turn(CT - 1, True)

        with ExitStack() as c4:
            s4 = sb_in(c4)
            pz = s4("pz", [P, CT, T])
            gH = s4("gH", [P, CT, T], F32R)
            gL = s4("gL", [P, CT, T], F32R)
            tg = s4("tg", [P, 2, T])
            glub = s4("glub", [P, CT])
            wgate = s4("wgate", [P, 2, KT, CW])
            gacc = s4("gacc", [P, D])
            wg_in, wg_free = [sem("wg_in0"), sem("wg_in1")], sem("wg_free")
            gacc_step, gate_cols, gate_made = sem("gacc_step"), sem("gate_cols"), sem("gate_made")
            pz_in, gb_in, gH_done, gL_pool, gL_dve, hb_done = (sem(n) for n in ("pz_in", "gb_in", "gH_done", "gL_pool", "gL_dve", "hb_done"))
            glu_full, glu_act, yg_done, yg_stored = sem("glu_full"), sem("glu_act"), sem("yg_done"), sem("yg_stored")

            def glu_lo(eng, m, done):
                eng.wait_ge(gH_done, m + 1)
                eng.tensor_tensor(gL[:, m, :], gy[:, m, :], gH[:, m, :].bitcast(F32), ALU.subtract).then_inc(done, 1)

            with nc.Block() as block:
                @block.sync
                def _(sp):
                    sp.dma_start(glub[:, :], a["glub"]).then_inc(gb_in, 16)
                    sp.dma_start(pz[:, :, :], yg_dram.rearrange("m p t -> p m t")).then_inc(pz_in, 16)
                    load_w(sp, 12)
                    for c in range(CK):
                        if c >= 2:
                            sp.wait_ge(wg_free, c - 1)
                        sp.dma_start(wgate[:, c % 2, :, :], a["wada"][GATE][:, :, c * CW:(c + 1) * CW]).then_inc(wg_in[c % 2], 16)
                    for m in range(CT):
                        sp.wait_ge(yg_done, m + 1)
                        sp.dma_start(yg_dram[m], pz[:, m, :]).then_inc(yg_stored, 16)
                    load_w(sp, 13)
                    sp.wait_ge(yg_stored, 16 * CT)

                @block.gpsimd
                def _(pool):
                    for m in range(0, CT, 2):
                        glu_lo(pool, m, gL_pool)
                    split_lo(pool, 11)
                    split_lo(pool, 12)

                @block.tensor
                def _(pe):
                    for m in range(CT):
                        if m % 2 == 0:
                            pe.wait_ge(w_lo, 10 + m // 2)
                        if m >= 2:
                            pe.wait_ge(glu_act, m - 1)
                        sl = (TILE_GLU + m // 2) % 2
                        for n in range(2):
                            for k in range(CT):
                                if m == 0 and n == 0:
                                    pe.wait_ge((gL_pool, gL_dve)[k % 2], k // 2 + 1)
                                o = (m % 2) * HALF + k * P
                                mm = product3(pe, pair[m % 2][:, n, :], wH[:, sl, o:o + P], wL[:, sl, o:o + P],
                                              gH[:, k, n * HALF:(n + 1) * HALF], gL[:, k, n * HALF:(n + 1) * HALF], k == 0, k == CT - 1)
                        mm.then_inc(glu_full, 1)
                        if m % 2:
                            pe.wait_ge(glu_full, m + 1)
                            pe.sem_inc(w_used, 1)
                    summed_columns(pe, GATE, gacc, gacc_step).then_inc(gate_cols, 1)

                @block.scalar
                def _(act):
                    for m in range(CT):
                        act.activation(gH[:, m, :], gy[:, m, :], ACT.Copy).then_inc(gH_done, 1)
                    act.wait_ge(hb_done, 1)
                    for m in range(CT):
                        act.wait_ge(glu_full, m + 1)
                        if m >= 2:
                            act.wait_ge(yg_done, m - 1)
                        act.activation(tg[:, m % 2, :], pair[m % 2][:, :, :].rearrange("p a b -> p (a b)"), ACT.Tanh,
                                       scale=0.25, bias=glub[:, m:m + 1]).then_inc(glu_act, 1)
                        if m % 2:
                            split_hi(act, 11 + m // 2)

                @block.vector
                def _(dve):
                    dve.wait_ge(gb_in, 16)
                    dve.tensor_scalar(glub[:, :], glub[:, :], 0.5, None, ALU.mult).then_inc(hb_done, 1)
                    for m in range(1, CT, 2):
                        glu_lo(dve, m, gL_dve)
                    for m in range(CT):
                        dve.wait_ge(wg_in[m % 2], 16 * (m // 2 + 1))
                        ada_sum(dve, wgate[:, m % 2, :, :], gacc, m, gacc_step)
                        dve.sem_inc(wg_free, 1)
                        if m == 0:
                            dve.wait_ge(pz_in, 16)
                        dve.wait_ge(glu_act, m + 1)
                        dve.scalar_tensor_tensor(pz[:, m, :], tg[:, m % 2, :], 1.0, pz[:, m, :], ALU.add, ALU.mult).then_inc(yg_done, 1)
                    dve.wait_ge(gate_cols, 1)
                    dve.tensor_tensor(modT[:, 2 * KT:3 * KT], work[:, GATE, 0:KT], bada[:, 2 * KT:3 * KT], ALU.add).then_inc(gate_made, 1)
        gstack.close()

        with ExitStack() as c5:
            s5 = sb_in(c5)
            qc, kc, vc = s5("qc", [P, T]), s5("kc", [P, T]), s5("vc", [P, T])
            zs = s5("zs5", [P, T])
            cin = s5("cin", [P, CONV_K - 1 + T])
            acc = s5("acc", [P, T])
            th = s5("th5", [P, T])
            cw_all = s5("cw_all", [P, HEADS, 3 * CONV_K])
            cw = s5("cw", [P, 3 * CONV_K])
            nw = s5("nw", [P, 1])
            col = s5("col", [P, NCOL, NT])
            ssq = s5("ssq", [P, NQ, 3, GT])
            rsq = s5("rsq", [P, NQ, 3, GT])
            cqd = s5("cqd", [P, NQ, GT])
            mh = s5("mh", [P, 2 * GT])
            st = s5("state", [P, P])
            vnew = s5("vnew", [P, P])
            names = ("vb", "kh", "kbg", "kd", "khT", "qd", "qdT", "dec", "decA", "decS", "mm_", "attnT", "mb", "X", "Y", "R", "wT")
            B = {n: s5("d_" + n, [P, NT, P]) for n in names}
            B["qn"], B["kn"], B["rg"], B["attn"], B["on"], B["onx"], B["oz"] = B["X"], B["Y"], B["R"], B["mb"], B["dec"], B["decA"], B["decS"]
            SQ = [B["wT"], B["mb"]]
            tiles4 = lambda n, g: B[n][:, GT * g:GT * g + GT, :]
            flat = lambda n, g: tiles4(n, g).rearrange("p n d -> p (n d)")
            bank4 = lambda b: work[:, b, :].rearrange("p (n d) -> p n d", n=GT)
            rows = lambda c, g: col[:, c, GT * g:GT * g + GT].unsqueeze(2).to_broadcast([P, GT, P])
            mat4 = lambda m: cst[:, m:m + 1, :].to_broadcast([P, GT, P])

            order = ["nq0", "nk0", "nv0", "nq1", "nk1", "nv1", "D0", "D1", "kh0", "qd0", "kh1", "qd1", "kk0", "qk0", "kk1", "qk1",
                     "at0", "m10", "at1", "m11"]
            NL = len(LEVELS)
            for l in range(1, NL):
                order += [f"R0_{l}", f"R1_{l}"]
                order += [f"X0_{l}", f"Y0_{l}", f"X1_{l}", f"Y1_{l}"] if l < NL - 1 else [f"Y0_{l}", f"Y1_{l}"]
            order += ["w0", "w1"]
            banks = [(n, i % 4) for i, n in enumerate(order)]
            for n in range(NT):
                banks += [(f"vn{n}", 0), (f"s{n}", 1)]
            banks += [("o0", 2), ("o1", 3), ("on0", 0), ("on1", 1)]
            per_bank = [sum(b == k for _, b in banks) for k in range(4)]
            use = {n: (b, sum(bb == b for _, bb in banks[:i])) for i, (n, b) in enumerate(banks)}
            per_out = [per_bank[k] - (NT if k == 1 else 0) for k in range(4)]
            use_out = {n: (b, sum(bb == b and m[0] != "s" for m, bb in banks[:i])) for i, (n, b) in enumerate(banks)}
            full = [sem(f"bank_full{b}") for b in range(4)]
            evicted = [sem(f"bank_evicted{b}") for b in range(4)]
            R_ = {n: sem("r_" + n) for n in ("rg", "sqq", "sqk", "ssq", "rr", "kh", "qd", "kbg", "kd", "decI", "decS", "decB", "decA", "cq", "X1",
                                              "sqo", "sso", "ro", "onx", "oz")}
            mb_done, mh_ready = sem("mb_done"), sem("mh_ready")
            col_ready, s_ready, conv_ready, zs_ready = sem("col_ready"), sem("s_ready"), sem("conv_ready"), sem("zs_ready")
            cin_ready, th_ready, conv_step = sem("cin_ready"), sem("th_ready"), sem("conv_step")
            conv_in, const_ready, nw_ready, oz_stored = sem("conv_in"), sem("const_ready"), sem("nw_ready"), sem("oz_stored")

            class Turn:

                def __init__(self, eng, i):
                    self.eng, self.i = eng, i

                def need(self, name, g):
                    self.eng.wait_ge(R_[name], self.i * NQ + (g + 1))

                def fill(self, name):
                    b, n = use_out[name]
                    self.eng.wait_ge(evicted[b], self.i * per_out[b] + (n + 1))
                    return work[:, b, :]

                def filled(self, name):
                    b, n = use[name]
                    self.eng.wait_ge(full[b], self.i * per_bank[b] + (n + 1))
                    return work[:, b, :]

                def out(self, name):
                    b, n = use_out[name]
                    self.eng.wait_ge(evicted[b], self.i * per_out[b] + (n + 2))

            def full_of(name):
                return full[use[name][0]]

            def evicted_of(name):
                return evicted[use[name][0]]

            def proj_units(pe, base, it, u0, u1):
                for u in range(u0, u1):
                    s, n, k = u // 16, u // 8 % 2, u % 8
                    t = base + s
                    if u % 16 == 0:
                        pe.wait_ge(w_lo, it * 4 + (t + 1))
                        if s == 1:
                            pe.wait_ge(zs_ready, it + 1)
                        else:
                            pe.wait_ge(cin_ready, it * 3 + (3, 0, 4, 5)[s])
                    mm = product3(pe, pair[s % 2][:, n, :], wH[:, t % 2, k * P:(k + 1) * P], wL[:, t % 2, k * P:(k + 1) * P],
                                  hH[:, k, n * HALF:(n + 1) * HALF], hL[:, k, n * HALF:(n + 1) * HALF], k == 0, k == KT - 1)
                    if u % 16 == 15:
                        mm.then_inc(w_used, 1)

            def act_copy(act, base, it, s):
                act.wait_ge(w_used, it * 4 + (base + s + 1))
                act.wait_ge(conv_step, it * 12 + (4 * s + 13))
                act.activation(cin[:, CONV_K - 1:], pair[s % 2][:, :, :].rearrange("p a b -> p (a b)"), ACT.Copy).then_inc(cin_ready, 1)

            def act_tanh(act, it, s):
                act.wait_ge(conv_step, it * 12 + (4 * s + 17))
                if s == 0:
                    act.wait_ge(zs_ready, it + 1)
                else:
                    act.wait_ge(conv_ready, it * 3 + (3 + s))
                act.activation(th[:, :], acc[:, :], ACT.Tanh, scale=0.5).then_inc(th_ready, 1)

            def dve_conv(dve, it, s, tap):
                if tap == 0:
                    dve.wait_ge(cin_ready, it * 3 + (s + 4))
                    dve.wait_ge(conv_ready, it * 3 + (3 + s))
                    dve.tensor_scalar(acc[:, :], cin[:, 0:T], cw[:, CONV_K * s:CONV_K * s + 1], None, ALU.mult).then_inc(conv_step, 1)
                else:
                    dve.wait_ge(conv_step, it * 12 + (4 * s + tap + 13))
                    dve.scalar_tensor_tensor(acc[:, :], cin[:, tap:tap + T], cw[:, CONV_K * s + tap:CONV_K * s + tap + 1], acc[:, :],
                                             ALU.mult, ALU.add).then_inc(conv_step, 1)

            def dve_silu(dve, it, s):
                dve.wait_ge(th_ready, it * 4 + (s + 5))
                dve.scalar_tensor_tensor((qc, kc, vc)[s][:, :], th[:, :], 1.0, acc[:, :], ALU.add, ALU.mult).then_inc(conv_ready, 1)

            def act_z(act, base, it):
                act.wait_ge(w_used, it * 4 + (base + 4))
                act.wait_ge(conv_ready, it * 3 + 6)
                act.activation(th[:, :], pair[1][:, :, :].rearrange("p a b -> p (a b)"), ACT.Tanh, scale=0.5).then_inc(th_ready, 1)

            def dve_z(dve, it):
                dve.wait_ge(th_ready, it * 4 + 8)
                dve.scalar_tensor_tensor(zs[:, :], th[:, :], 1.0, pair[1][:, :, :].rearrange("p a b -> p (a b)"), ALU.add,
                                         ALU.mult).then_inc(zs_ready, 1)

            def dve_cw(dve, head):
                dve.tensor_copy(cw[:, :], cw_all[:, head, :]).then_inc(const_ready, 1)

            def pe_turn(pe, i):
                t = Turn(pe, i)
                base = TILE_HEAD + 4

                def units(u0, u1):
                    proj_units(pe, base, i, u0, u1)

                def trans(name, src, g):
                    bank = t.fill(name)
                    for n in range(GT):
                        tr = pe.transpose(bank[:, n * P:(n + 1) * P], src(GT * g + n), ident)
                    tr.then_inc(full_of(name), 1)

                def prod(name, lhs, rhs, g):
                    bank = t.fill(name)
                    for n in range(GT):
                        mm = pe.matmul(bank[:, n * P:(n + 1) * P], lhs(GT * g + n), rhs(GT * g + n), start=True, stop=True)
                    mm.then_inc(full_of(name), 1)
                ch = lambda tile: (lambda n: tile[:, n * P:(n + 1) * P])
                bf = lambda name: (lambda n: B[name][:, n, :])
                pe.wait_ge(conv_ready, i * 3 + 3)
                for g in range(NQ):
                    trans(f"nq{g}", ch(qc), g)
                    trans(f"nk{g}", ch(kc), g)
                    trans(f"nv{g}", ch(vc), g)
                    units(4 * g, 4 * g + 4)
                for g in range(NQ):
                    t.need("rg", g)
                    bank = t.fill(f"D{g}")
                    pe.matmul(bank, cst[:, LE, :], flat("rg", g), start=True, stop=True).then_inc(full_of(f"D{g}"), 1)
                    units(8 + 4 * g, 12 + 4 * g)
                for g in range(NQ):
                    t.need("kh", g)
                    trans(f"kh{g}", bf("kh"), g)
                    t.need("qd", g)
                    trans(f"qd{g}", bf("qd"), g)
                    units(16 + 4 * g, 20 + 4 * g)
                for g in range(NQ):
                    t.out(f"kh{g}")
                    prod(f"kk{g}", bf("khT"), bf("khT"), g)
                    prod(f"qk{g}", ch(qc), bf("khT"), g)
                    units(24 + 2 * g, 26 + 2 * g)
                for g in range(NQ):
                    t.out(f"qk{g}")
                    trans(f"at{g}", bf("attn"), g)
                    pe.wait_ge(mb_done, i * (NQ * NL) + (g + 1))
                    trans(f"m1{g}", bf("mb"), g)
                    units(28 + 2 * g, 30 + 2 * g)
                for l in range(1, NL):
                    for g in range(NQ):
                        t.out(f"m1{g}" if l == 1 else f"Y{g}_{l - 1}")
                        pe.wait_ge(mb_done, i * (NQ * NL) + (NQ * l + g + 1))
                        prod(f"R{g}_{l}", bf("mb"), bf("Y"), g)
                    units(30 + 2 * l, 31 + 2 * l)
                    for g in range(NQ):
                        t.out(f"R{g}_{l}")
                        if l > 1:
                            t.out(f"X{g}_{l - 1}")
                        else:
                            t.need("X1", g)
                        if l < NL - 1:
                            prod(f"X{g}_{l}", bf("R"), bf("X"), g)
                        prod(f"Y{g}_{l}", bf("X"), bf("R"), g)
                    units(31 + 2 * l, 32 + 2 * l)
                for g in range(NQ):
                    t.need("kbg", g)
                    t.out(f"Y{g}_{NL - 1}")
                    prod(f"w{g}", bf("kbg"), bf("Y"), g)
                    units(44 + g, 45 + g)
                t.need("kd", 1)
                t.out("w1")
                t.out("at1")
                t.out("qd1")
                t.out("nv1")
                for n in range(NT):
                    g = n // GT
                    bank = t.fill(f"vn{n}")[:, 0:P]
                    pe.wait_ge(s_ready, i * (NT + 1) + (n + 1))
                    pe.matmul(bank, B["Y"][:, n, :], B["vb"][:, n, :], start=True, stop=False)
                    pe.matmul(bank, B["wT"][:, n, :], st[:, :], start=False, stop=True).then_inc(full_of(f"vn{n}"), 1)
                    units(46 + 2 * n, 47 + 2 * n)
                    if n % GT == 0:
                        obank = t.fill(f"o{g}")
                    o = obank[:, n % GT * P:(n % GT + 1) * P]
                    pe.matmul(o, B["qdT"][:, n, :], st[:, :], start=True, stop=False)
                    sbank = t.fill(f"s{n}")[:, 0:P]
                    t.out(f"vn{n}")
                    pe.matmul(sbank, B["kd"][:, n, :], vnew[:, :], start=True, stop=True).then_inc(full_of(f"s{n}"), 1)
                    mm = pe.matmul(o, B["attnT"][:, n, :], vnew[:, :], start=False, stop=True)
                    if n % GT == GT - 1:
                        mm.then_inc(full_of(f"o{g}"), 1)
                    units(47 + 2 * n, 48 + 2 * n)
                units(62, 64)
                pe.wait_ge(s_ready, i * (NT + 1) + (NT + 1))
                for g in range(NQ):
                    t.need("onx", g)
                    trans(f"on{g}", bf("onx"), g)

            early = [acc[:, :], th[:, :], cin[:, CONV_K - 1:], qc[:, :]]

            def act_turn(act, i, proj):
                t = Turn(act, i)
                base = TILE_HEAD + 4

                def copy(name, dst, g, scale=1.0):
                    act.activation(flat(dst, g), t.filled(name), ACT.Copy, scale=scale).then_inc(evicted_of(name), 1)

                def early_gate(s):
                    if s == 0:
                        act.wait_ge(conv_ready, 3 * HEADS)
                        act.wait_ge(zs_ready, HEADS)
                    if s == 3:
                        t.filled("qk1")
                    act.wait_ge(w_used, TILE_MERGE + s + 1)
                    act.activation(early[s], pair[s % 2][:, :, :].rearrange("p a b -> p (a b)"), ACT.Tanh, scale=0.5).then_inc(cin_ready, 1)

                def checkpoint(s):
                    if not proj:
                        act.wait_ge(w_used, TILE_MERGE + s + 1)
                        split_hi(act, TILE_MERGE + s + 2)
                        early_gate(s)
                    else:
                        split_hi(act, base + s + 2, i, 4)
                        if s < 3:
                            act_copy(act, base, i, s)
                copy("nq0", "qn", 0)
                copy("nq1", "qn", 1)
                for g in range(NQ):
                    act.activation(flat("dec", g), t.filled(f"D{g}"), ACT.Exp).then_inc(evicted_of(f"D{g}"), 1)
                copy("kh0", "khT", 0)
                checkpoint(0)
                copy("kh1", "khT", 1)
                for g in range(NQ):
                    copy(f"at{g}", "attnT", g)
                if proj:
                    act_tanh(act, i, 0)
                for l in range(1, NL):
                    for g in range(NQ):
                        copy(f"R{g}_{l}", "R", g)
                    if l == 1:
                        checkpoint(1)
                    if l == NL - 2 and proj:
                        act_tanh(act, i, 1)
                for g in range(NQ):
                    copy(f"w{g}", "wT", g, -1.0)
                for n in range(NT):
                    act.activation(vnew[:, :], t.filled(f"vn{n}")[:, 0:P], ACT.Copy).then_inc(evicted_of(f"vn{n}"), 1)
                    if n == 1:
                        checkpoint(2)
                    if n == GT:
                        copy("o0", "on", 0)
                    if n == NT - 1 and proj:
                        act_tanh(act, i, 2)
                copy("o1", "on", 1)
                checkpoint(3)
                if proj:
                    act_z(act, base, i)

            def dve_turn(dve, i, proj):
                t = Turn(dve, i)
                tt = dve.tensor_tensor

                def conv(s, tap):
                    if proj:
                        dve_conv(dve, i, s, tap)
                dve.tensor_copy(col[:, :, :], cols[:, i, :, :]).then_inc(col_ready, 1)
                dve.memset(st[:, :], 0.0).then_inc(s_ready, 1)
                dve.wait_ge(col_ready, i + 1)
                for g in range(NQ):
                    dve.tensor_copy(flat("kn", g), t.filled(f"nk{g}")).then_inc(evicted_of(f"nk{g}"), 1)
                    t.filled(f"nv{g}")
                    tt(tiles4("vb", g), bank4(use[f"nv{g}"][0]), rows(C_HB, g), ALU.mult).then_inc(evicted_of(f"nv{g}"), 1)
                for g in range(NQ):
                    t.need("sqq", g)
                    t.need("sqk", g)
                    dve.tensor_reduce(ssq[:, g, 0:2, :], SQ[g][:, :, :].rearrange("p (a n) d -> p a n d", a=2), AX, ALU.add).then_inc(R_["ssq"], 1)
                    dve.wait_ge(R_["ssq"], i * (3 * NQ) + (3 * g + 1))
                    dve.tensor_scalar(ssq[:, g, 0, :], ssq[:, g, 0, :], 4 * EPS, float(HD), ALU.add, ALU.mult).then_inc(R_["ssq"], 1)
                    dve.tensor_scalar(ssq[:, g, 1, :], ssq[:, g, 1, :], 4 * EPS, None, ALU.add).then_inc(R_["ssq"], 1)
                for g in range(NQ):
                    t.need("rr", g)
                    tt(tiles4("kh", g), tiles4("kn", g), rsq[:, g, 1, :].unsqueeze(2).to_broadcast([P, GT, P]), ALU.mult).then_inc(R_["kh"], 1)
                for g in range(NQ):
                    dve.tensor_copy(flat("qdT", g), t.filled(f"qd{g}")).then_inc(evicted_of(f"qd{g}"), 1)
                if proj:
                    dve.wait_ge(conv_step, i * 12 + 13)
                    dve_cw(dve, i + 1)
                    dve.wait_ge(const_ready, i + 3)
                for g in range(NQ):
                    t.need("decB", g)
                    tt(flat("mm_", g), t.filled(f"kk{g}"), flat("decS", g), ALU.mult).then_inc(evicted_of(f"kk{g}"), 1)
                    t.need("decA", g)
                    tt(flat("attn", g), t.filled(f"qk{g}"), flat("decA", g), ALU.mult).then_inc(evicted_of(f"qk{g}"), 1)
                    conv(0, 2 * g)
                    conv(0, 2 * g + 1)
                for g in range(NQ):
                    dve.wait_ge(mb_done, i * (NQ * NL) + (g + 1))
                    tt(tiles4("X", g), mat4(IDENT), tiles4("mb", g), ALU.subtract).then_inc(R_["X1"], 1)
                    t.filled(f"m1{g}")
                    tt(tiles4("Y", g), mat4(IDENT), bank4(use[f"m1{g}"][0]), ALU.subtract).then_inc(evicted_of(f"m1{g}"), 1)
                if proj:
                    dve_silu(dve, i, 0)
                for l in range(1, NL):
                    for g in range(NQ):
                        t.filled(f"Y{g}_{l}")
                        if l < NL - 1:
                            tt(flat("X", g), flat("X", g), t.filled(f"X{g}_{l}"), ALU.subtract).then_inc(evicted_of(f"X{g}_{l}"), 1)
                        t.out(f"m1{g}" if l == 1 else f"Y{g}_{l - 1}")
                        tt(flat("Y", g), flat("Y", g), t.filled(f"Y{g}_{l}"), ALU.subtract).then_inc(evicted_of(f"Y{g}_{l}"), 1)
                    if 2 <= l < 6:
                        conv(1, l - 2)
                def mean_square(g):
                    t.need("sqo", g)
                    dve.tensor_reduce(ssq[:, g, 2, :], tiles4("onx", g), AX, ALU.add).then_inc(R_["sso"], 1)
                    dve.wait_ge(R_["sso"], i * (2 * NQ) + (2 * g + 1))
                    dve.tensor_scalar(ssq[:, g, 2, :], ssq[:, g, 2, :], 1.0 / HD, EPS, ALU.mult, ALU.add).then_inc(R_["sso"], 1)

                def norm(g):
                    t.need("ro", g)
                    tt(tiles4("onx", g), tiles4("on", g), rsq[:, g, 2, :].unsqueeze(2).to_broadcast([P, GT, P]), ALU.mult).then_inc(R_["onx"], 1)
                for n in range(NT):
                    dve.wait_ge(s_ready, i * (NT + 1) + (n + 1))
                    bank = t.filled(f"s{n}")[:, 0:P]
                    dve.scalar_tensor_tensor(st[:, :], st[:, :], col[:, C_EGL, n:n + 1], bank, ALU.mult, ALU.add).then_inc(s_ready, 1)
                    if n == 0 and proj:
                        dve_silu(dve, i, 1)
                    if 2 <= n < 6:
                        conv(2, n - 2)
                    if n == 6:
                        mean_square(0)

                norm(0)
                if proj:
                    dve_silu(dve, i, 2)
                mean_square(1)
                norm(1)
                for g in range(NQ):
                    dve.wait_ge(zs_ready, i + 1)
                    bank = t.filled(f"on{g}")
                    dve.scalar_tensor_tensor(flat("oz", g), bank, nw[:, 0:1], zs[:, g * HALF:(g + 1) * HALF], ALU.mult, ALU.mult).then_inc(R_["oz"], 1)
                    dve.wait_ge(R_["oz"], i * NQ + (g + 1))
                    dve.sem_inc(evicted_of(f"on{g}"), 1)
                if proj:
                    dve_z(dve, i)

            def pool_turn(pool, i):
                t = Turn(pool, i)
                tt = pool.tensor_tensor
                pool.wait_ge(col_ready, i + 1)
                for g in range(NQ):
                    tt(tiles4("rg", g), mat4(GT_), rows(C_G, g), ALU.mult).then_inc(R_["rg"], 1)
                for g in range(NQ):
                    t.out(f"nq{g}")
                    tt(SQ[g][:, 0:GT, :], tiles4("qn", g), tiles4("qn", g), ALU.mult).then_inc(R_["sqq"], 1)
                    t.out(f"nk{g}")
                    tt(SQ[g][:, GT:NT, :], tiles4("kn", g), tiles4("kn", g), ALU.mult).then_inc(R_["sqk"], 1)
                for g in range(NQ):
                    pool.wait_ge(R_["ssq"], i * (3 * NQ) + (3 * g + 3))
                    tt(rsq[:, g, 0:2, :], ssq[:, g, 0:2, :], mh[:, :].rearrange("p (a n) -> p a n", a=2), ALU.pow).then_inc(R_["rr"], 1)
                    t.need("rr", g)
                    tt(cqd[:, g, :], rsq[:, g, 0, :], col[:, C_EG, GT * g:GT * g + GT], ALU.mult).then_inc(R_["cq"], 1)
                    t.need("cq", g)
                    tt(tiles4("qd", g), tiles4("qn", g), cqd[:, g, :].unsqueeze(2).to_broadcast([P, GT, P]), ALU.mult).then_inc(R_["qd"], 1)
                pool.wait_ge(oz_stored, i * (16 * NQ) + 16)
                for g in range(NQ):
                    t.out(f"D{g}")
                    tt(tiles4("decA", g), tiles4("dec", g), mat4(GE), ALU.mult).then_inc(R_["decI"], 1)
                    tt(tiles4("decS", g), tiles4("dec", g), mat4(GT_), ALU.mult).then_inc(R_["decS"], 1)
                    t.need("decS", g)
                    tt(tiles4("decS", g), tiles4("decS", g), rows(C_BETA, g), ALU.mult).then_inc(R_["decB"], 1)
                    t.need("decI", g)
                    tt(tiles4("decA", g), tiles4("decA", g), rsq[:, g, 0, :].unsqueeze(2).to_broadcast([P, GT, P]), ALU.mult).then_inc(R_["decA"], 1)
                split_lo(pool, TILE_HEAD + 6, i, 4)

                def level(l):
                    for g in range(NQ):
                        if l == 0:
                            t.out(f"kk{g}")
                            t.filled(f"at{g}")
                        elif l == 1:
                            t.filled(f"m1{g}")
                            t.need("X1", g)
                        else:
                            t.filled(f"R{g}_{l - 1}")
                        tt(tiles4("mb", g), tiles4("mm_", g), mat4(LEVEL0 + l), ALU.mult).then_inc(mb_done, 1)
                level(0)
                level(1)
                for g in range(NQ):
                    t.need("kh", g)
                    tt(tiles4("kbg", g), tiles4("kh", g), rows(C_BEG, g), ALU.mult).then_inc(R_["kbg"], 1)
                level(2)
                for g in range(NQ):
                    tt(tiles4("kd", g), tiles4("kh", g), rows(C_ES, g), ALU.mult).then_inc(R_["kd"], 1)
                split_lo(pool, TILE_HEAD + 7, i, 4)
                for l in range(3, NL):
                    level(l)
                split_lo(pool, TILE_HEAD + 8, i, 4)
                for g in range(NQ):
                    t.out(f"o{g}")
                    tt(tiles4("onx", g), tiles4("on", g), tiles4("on", g), ALU.mult).then_inc(R_["sqo"], 1)
                    pool.wait_ge(R_["sso"], i * (2 * NQ) + (2 * g + 2))
                    tt(rsq[:, g, 2, :], ssq[:, g, 2, :], mh[:, 0:GT], ALU.pow).then_inc(R_["ro"], 1)
                split_lo(pool, TILE_HEAD + 9, i, 4)

            def sp_turn(sp, i, proj):
                for s in range(4):
                    load_w(sp, TILE_HEAD + 7 + s, i, 4)
                if not proj:
                    for s in range(4):
                        sp.wait_ge(cin_ready, 3 * HEADS + s + 1)
                        sp.dma_start(mg_dram[4 + s], early[s]).then_inc(oz_stored, 16)
                for g in range(NQ):
                    sp.wait_ge(R_["oz"], i * NQ + (g + 1))
                    sp.dma_start(oz_dram[i][:, g * HALF:(g + 1) * HALF], flat("oz", g)).then_inc(oz_stored, 16)

            with nc.Block() as block:
                @block.sync
                def _(sp):
                    sp.dma_start(cw_all[:, :, :], a["conv"]).then_inc(conv_in, 16)
                    sp.dma_start(nw[:, :], a["normw"]).then_inc(conv_in, 16)
                    sp.sem_inc(oz_stored, 16)
                    load_w(sp, TILE_HEAD + 3)
                    for s in range(3):
                        load_w(sp, TILE_HEAD + 4 + s)
                    with sp.Fori(0, HEADS - 1) as i:
                        sp_turn(sp, i, True)
                    sp_turn(sp, HEADS - 1, False)
                    sp.wait_ge(oz_stored, 16 * NQ * HEADS + 16 + 64)

                @block.tensor
                def _(pe):
                    for u in range(64):
                        s, n, k = u // 16, u // 8 % 2, u % 8
                        t = TILE_HEAD + s
                        if u % 16 == 0:
                            pe.wait_ge(w_lo, t + 1)
                            if s >= 2:
                                pe.wait_ge(cin_ready, 1 + s - 2)
                        mm = product3(pe, pair[s % 2][:, n, :], wH[:, t % 2, k * P:(k + 1) * P], wL[:, t % 2, k * P:(k + 1) * P],
                                      hH[:, k, n * HALF:(n + 1) * HALF], hL[:, k, n * HALF:(n + 1) * HALF], k == 0, k == KT - 1)
                        if u % 16 == 15:
                            mm.then_inc(w_used, 1)
                    for b in range(4):
                        pe.sem_inc(evicted[b], 1)
                    with pe.Fori(0, HEADS - 1) as i:
                        pe_turn(pe, i)
                    pe_turn(pe, HEADS - 1)

                @block.scalar
                def _(act):
                    for s in range(4):
                        if s < 3:
                            act.wait_ge(w_used, TILE_HEAD + s + 1)
                            act.wait_ge(conv_step, 4 * s + 1)
                            act.activation(cin[:, CONV_K - 1:], pair[s % 2][:, :, :].rearrange("p a b -> p (a b)"), ACT.Copy).then_inc(cin_ready, 1)
                            split_hi(act, TILE_HEAD + 2 + s)
                            act.wait_ge(conv_step, 4 * s + 5)
                            if s:
                                act.wait_ge(conv_ready, s)
                            act.activation(th[:, :], acc[:, :], ACT.Tanh, scale=0.5).then_inc(th_ready, 1)
                        else:
                            act.wait_ge(w_used, TILE_HEAD + 4)
                            split_hi(act, TILE_HEAD + 5)
                            act.wait_ge(conv_ready, 3)
                            act.activation(th[:, :], pair[1][:, :, :].rearrange("p a b -> p (a b)"), ACT.Tanh, scale=0.5).then_inc(th_ready, 1)
                    with act.Fori(0, HEADS - 1) as i:
                        act_turn(act, i, True)
                    act_turn(act, HEADS - 1, False)

                @block.gpsimd
                def _(pool):
                    pool.memset(mh[:, :], -0.5).then_inc(mh_ready, 1)
                    pool.wait_ge(mh_ready, 1)
                    for s in range(4):
                        split_lo(pool, TILE_HEAD + 2 + s)
                    with pool.Fori(0, HEADS - 1) as i:
                        pool_turn(pool, i)
                    pool_turn(pool, HEADS - 1)

                @block.vector
                def _(dve):
                    dve.memset(cin[:, 0:CONV_K - 1], 0.0).then_inc(const_ready, 1)
                    dve.sem_inc(conv_step, 1)
                    dve.wait_ge(conv_in, 32)
                    dve_cw(dve, 0)
                    dve.wait_ge(const_ready, 2)
                    dve.tensor_scalar(nw[:, :], nw[:, :], 0.5, None, ALU.mult).then_inc(nw_ready, 1)
                    dve.wait_ge(nw_ready, 1)
                    for s in range(3):
                        dve.wait_ge(cin_ready, s + 1)
                        if s:
                            dve.wait_ge(conv_ready, s)
                        dve.tensor_scalar(acc[:, :], cin[:, 0:T], cw[:, CONV_K * s:CONV_K * s + 1], None, ALU.mult).then_inc(conv_step, 1)
                        for tap in range(1, CONV_K):
                            dve.wait_ge(conv_step, 4 * s + tap + 1)
                            dve.scalar_tensor_tensor(acc[:, :], cin[:, tap:tap + T], cw[:, CONV_K * s + tap:CONV_K * s + tap + 1], acc[:, :],
                                                     ALU.mult, ALU.add).then_inc(conv_step, 1)
                        dve.wait_ge(th_ready, s + 1)
                        dve.scalar_tensor_tensor((qc, kc, vc)[s][:, :], th[:, :], 1.0, acc[:, :], ALU.add, ALU.mult).then_inc(conv_ready, 1)
                    dve.wait_ge(th_ready, 4)
                    dve.scalar_tensor_tensor(zs[:, :], th[:, :], 1.0, pair[1][:, :, :].rearrange("p a b -> p (a b)"), ALU.add,
                                             ALU.mult).then_inc(zs_ready, 1)
                    with dve.Fori(0, HEADS - 1) as i:
                        dve_turn(dve, i, True)
                    dve_turn(dve, HEADS - 1, False)

        dstack.close()

        with ExitStack() as c6:
            s6 = sb_in(c6)
            ozH, ozL = s6("ozH", [P, HEADS, T], F32R), s6("ozL", [P, HEADS, T], F32R)
            ygH, ygL = s6("ygH", [P, CT, T], F32R), s6("ygL", [P, CT, T], F32R)
            stg = s6("stg", [P, 4, T])
            TA, TB, M1, MG = range(4)
            NB = HEADS + CT
            by_pool = [j for j in range(NB) if j % 3 == 0]
            by_dve = [j for j in range(NB) if j % 3]
            b_landed = [sem(f"b_landed{n}") for n in range(4)]
            bH_done, bL_pool, bL_dve = sem("bH_done"), sem("bL_pool"), sem("bL_dve")
            gate_act = sem("gate_act")
            merge_dve = sem("merge_dve")
            mg_stored = sem("mg_stored")
            hi_of = lambda j: ozH[:, j, :] if j < HEADS else ygH[:, j - HEADS, :]
            lo_of = lambda j: ozL[:, j, :] if j < HEADS else ygL[:, j - HEADS, :]

            def branch_lo(eng, j, done):
                eng.wait_ge(bH_done, j + 1)
                eng.tensor_tensor(lo_of(j), stg[:, j % 4, :], hi_of(j).bitcast(F32), ALU.subtract).then_inc(done, 1)


            def gates_pe(pe, i):
                for s in range(2):
                    t = TILE_LOOP + s
                    pe.wait_ge(w_lo, i * 4 + (t + 1))
                    pe.wait_ge(gate_act, i * 2 + (s + 1))
                    for n in range(2):
                        for k in range(KT):
                            mm = product3(pe, pair[s][:, n, :], wH[:, t % 2, k * P:(k + 1) * P], wL[:, t % 2, k * P:(k + 1) * P],
                                          hH[:, k, n * HALF:(n + 1) * HALF], hL[:, k, n * HALF:(n + 1) * HALF], k == 0, k == KT - 1)
                    mm.then_inc(w_used, 1)

            def branches_pe(pe, tile, i, m0, first=False):
                for s, (dst, xh, xl, kt) in enumerate(((work[:, 0:2, :], ozH, ozL, HEADS), (work[:, 2:4, :], ygH, ygL, CT))):
                    t = tile + s
                    pe.wait_ge(w_lo, i * 4 + (t + 1))
                    pe.wait_ge(merge_dve, i * 4 + (4 * m0 + 2 * s + 1))
                    for k in range(kt):
                        if first:
                            j = k + s * HEADS
                            if j in by_pool:
                                pe.wait_ge(bL_pool, by_pool.index(j) + 1)
                            else:
                                pe.wait_ge(bL_dve, by_dve.index(j) + 1)
                        for n in range(2):
                            mm = product3(pe, dst[:, n, :], wH[:, t % 2, k * P:(k + 1) * P], wL[:, t % 2, k * P:(k + 1) * P],
                                          xh[:, k, n * HALF:(n + 1) * HALF], xl[:, k, n * HALF:(n + 1) * HALF], k == 0, k == kt - 1)
                    mm.then_inc(w_used, 1)

            def merge_act(act, i, last):
                for s in range(4):
                    act.wait_ge(w_used, i * 4 + (TILE_LOOP + s + 1))
                    if not (last and s >= 2):
                        split_hi(act, TILE_LOOP + 2 + s, i, 4)
                    if s < 2:
                        act.wait_ge(merge_dve, i * 4 + (4 * EARLY + 2 * s + 1))
                        act.activation(stg[:, (TA, TB)[s], :], pair[s][:, :, :].rearrange("p a b -> p (a b)"), ACT.Tanh,
                                       scale=0.5).then_inc(gate_act, 1)

            def merge_dve_turn(dve, tile, i, m0):
                dve.wait_ge(w_used, i * 4 + (tile + 1))
                dve.wait_ge(merge_dve, i * 4 + (4 * m0 + 4))
                dve.scalar_tensor_tensor(stg[:, M1, :], stg[:, TA, :], 1.0, work[:, 0:2, :].rearrange("p a b -> p (a b)"),
                                         ALU.add, ALU.mult).then_inc(merge_dve, 1)
                dve.tensor_scalar(stg[:, TB, :], stg[:, TB, :], 1.0, 0.125, ALU.add, ALU.mult).then_inc(merge_dve, 1)
                dve.wait_ge(w_used, i * 4 + (tile + 2))
                dve.wait_ge(merge_dve, i * 4 + (4 * m0 + 6))
                dve.wait_ge(mg_stored, i * 16 + (16 * m0 + 16))
                dve.tensor_tensor(stg[:, MG, :], stg[:, TB, :], work[:, 2:4, :].rearrange("p a b -> p (a b)"), ALU.mult).then_inc(merge_dve, 1)
                dve.wait_ge(merge_dve, i * 4 + (4 * m0 + 7))
                dve.tensor_tensor(stg[:, MG, :], stg[:, M1, :], stg[:, MG, :], ALU.add).then_inc(merge_dve, 1)

            def merge_sp(sp, i, last):
                for s in range(1 if last else 4):
                    load_w(sp, TILE_LOOP + 3 + s, i, 4)
                sp.wait_ge(merge_dve, i * 4 + (4 * EARLY + 8))
                sp.dma_start(mg_dram[i + EARLY], stg[:, MG, :]).then_inc(mg_stored, 16)

            LATE = KT - EARLY
            with nc.Block() as block:
                @block.sync
                def _(sp):
                    for j in range(NB):
                        if j >= 4:
                            if j - 4 in by_pool:
                                sp.wait_ge(bL_pool, by_pool.index(j - 4) + 1)
                            else:
                                sp.wait_ge(bL_dve, by_dve.index(j - 4) + 1)
                        sp.dma_start(stg[:, j % 4, :], oz_dram[j] if j < HEADS else yg_dram[j - HEADS]).then_inc(b_landed[j % 4], 16)
                    sp.sem_inc(mg_stored, 16)
                    for m in range(EARLY):
                        for s, slot in enumerate((TA, TB)):
                            if m == 0:
                                sp.wait_ge(bL_pool, len(by_pool))
                                sp.wait_ge(bL_dve, len(by_dve))
                            else:
                                sp.wait_ge(merge_dve, 4 * m + 2 * s + 1)
                            sp.dma_start(stg[:, slot, :], mg_dram[4 + 2 * m + s]).then_inc(b_landed[s], 16)
                        for s in range(2):
                            load_w(sp, TILE_FIRST + 3 + 2 * m + s)
                    for m in range(EARLY):
                        sp.wait_ge(merge_dve, 4 * m + 8)
                        sp.dma_start(mg_dram[m], stg[:, MG, :]).then_inc(mg_stored, 16)
                    with sp.Fori(0, LATE - 1) as i:
                        merge_sp(sp, i, False)
                    merge_sp(sp, LATE - 1, True)
                    sp.wait_ge(mg_stored, 16 * KT + 16)

                @block.tensor
                def _(pe):
                    for m in range(EARLY):
                        branches_pe(pe, TILE_FIRST + 2 * m, 0, m, first=(m == 0))
                    with pe.Fori(0, LATE) as i:
                        gates_pe(pe, i)
                        branches_pe(pe, TILE_LOOP + 2, i, EARLY)

                @block.scalar
                def _(act):
                    act.sem_inc(gate_act, 2)
                    for j in range(NB):
                        act.wait_ge(b_landed[j % 4], 16 * (j // 4 + 1))
                        act.activation(hi_of(j), stg[:, j % 4, :], ACT.Copy).then_inc(bH_done, 1)
                    for t in range(TILE_FIRST, TILE_LOOP):
                        split_hi(act, t + 2)
                    with act.Fori(0, LATE - 1) as i:
                        merge_act(act, i, False)
                    merge_act(act, LATE - 1, True)

                @block.gpsimd
                def _(pool):
                    for j in by_pool:
                        branch_lo(pool, j, bL_pool)
                    for t in range(TILE_FIRST, TILE_LOOP):
                        split_lo(pool, t + 2)
                    with pool.Fori(0, LATE - 1) as i:
                        for s in range(4):
                            split_lo(pool, TILE_LOOP + 2 + s, i, 4)
                    for s in range(2):
                        split_lo(pool, TILE_LOOP + 2 + s, LATE - 1, 4)

                @block.vector
                def _(dve):
                    dve.sem_inc(merge_dve, 4)
                    for j in by_dve:
                        branch_lo(dve, j, bL_dve)
                    for m in range(EARLY):
                        for s in range(2):
                            dve.wait_ge(b_landed[s], 16 * (NB // 4 + m + 1))
                        if m == 0:
                            dve.wait_ge(bL_pool, len(by_pool))
                        merge_dve_turn(dve, TILE_FIRST + 2 * m, 0, m)
                    with dve.Fori(0, LATE) as i:
                        dve.wait_ge(gate_act, i * 2 + 4)
                        merge_dve_turn(dve, TILE_LOOP + 2, i, EARLY)
        hstack.close()

        with ExitStack() as c7:
            s7 = sb_in(c7)
            wo = s7("wo", [P, KT, D])
            woH, woL = s7("woH", [P, KT, D], F32R), s7("woL", [P, KT, D], F32R)
            diag = s7("diag", [P, KT, P])
            gate = s7("gate", [P, D])
            fnw = s7("fnw", [P, D])
            xt = s7("xt", [P, 2, D])
            y = s7("y", [P, 2, D])
            ss = s7("ss7", [P, 2])
            rs = s7("rs7", [P, 2])
            mh = s7("mh7", [P, 1])
            wo_in = [sem(f"wo_in{k}") for k in range(KT // 2)]
            woH_done, woL_pool, woL_dve = sem("woH_done"), sem("woL_pool"), sem("woL_dve")
            fn_in, diag_done = sem("fn_in"), sem("diag_done")
            gate_full, gate_done = sem("gate_full"), sem("gate_done")
            x7_in, out_stored = [sem("x7_in0"), sem("x7_in1")], [sem("out_stored0"), sem("out_stored1")]
            out_dve = sem("out_dve")
            sq7_done, rs_done, mh7_done = sem("sq7_done"), sem("rs_done"), sem("mh7_done")
            wo_pool = [2, 6]
            wo_dve = [k for k in range(KT) if k not in wo_pool]
            mgv = mg_dram.rearrange("m p (n t) -> n p m t", n=NT)
            with nc.Block() as block:
                @block.sync
                def _(sp):
                    def load_merged(i, s):
                        t = TILE_OUT + s
                        sp.wait_ge(w_lo, i * 2 + (t - 1))
                        sp.dma_start(raw[:, t % 2, :].rearrange("p (m t) -> p m t", m=KT), mgv[i * 2 + s]).then_inc(w_landed[t % 2], 16)
                    load_merged(0, 0)
                    load_merged(0, 1)
                    for k in range(0, KT, 2):
                        sp.dma_start(wo[:, k:k + 2, :], a["wout"][:, k:k + 2, :]).then_inc(wo_in[k // 2], 16)
                    for s in range(2):
                        sp.sem_inc(out_stored[s], 16)

                    def out_turn(i, last):
                        for s in range(2):
                            sp.wait_ge(out_dve, i * 8 + (4 * s + 2))
                            sp.dma_start(xt[:, s, :], a["x"][i * 2 + s]).then_inc(x7_in[s], 16)
                        if not last:
                            for s in range(2):
                                load_merged(i + 1, s)
                        for s in range(2):
                            sp.wait_ge(out_dve, i * 8 + (4 * s + 12))
                            sp.dma_start(out[0].rearrange("(n p) d -> n p d", p=P)[i * 2 + s], y[:, s, :]).then_inc(out_stored[s], 16)
                    with sp.Fori(0, NT // 2 - 1) as i:
                        out_turn(i, False)
                    out_turn(NT // 2 - 1, True)
                    for s in range(2):
                        sp.wait_ge(out_stored[s], 16 * (NT // 2) + 16)

                @block.tensor
                def _(pe):
                    pe.wait_ge(diag_done, KT)
                    for k in range(KT):
                        mm = pe.matmul(work[:, k // 4, k % 4 * P:(k % 4 + 1) * P], cst[:, ONES, :], diag[:, k, :], start=True, stop=True)
                    mm.then_inc(gate_full, 1)
                    with pe.Fori(0, NT // 2) as i:
                        for s in range(2):
                            t = TILE_OUT + s
                            pe.wait_ge(w_lo, i * 2 + (t + 1))
                            pe.wait_ge(out_dve, i * 8 + (4 * s + 1))
                            for k in range(KT):
                                if s == 0:
                                    if k in wo_pool:
                                        pe.wait_ge(woL_pool, wo_pool.index(k) + 1)
                                    else:
                                        pe.wait_ge(woL_dve, wo_dve.index(k) + 1)
                                for n in range(2):
                                    mm = product3(pe, pair[s][:, n, :], wH[:, t % 2, k * P:(k + 1) * P], wL[:, t % 2, k * P:(k + 1) * P],
                                                  woH[:, k, n * HALF:(n + 1) * HALF], woL[:, k, n * HALF:(n + 1) * HALF], k == 0, k == KT - 1)
                            mm.then_inc(w_used, 1)

                @block.scalar
                def _(act):
                    act.dma_start(fnw[:, :], a["fnw"]).then_inc(fn_in, 16)
                    split_hi(act, TILE_OUT)
                    for k in range(KT):
                        act.wait_ge(wo_in[k // 2], 16)
                        act.activation(woH[:, k, :], wo[:, k, :], ACT.Copy).then_inc(woH_done, 1)
                    act.sem_inc(sq7_done, 1)

                    def act_out(i, last):
                        for s in range(2):
                            if not (last and s):
                                split_hi(act, TILE_OUT + 1 + s, i, 2)
                            act.wait_ge(out_dve, i * 8 + (4 * s + 10))
                            act.wait_ge(sq7_done, i * 2 + (s + 1))
                            act.activation(wo[:, 0, :], y[:, s, :], ACT.Square, accum_out=ss[:, s:s + 1]).then_inc(sq7_done, 1)
                    with act.Fori(0, NT // 2 - 1) as i:
                        act_out(i, False)
                    act_out(NT // 2 - 1, True)

                @block.gpsimd
                def _(pool):
                    pool.memset(mh[:, :], -0.5).then_inc(mh7_done, 1)
                    pool.wait_ge(mh7_done, 1)
                    split_lo(pool, TILE_OUT)
                    for k in wo_pool:
                        pool.wait_ge(woH_done, k + 1)
                        pool.tensor_tensor(woL[:, k, :], wo[:, k, :], woH[:, k, :].bitcast(F32), ALU.subtract).then_inc(woL_pool, 1)

                    def pool_out(i, last):
                        for s in range(2):
                            if not (last and s):
                                split_lo(pool, TILE_OUT + 1 + s, i, 2)
                            pool.wait_ge(out_dve, i * 8 + (4 * s + 11))
                            pool.tensor_tensor(rs[:, s:s + 1], ss[:, s:s + 1], mh[:, :], ALU.pow).then_inc(rs_done, 1)
                    with pool.Fori(0, NT // 2 - 1) as i:
                        pool_out(i, False)
                    pool_out(NT // 2 - 1, True)

                @block.vector
                def _(dve):
                    dve.sem_inc(out_dve, 8)
                    for k in range(KT):
                        dve.tensor_scalar(diag[:, k, :], ident, modT[:, 2 * KT + k:2 * KT + k + 1], 0.5, ALU.mult, ALU.mult).then_inc(diag_done, 1)
                    for k in wo_dve:
                        dve.wait_ge(woH_done, k + 1)
                        dve.tensor_tensor(woL[:, k, :], wo[:, k, :], woH[:, k, :].bitcast(F32), ALU.subtract).then_inc(woL_dve, 1)
                    dve.wait_ge(woL_pool, len(wo_pool))
                    dve.wait_ge(gate_full, 1)
                    dve.tensor_copy(gate[:, :], work[:, 0:2, :].rearrange("p a b -> p (a b)")).then_inc(gate_done, 1)
                    dve.wait_ge(gate_done, 1)
                    dve.wait_ge(fn_in, 16)
                    with dve.Fori(0, NT // 2) as i:
                        for s in range(2):
                            dve.wait_ge(w_used, i * 2 + (TILE_OUT + s + 1))
                            dve.wait_ge(out_stored[s], i * 16 + 16)
                            dve.tensor_tensor(y[:, s, :], pair[s][:, :, :].rearrange("p a b -> p (a b)"), gate[:, :], ALU.mult).then_inc(out_dve, 1)
                            dve.wait_ge(out_dve, i * 8 + (4 * s + 9))
                            dve.wait_ge(x7_in[s], i * 16 + 16)
                            dve.tensor_tensor(y[:, s, :], y[:, s, :], xt[:, s, :], ALU.add).then_inc(out_dve, 1)
                            dve.wait_ge(sq7_done, i * 2 + (s + 2))
                            dve.tensor_scalar(ss[:, s:s + 1], ss[:, s:s + 1], 1.0 / D, EPS, ALU.mult, ALU.add).then_inc(out_dve, 1)
                            dve.wait_ge(rs_done, i * 2 + (s + 1))
                            dve.scalar_tensor_tensor(y[:, s, :], y[:, s, :], rs[:, s:s + 1], fnw[:, :], ALU.mult, ALU.mult).then_inc(out_dve, 1)


def _layout(i):
    import numpy as np
    f = lambda n: np.asarray(i[n])
    w_in = f('w_in')[0]
    qkvz = 4 * HEADS * HD
    u0 = qkvz + 2 * HEADS

    def tiles(w, col, n=1):
        k = w.shape[0] // P
        return np.concatenate([w[:, col + P * m:col + P * (m + 1)].reshape(k, P, P).transpose(1, 0, 2).reshape(P, k * P)[None]
                               for m in range(n)])
    glu, wa, wb = f('s5_glu_w')[0], f('w_proj_a')[0], f('w_proj_b')[0]
    parts = [tiles(w_in, qkvz)]
    for m in range(CT):
        parts += [tiles(w_in, u0 + m * P), tiles(w_in, u0 + S5W + m * P)]
    gt = tiles(glu, 0, CT)
    parts.append(np.stack([np.concatenate([gt[2 * m], gt[2 * m + 1]], 1) for m in range(2)]))
    for h in range(HEADS):
        for s in range(4):
            parts.append(tiles(w_in, s * HEADS * HD + h * HD))
    gates = lambda m: [tiles(w_in, u0 + 2 * S5W + m * P), tiles(w_in, u0 + 2 * S5W + D + m * P)]
    branches = lambda m: [tiles(wa, m * P), np.concatenate([tiles(wb, m * P)] * 2, 2)]
    parts += [t for m in range(EARLY) for t in gates(m)] + [t for m in range(EARLY) for t in branches(m)]
    for m in range(EARLY, KT):
        parts += gates(m) + branches(m)
    col = lambda v: v.reshape(-1, P).T
    ada = f('w_ada')[0].reshape(KT, P, 3, D).transpose(2, 1, 0, 3)
    dup = lambda v: np.concatenate([v, v], 0)
    p_, f_ = np.arange(P)[:, None], np.arange(P)[None, :]
    cst = [p_ == f_, p_ <= f_, p_ > f_, p_ >= f_, p_ >= 0 * f_]
    cst += [(p_ // (2 * b) == f_ // (2 * b)) & (p_ % (2 * b) >= b) & (f_ % (2 * b) < b) for b in LEVELS]
    conv = f('dn_conv_w')[0].reshape(CONV_K, 3, HEADS, P).transpose(3, 2, 1, 0)
    d = {
        'w': np.concatenate(parts),
        'x': f('x')[0].reshape(NT, P, D),
        'cT': col(f('c')[0]),
        'bada': col(f('b_ada')[0]),
        'wada': ada,
        'cst': np.stack([np.broadcast_to(m, (P, P)).astype(np.float32) for m in cst], 1),
        'dtb': np.broadcast_to(f('dn_dt_bias')[0], (P, HEADS)),
        'alog': np.broadcast_to(f('dn_a_log')[0], (P, HEADS)),
        'conv': conv.reshape(P, HEADS, 3 * CONV_K),
        'normw': f('dn_norm_w')[0].reshape(P, 1),
        's5p': np.stack([dup(f('s5_lambda_re')[0].T), dup(f('s5_lambda_im')[0].T),
                         np.broadcast_to(f('s5_log_dt')[0], (P, GROUPS))], 1),
        's5b': np.stack([dup(f('s5_b_re')[0].transpose(1, 0, 2)), dup(f('s5_b_im')[0].transpose(1, 0, 2))], 1),
        's5c': np.stack([dup(f('s5_c_re')[0].transpose(2, 0, 1)), dup(f('s5_c_im')[0].transpose(2, 0, 1))], 1),
        's5d': col(f('s5_d')[0]),
        'glub': col(f('s5_glu_b')[0]),
        'wout': f('w_out')[0].reshape(KT, P, D).transpose(1, 0, 2),
        'fnw': np.broadcast_to(f('final_norm_w'), (P, D)),
    }
    return {k: np.ascontiguousarray(v) for k, v in d.items()}


def kernel(**inputs):
    import concourse.bacc as _bacc
    from concourse.bass_utils import run_bass_kernel_spmd as _run

    nc = _bacc.Bacc("TRN2", target_bir_lowering=False, num_devices=1)
    arrays, aps = {}, {}
    for name, v in _layout(inputs).items():
        arrays[f"in_{name}_dram"] = v
        aps[name] = nc.dram_tensor(f"in_{name}_dram", v.shape, mybir.dt.from_np(v.dtype), kind="ExternalInput").ap()
    out = nc.dram_tensor("out_0_dram", (1, T, D), F32, kind="ExternalOutput").ap()
    oz = nc.dram_tensor("oz_scratch", (HEADS, P, T), F32, kind="Internal").ap()
    yg = nc.dram_tensor("yg_scratch", (CT, P, T), F32, kind="Internal").ap()
    mg = nc.dram_tensor("mg_scratch", (KT, P, T), F32, kind="Internal").ap()
    build_program(nc, aps, out, oz, yg, mg)
    r = _run(nc, [arrays], core_ids=[0])
    return r.results[0]["out_0_dram"]
```
